# Optimizing a Trainium2 kernel written in Bass

```python
import jax, jax.numpy as jnp
from jax import lax
import numpy as np

D_MODEL = 2048
BATCH = 1
SEQ = 256
DEPTH = 1

GRID_W = 64
MIX_WIDTH = D_MODEL
NA_WIDTH = D_MODEL // 4
NA_HEAD_DIM = 64
NA_HEADS = NA_WIDTH // NA_HEAD_DIM
NA_WIN_ROWS = 8
NA_WIN_COLS = 16
RW_WIDTH = 3 * D_MODEL // 8
RW_HEAD_DIM = 64
RW_HEADS = RW_WIDTH // RW_HEAD_DIM
DECAY_LORA = 64
ICLR_LORA = 64
GATE_LORA = 128
RET_WIDTH = MIX_WIDTH - NA_WIDTH - RW_WIDTH
RET_HEAD_DIM = 128
RET_HEADS = RET_WIDTH // RET_HEAD_DIM
RET_CHUNK = 128
NA_IN_COLS = 3 * NA_WIDTH
RW_IN_COLS = 3 * RW_WIDTH + 2 * DECAY_LORA + 2 * ICLR_LORA + GATE_LORA
RET_IN_COLS = 4 * RET_WIDTH
IN_COLS = NA_IN_COLS + RW_IN_COLS + RET_IN_COLS
D_FF = 4 * D_MODEL
NORM_EPS = 1e-6
LNX_EPS = 64e-5

kernel_name = 'hybrid_natten_rwkv7_retention_encoder'

def rms_norm(x, g):
    xf = x.astype(jnp.float32)
    y = xf * lax.rsqrt(jnp.mean(xf * xf, axis=-1, keepdims=True) + NORM_EPS)
    return (y * g.astype(jnp.float32)).astype(x.dtype)

def split_heads(u, n_heads):
    return u.reshape(*u.shape[:-1], n_heads, u.shape[-1] // n_heads)

def neighbourhood_attention(q, k, v, rpb):
    b, t, h, d = q.shape
    rows = t // GRID_W
    kh = min(NA_WIN_ROWS, rows)
    kw = NA_WIN_COLS
    scale = d ** -0.5
    qg = jnp.moveaxis(q.reshape(b, rows, GRID_W, h, d), 1, 0)
    kg = k.reshape(b, rows, GRID_W, h, d)
    vg = v.reshape(b, rows, GRID_W, h, d)
    row_ids = jnp.arange(rows)
    row_start = jnp.clip(row_ids - kh // 2, 0, rows - kh)
    cols = jnp.arange(GRID_W)
    col_idx = jnp.clip(cols - kw // 2, 0, GRID_W - kw)[:, None] + jnp.arange(kw)[None, :]
    col_bias = rpb[:, :, col_idx - cols[:, None] + (NA_WIN_COLS - 1)]

    def row_block(args):
        q_row, i, s = args
        k_nb = lax.dynamic_slice_in_dim(kg, s, kh, axis=1)[:, :, col_idx]
        v_nb = lax.dynamic_slice_in_dim(vg, s, kh, axis=1)[:, :, col_idx]
        sc = jnp.einsum('bqhd,brqchd->bhqrc', q_row, k_nb).astype(jnp.float32) * scale
        row_off = s + jnp.arange(kh) - i + (NA_WIN_ROWS - 1)
        bias = jnp.transpose(col_bias[:, row_off], (0, 2, 1, 3))
        sc = sc + bias.astype(jnp.float32)[None]
        p = jax.nn.softmax(sc.reshape(b, h, GRID_W, kh * kw), axis=-1)
        p = p.reshape(b, h, GRID_W, kh, kw).astype(v.dtype)
        return jnp.einsum('bhqrc,brqchd->bqhd', p, v_nb)

    out = lax.map(row_block, (qg, row_ids, row_start))
    return jnp.moveaxis(out, 0, 1).reshape(b, t, h * d)

def token_shift(z, mu_prev, mu_next):
    z_prev = jnp.pad(z[:, :-1], ((0, 0), (1, 0), (0, 0)))
    z_next = jnp.pad(z[:, 1:], ((0, 0), (0, 1), (0, 0)))
    return z + mu_prev * (z_prev - z) + mu_next * (z_next - z)

def dir_stack(fwd, bwd):
    return jnp.moveaxis(jnp.stack([fwd, jnp.flip(bwd, axis=1)], axis=0), 2, 0)

def rwkv7_step(state, inp):
    r, w, k, v, a, bb = inp
    sa = jnp.einsum('dbhvk,dbhk->dbhv', state, a)
    state = state * w[..., None, :] + sa[..., :, None] * bb[..., None, :] + v[..., :, None] * k[..., None, :]
    return state, jnp.einsum('dbhvk,dbhk->dbhv', state, r)

def rwkv7_mixer(z, mu_prev, mu_next, w0, w2, a0, a2, k_k, k_a, r_k, g2, lnx_g, lnx_b):
    f32 = jnp.float32
    bsz, t, _ = z.shape
    z = token_shift(z, mu_prev, mu_next)
    o1 = 3 * RW_WIDTH + 2 * DECAY_LORA
    r, k, v, wd, ad, gd = jnp.split(z, [RW_WIDTH, 2 * RW_WIDTH, 3 * RW_WIDTH, o1, o1 + 2 * ICLR_LORA], axis=-1)
    wd = wd.reshape(bsz, t, 2, DECAY_LORA)
    ad = ad.reshape(bsz, t, 2, ICLR_LORA)
    w = (w0 + jnp.einsum('btdr,drc->btdc', jnp.tanh(wd), w2)).astype(f32)
    decay = jnp.exp(-jnp.exp(-jax.nn.softplus(-w) - 0.5))
    a = jax.nn.sigmoid((a0 + jnp.einsum('btdr,drc->btdc', ad, a2)).astype(f32))
    g = jax.nn.sigmoid(gd) @ g2
    r32, k32, v32 = r.astype(f32), k.astype(f32), v.astype(f32)
    kk = split_heads(k32 * k_k, RW_HEADS)
    kk = kk / jnp.maximum(jnp.sqrt(jnp.sum(kk * kk, axis=-1, keepdims=True)), 1e-12)
    kd = split_heads(k32[:, :, None] * (1.0 + (a - 1.0) * k_a), RW_HEADS)
    b_vec = kk[:, :, None] * split_heads(a, RW_HEADS)
    dec_h = split_heads(decay, RW_HEADS)
    rh = split_heads(r32, RW_HEADS)
    vh = split_heads(v32, RW_HEADS)
    xs = (dir_stack(rh, rh), dir_stack(dec_h[:, :, 0], dec_h[:, :, 1]),
          dir_stack(kd[:, :, 0], kd[:, :, 1]), dir_stack(vh, vh),
          dir_stack(-kk, -kk), dir_stack(b_vec[:, :, 0], b_vec[:, :, 1]))
    state0 = jnp.zeros((2, bsz, RW_HEADS, RW_HEAD_DIM, RW_HEAD_DIM), f32)
    _, ys = lax.scan(rwkv7_step, state0, xs)
    y = jnp.moveaxis(ys[:, 0] + jnp.flip(ys[:, 1], axis=0), 0, 1)
    mu = jnp.mean(y, axis=-1, keepdims=True)
    var = jnp.mean(jnp.square(y - mu), axis=-1, keepdims=True)
    y = ((y - mu) * lax.rsqrt(var + LNX_EPS)).reshape(bsz, t, RW_WIDTH) * lnx_g + lnx_b
    bonus = jnp.sum(rh[:, :, None] * kd * r_k, axis=-1, keepdims=True) * vh[:, :, None]
    y = y + jnp.sum(bonus, axis=2).reshape(bsz, t, RW_WIDTH)
    return (y * g).astype(z.dtype)

def rotary_interleaved(x, ang):
    x2 = x.astype(jnp.float32).reshape(*x.shape[:-1], x.shape[-1] // 2, 2)
    c = jnp.cos(ang)[None, :, None, :]
    s = jnp.sin(ang)[None, :, None, :]
    x0, x1 = x2[..., 0], x2[..., 1]
    return jnp.stack([x0 * c - x1 * s, x0 * s + x1 * c], axis=-1).reshape(x.shape)

def retention_mixer(q, k, v, g):
    f32 = jnp.float32
    bsz, t, _ = q.shape
    n_chunks = t // RET_CHUNK
    d = RET_HEAD_DIM
    q, k, v, g = (split_heads(u, RET_HEADS) for u in (q, k, v, g))
    theta = 1.0 / (10000.0 ** jnp.linspace(0.0, 1.0, d // 2, dtype=f32))
    ang = jnp.arange(t, dtype=f32)[:, None] * theta[None, :]
    q = rotary_interleaved(q, ang)
    k = rotary_interleaved(k, ang) * (d ** -0.5)
    v = v.astype(f32)
    log_gamma = jnp.log(1.0 - 2.0 ** (-5.0 - jnp.arange(RET_HEADS, dtype=f32)))
    shape = (bsz, n_chunks, RET_CHUNK, RET_HEADS, d)
    qc, kc, vc = q.reshape(shape), k.reshape(shape), v.reshape(shape)
    idx = jnp.arange(RET_CHUNK, dtype=f32)
    dist = jnp.abs(idx[:, None] - idx[None, :])
    d_mask = jnp.exp(dist[None] * log_gamma[:, None, None])
    sc = jnp.einsum('bcnhk,bcmhk->bchnm', qc, kc) * d_mask
    intra = jnp.einsum('bchnm,bcmhv->bcnhv', sc, vc)
    key_dec_f = jnp.exp((RET_CHUNK - 1 - idx)[:, None] * log_gamma)[..., None]
    key_dec_b = jnp.exp(idx[:, None] * log_gamma)[..., None]
    s_f = jnp.einsum('bcmhk,bcmhv->bchkv', kc * key_dec_f, vc)
    s_b = jnp.einsum('bcmhk,bcmhv->bchkv', kc * key_dec_b, vc)
    chunk_dec = jnp.exp(RET_CHUNK * log_gamma)[:, None, None]

    def chunk_step(carry, s_c):
        return carry * chunk_dec + s_c, carry

    xs = jnp.moveaxis(jnp.stack([s_f, jnp.flip(s_b, axis=1)], axis=0), 2, 0)
    _, prev = lax.scan(chunk_step, jnp.zeros(xs.shape[1:], f32), xs)
    r_f = jnp.moveaxis(prev[:, 0], 0, 1)
    r_b = jnp.moveaxis(jnp.flip(prev[:, 1], axis=0), 0, 1)
    q_dec_f = jnp.exp((idx + 1.0)[:, None] * log_gamma)[..., None]
    q_dec_b = jnp.exp((RET_CHUNK - idx)[:, None] * log_gamma)[..., None]
    cross = (jnp.einsum('bcnhk,bchkv->bcnhv', qc * q_dec_f, r_f)
             + jnp.einsum('bcnhk,bchkv->bcnhv', qc * q_dec_b, r_b))
    o = (intra + cross).reshape(bsz, t, RET_HEADS, d)
    o = o * lax.rsqrt(jnp.mean(o * o, axis=-1, keepdims=True) + NORM_EPS)
    return (o * jax.nn.silu(g.astype(f32))).reshape(bsz, t, RET_WIDTH).astype(g.dtype)

def setup_inputs(seed: int = 0) -> dict:
    key = jax.random.key(seed)
    ks = jax.random.split(key, 24)
    f32 = jnp.float32

    def nrm(k, shape, scale):
        return jax.random.normal(k, shape, f32) * scale

    def gain(k, shape, base=1.0):
        return base + 0.05 * jax.random.normal(k, shape, f32)

    return {
        'x': nrm(ks[0], (BATCH, SEQ, D_MODEL), 1.0),
        'pre_mix_g': gain(ks[1], (DEPTH, D_MODEL)),
        'w_in': nrm(ks[2], (DEPTH, D_MODEL, IN_COLS), D_MODEL ** -0.5),
        'na_rpb': nrm(ks[3], (DEPTH, NA_HEADS, 2 * NA_WIN_ROWS - 1, 2 * NA_WIN_COLS - 1), 0.5),
        'rw_mu_prev': jax.random.uniform(ks[4], (DEPTH, RW_IN_COLS), f32, 0.0, 0.5),
        'rw_mu_next': jax.random.uniform(ks[5], (DEPTH, RW_IN_COLS), f32, 0.0, 0.5),
        'rw_w0': jax.random.uniform(ks[6], (DEPTH, 2, RW_WIDTH), f32, -4.0, 1.0),
        'rw_w2': nrm(ks[7], (DEPTH, 2, DECAY_LORA, RW_WIDTH), 0.5 * DECAY_LORA ** -0.5),
        'rw_a0': nrm(ks[8], (DEPTH, 2, RW_WIDTH), 0.5),
        'rw_a2': nrm(ks[9], (DEPTH, 2, ICLR_LORA, RW_WIDTH), 0.5 * ICLR_LORA ** -0.5),
        'rw_k_k': gain(ks[10], (DEPTH, RW_WIDTH), 0.85),
        'rw_k_a': gain(ks[11], (DEPTH, RW_WIDTH), 1.0),
        'rw_r_k': nrm(ks[12], (DEPTH, RW_HEADS, RW_HEAD_DIM), 0.1),
        'rw_g2': nrm(ks[13], (DEPTH, GATE_LORA, RW_WIDTH), GATE_LORA ** -0.5),
        'rw_lnx_g': gain(ks[14], (DEPTH, RW_WIDTH)),
        'rw_lnx_b': nrm(ks[15], (DEPTH, RW_WIDTH), 0.02),
        'w_out': nrm(ks[16], (DEPTH, MIX_WIDTH, D_MODEL), MIX_WIDTH ** -0.5),
        'post_mix_g': gain(ks[17], (DEPTH, D_MODEL)),
        'pre_mlp_g': gain(ks[18], (DEPTH, D_MODEL)),
        'w_up': nrm(ks[19], (DEPTH, D_MODEL, D_FF), D_MODEL ** -0.5),
        'w_down': nrm(ks[20], (DEPTH, D_FF, D_MODEL), D_FF ** -0.5),
        'post_mlp_g': gain(ks[21], (DEPTH, D_MODEL)),
    }

def reference(x, pre_mix_g, w_in, na_rpb, rw_mu_prev, rw_mu_next, rw_w0, rw_w2, rw_a0, rw_a2,
              rw_k_k, rw_k_a, rw_r_k, rw_g2, rw_lnx_g, rw_lnx_b, w_out, post_mix_g, pre_mlp_g,
              w_up, w_down, post_mlp_g):
    bsz, t, _ = x.shape
    for l in range(DEPTH):
        h = rms_norm(x, pre_mix_g[l])
        z = h @ w_in[l]
        za, zb, zc = jnp.split(z, [NA_IN_COLS, NA_IN_COLS + RW_IN_COLS], axis=-1)
        qa, ka, va = (split_heads(u, NA_HEADS) for u in jnp.split(za, 3, axis=-1))
        ya = neighbourhood_attention(qa, ka, va, na_rpb[l])
        yb = rwkv7_mixer(zb, rw_mu_prev[l], rw_mu_next[l], rw_w0[l], rw_w2[l], rw_a0[l], rw_a2[l],
                         rw_k_k[l], rw_k_a[l], rw_r_k[l], rw_g2[l], rw_lnx_g[l], rw_lnx_b[l])
        qc, kc, vc, gc = jnp.split(zc, 4, axis=-1)
        yc = retention_mixer(qc, kc, vc, gc)
        y = jnp.concatenate([ya, yb, yc], axis=-1) @ w_out[l]
        x = x + rms_norm(y, post_mix_g[l])
        h = rms_norm(x, pre_mlp_g[l])
        u = jnp.square(jax.nn.relu(h @ w_up[l])) @ w_down[l]
        x = x + rms_norm(u, post_mlp_g[l])
    return x


_drawn_inputs = setup_inputs


def setup_inputs(seed=0):
    import zlib

    import numpy as np

    out = dict(_drawn_inputs(seed))
    spreads = {}
    factors = {'rw_w2': 2.84, 'rw_k_k': 4.04, 'rw_lnx_b': 5.356}
    for name, (base, spread) in spreads.items():
        noise = np.random.default_rng([zlib.crc32(name.encode()), seed]).standard_normal(out[name].shape)
        drawn = base * np.exp(spread * noise) if base else spread * noise
        out[name] = __import__('jax').numpy.asarray(drawn.astype(out[name].dtype))
    for name, factor in factors.items():
        out[name] = (out[name] * factor).astype(out[name].dtype)
    return out
```

```python
from contextlib import ExitStack
import math

import numpy as np

import concourse.bass as bass
from concourse import mybir

ALU = mybir.AluOpType
ACT = mybir.ActivationFunctionType
F32 = mybir.dt.float32
F32R = mybir.dt.float32r
AX_X = mybir.AxisListType.X
ds = bass.ds

P = 128
T = 256
TT = T // P
D = 2048
KT = D // P
NA_W, RW_W, RET_W = D // 4, 3 * D // 8, 3 * D // 8
NA_HEADS, NA_HD = NA_W // 64, 64
GRID_W, ROWS, WIN = 64, T // 64, 16
NA_T, RW_CT, RET_CT = 3 * NA_W // P, RW_W // P, RET_W // P
RW_T = 3 * RW_CT + 3
RET_T = 4 * RET_CT
W_IN_T = NA_T + RW_T + RET_T
FF = 4 * D
FF_T = FF // P
C = 64
NC = T // C
LEVELS = [2, 4, 8, 16, 32]
EPS, LNX_EPS = 1e-6, 64e-5
DECAY = math.exp(-0.5)

UNIT = 2048
RAW = 4
OUT_FIRST = W_IN_T
UP_FIRST = OUT_FIRST + KT
DOWN_FIRST = UP_FIRST + FF_T

VEC = {}
_at = 0
for _n, _w in (("g1", KT), ("g2", KT), ("mup", RW_T), ("mun", RW_T), ("w0", 2 * RW_CT), ("a0", 2 * RW_CT),
               ("kk", RW_CT), ("ka", RW_CT), ("rk", RW_CT), ("lg", RW_CT), ("lb", RW_CT)):
    VEC[_n] = (_at, _at + _w)
    _at += _w
VEC_N = _at
CST = {}
_at = 0
for _n, _w in (("ident", P), ("ones", P), ("turn", P), ("cos", T), ("sin", T), ("bm", 4 * P), ("lower", 2 * C),
               ("off", (len(LEVELS) + 1) * C), ("eye", C), ("keep", T), ("win", GRID_W)):
    CST[_n] = (_at, _at + _w)
    _at += _w
CST_N = _at


def constants():
    c = np.zeros((P, CST_N), np.float32)

    def put(name, a):
        c[:, CST[name][0]:CST[name][1]] = a.reshape(P, -1)

    put("ident", np.eye(P, dtype=np.float32))
    half = np.arange(P) // C
    put("ones", (half[:, None] == half[None]).astype(np.float32))
    turn = np.zeros((P, P), np.float32)
    for j in range(0, P, 2):
        turn[j + 1, j], turn[j, j + 1] = -1.0, 1.0
    put("turn", turn)
    theta = np.float32(1.0) / np.float32(10000.0) ** np.linspace(0.0, 1.0, P // 2, dtype=np.float32)
    ang = np.arange(T, dtype=np.float32)[:, None] * theta[None].astype(np.float32)
    put("cos", np.repeat(np.cos(ang).T, 2, axis=0))
    put("sin", np.repeat(np.sin(ang).T, 2, axis=0))
    j, t = np.arange(C)[:, None], np.arange(C)[None]
    strict = [(j < t), (j > t)]
    incl = [(j <= t), (j >= t)]
    bm = np.zeros((P, 2, 2, P), np.float32)
    for d in range(2):
        a_r = np.concatenate([strict[d], incl[d]], 1)
        bm[:, d, 0] = np.concatenate([a_r, a_r], 0)
        r_a = np.concatenate([incl[d], strict[d]], 1)
        bm[:, d, 1] = np.concatenate([r_a, r_a], 0)
    put("bm", bm)
    low = np.stack([strict[d].T for d in range(2)], 1).astype(np.float32)
    put("lower", np.concatenate([low, low], 0))
    off = np.stack([(j // (2 * m) == t // (2 * m)) & (j // m != t // m) for m in [1] + LEVELS], 1)
    put("off", np.concatenate([off, off], 0).astype(np.float32))
    put("eye", np.concatenate([np.eye(C), np.eye(C)], 0).astype(np.float32))
    keep = np.ones((P, T), np.float32)
    keep[:, 0::C] = 0.0
    put("keep", keep)
    col = np.arange(GRID_W)
    start = np.clip(col - WIN // 2, 0, GRID_W - WIN)
    seen = (col[None] >= start[:, None]) & (col[None] < start[:, None] + WIN)
    win = np.where(seen, 0.0, -1e30).astype(np.float32)
    put("win", np.concatenate([win[::-1], win[::-1]], 0))
    lg = np.log(1.0 - 2.0 ** (-5.0 - np.arange(RET_CT)))
    dist = np.abs(np.arange(3 * P)[None] - P - np.arange(P)[:, None])
    decay = np.exp(dist[:, None, :] * lg[None, :, None]) * P ** -0.5
    flip = np.zeros((P, P), np.float32)
    for p in range(P):
        flip[p, p // GRID_W * GRID_W + GRID_W - 1 - p % GRID_W] = 1.0
    return c, np.concatenate([decay.astype(np.float32).reshape(P, -1), flip], 1)


def layer(nc, x, pre_mix_g, w_in, na_rpb, rw_mu_prev, rw_mu_next, rw_w0, rw_w2, rw_a0, rw_a2, rw_k_k, rw_k_a,
          rw_r_k, rw_g2, rw_lnx_g, rw_lnx_b, w_out, post_mix_g, pre_mlp_g, w_up, w_down, post_mlp_g,
          cst_d, decay_d, out):
    with ExitStack() as ctx:
        def sb(name, shape, dt=F32):
            return ctx.enter_context(nc.sbuf_tensor(name, shape, dt))

        def sem(name):
            return ctx.enter_context(nc.semaphore(name))

        raw = sb("raw", [P, RAW, UNIT])
        w_hi = sb("w_hi", [P, 2, UNIT], F32R)
        w_lo = sb("w_lo", [P, 2, UNIT], F32R)
        act_hi = sb("act_hi", [P, KT, T], F32R)
        act_lo = sb("act_lo", [P, KT, T], F32R)
        u_hi = sb("u_hi", [P, 2, T], F32R)
        u_lo = sb("u_lo", [P, 2, T], F32R)
        cst = sb("cst", [P, CST_N])
        vec = sb("vec", [P, VEC_N])
        small = sb("small", [P, 256])
        ARENA = 24640
        arena = sb("arena", [P, ARENA])
        psum = ctx.enter_context(nc.psum_tensor("psum", [P, 8, 512], F32))
        bank = [psum[:, b] for b in range(8)]
        scores = psum[:, 2:4].rearrange("p e (t k) -> p e t k", t=TT)

        def const(name):
            return cst[:, CST[name][0]:CST[name][1]]

        def vect(name):
            return vec[:, VEC[name][0]:VEC[name][1]]

        ident, ones, turn = const("ident"), const("ones"), const("turn")
        bm_mask = const("bm").rearrange("p (d e t) -> p d e t", d=2, e=2)
        lower = const("lower").rearrange("p (d j) -> p d j", d=2)
        off = const("off").rearrange("p (m t) -> p m t", t=C)
        eye = const("eye")
        keep = const("keep")

        def cut(at, *shape):
            n = int(np.prod(shape))
            assert at + n <= ARENA, (at, n)
            v = arena[:, at:at + n]
            names = "abcd"[:len(shape)]
            if len(shape) == 1:
                return v
            return v.rearrange(f"p ({' '.join(names)}) -> p {' '.join(names)}",
                               **{k: s for k, s in zip(names[1:], shape[1:])})

        zs = cut(0, RW_T, T)
        zr, zk, zv = zs[:, 0:RW_CT], zs[:, RW_CT:2 * RW_CT], zs[:, 2 * RW_CT:3 * RW_CT]
        z_wd, z_ad, z_gd = (zs[:, 3 * RW_CT + n] for n in range(3))
        a0_ = RW_T * T
        sig_w = cut(a0_, 2, RW_CT, T)
        rate = cut(a0_ + 3072, 2, RW_CT, T)
        kkn = cut(a0_ + 6144, RW_CT, T)
        L = a0_ + 7680
        x_in = cut(L, TT, D)
        x_n = cut(L + 4096, TT, D)
        zpad = cut(L + 8192, 2, 2, T + 2)
        vstage = cut(L + 9300, P)
        w2s = cut(L, RW_W)
        a2s = cut(L + RW_W, RW_W)
        kk_ss = cut(L + 2 * RW_W, RW_CT, T)
        kk_sq = cut(L + 4 * RW_W, RW_CT, T)
        cs = cut(L, T)
        ce = cut(L + 256, T)
        e_inc = cut(L + 512, T)
        e_exc = cut(L + 768, T)
        e_inv = cut(L + 1024, T)
        kd = cut(L + 1280, 2, T)
        bn = cut(L + 1792, T)
        tmp = cut(L + 2048, T)
        zd = cut(L, 2 * NC, 2, C)
        xbd = cut(L + 1024, 2 * NC, P)
        p1s = cut(L + 2048, 2 * NC, C)
        ar = cut(L + 2560, 2, NC, 3 * C)
        bk = cut(L + 4096, 2, NC, 3 * C)
        bms = cut(L + 5632, 4 * NC, P)
        abd = cut(L + 7680, 2 * NC, P)
        bkt = cut(L + 8704, 2, 2 * NC, C)
        uv = cut(L + 9728, 2 * NC, 2, C)
        gs = cut(L + 10752, 2, C)
        state = cut(L + 10880, 2, C)
        state_dec = cut(L + 11008, 2, C)
        vst = cut(L + 11136, T)
        ec = small[:, 16:24].rearrange("p (d c) -> p d c", d=2)
        gate = cut(a0_, RW_CT, T)
        g2s = cut(a0_ + 3072, RW_W)
        ysq = cut(L, RW_CT * NC, C)
        y_rw = cut(a0_ + 6144, RW_CT, T)
        znr = cut(0, NA_T + RET_T, T)
        o_all = cut(9216, RET_CT, TT, P)
        v_cp = cut(10752, T)
        v_tok = cut(11008, TT, P)
        bias = cut(L, NA_HEADS, TT, T)
        decay = cut(L + 4096, RET_CT, 3 * P)
        W_ = L + 6400
        v_na = cut(W_, TT, NA_W)
        q_s = cut(W_ + 1024, T)
        k_s = cut(W_ + 1280, T)
        sx = cut(W_ + 1536, 2, TT, T)
        pts = cut(W_ + 2560, 2, TT, TT, P)
        yq = cut(W_ + 3584, TT, P)
        flip = cut(W_ + 3840, P)
        silu_s = cut(9216, RET_CT, T)
        qk = cut(W_, 2, T)
        qk_cos = cut(W_ + 512, 2, T)
        sts = cut(W_ + 1024, TT, T)
        y_f = cut(W_ + 1536, 2, T)
        junk = cut(W_ + 2048, TT, P)
        u = cut(0, FF_T, T)
        x1 = cut(16384, TT, D)
        gains = cut(20480, D)
        relu_t = cut(22528, 2, 512)
        o_sb = cut(0, TT, D)
        y_sb = cut(0, TT, D)

        s = {n: sem(n) for n in (
            "x_in", "consts_in", "vec_in", "lora_in", "g2_in", "bias_in", "flip_in", "decay_in", "gain_in", "x_again", "out_written",
            "ss_done", "ms_done", "sq_done", "rs_done", "xn_ready", "xt_done", "h_hi", "h_lo",
            "vec_t", "vec_ready", "coef_ready",
            "hi_done", "lo_done", "gemm_done", "bank_free", "pad_free", "zs_ready",
            "gates_ready", "lora_done", "lora_free", "kk_raw", "kk_sqd", "kk_summed", "kk_root", "kk_ready",
            "cum_ready", "exp_ready", "kb_ready", "bonus_in", "kd_scaled", "kd_summed", "pool_passed", "act_passed", "v_copied", "tilde_ready", "bm_done", "a_done",
            "bkt_done", "vb_done", "bm_ready", "a_ready", "bkt_ready", "vb_ready", "zd_ready", "t_done", "x_ready", "x_clear",
            "p1_done", "v_part", "p1_ready", "q_done", "z_ready", "gy_done", "g_low", "g_high", "u_done", "u_low", "u_high",
            "s_done", "s_ready", "dec_ready", "y_done", "y_copied", "y_added", "rw_cleared",
            "ln_ms", "ln_root", "ln_ready", "gate_done", "gate_ready", "yt_done", "y_rw_ready",
            "bias_ready", "vna_done", "vna_ready", "k_copied", "q_ready", "sc_done", "mx_ready", "p_ready", "rinv_ready",
            "pt_done", "pt_ready", "o_done", "yq_ready", "yqt_done", "y_na_hi", "y_na_lo",
            "silu_sig", "silu_ready", "rot_in", "rot_done", "qk_ready", "vt_done", "v_tok_ready", "st_done", "st_ready",
            "ro_done", "ro_ready", "ret_ms", "ret_root", "ret_rs", "on_ready", "ont_done", "yf_ready", "y_ret_hi",
            "y_rw_hi", "y_lo", "out_acc", "yss_done", "yms_done", "yroot_done", "yrs_done", "x1_ready", "hss_done",
            "relu_free", "uhi_done", "ulo_done", "down_done", "o_ready",
            "act_step", "dve_step", "pool_step")}
        raw_in = [sem(f"raw_in{r}") for r in range(RAW)]
        block = ctx.enter_context(nc.Block())

        def stream(eng, first, count, convert, drain=None):
            quads = count // 4
            convert(first, 0)
            convert(first + 1, 0)
            with eng.Fori(0, quads - 1) as i:
                for pair in range(2):
                    convert(first + 2 * pair + 2, i)
                    convert(first + 2 * pair + 3, i)
                    if drain:
                        drain(pair, i)
            rest = [first + n for n in range(4 * quads - 2, count)]
            pairs = list(range(2 * quads - 2, (count + 1) // 2))
            while rest or pairs:
                for n in rest[:2]:
                    convert(n, 0)
                rest = rest[2:]
                if pairs and drain:
                    drain(pairs[0], 0)
                pairs = pairs[1:]

        def raw_landed(eng, c, i):
            eng.wait_ge(raw_in[c % RAW], 16 * (i + c // RAW + 1))

        def link(eng, counter, name, ins):
            counter[0] += 1
            ins.then_inc(s[name], 1)
            eng.wait_ge(s[name], counter[0])

        def stand(eng, name, value, passed):
            eng.wait_ge(s[name], value)
            eng.sem_inc(s[passed], 1)

        def tile_of(view, i):
            return view[:, ds(i, 1), :].rearrange("p a t -> p (a t)")

        def chunks(view):
            return view.rearrange("p (c t) -> p c t", t=C)

        RW_PAIRS, NR_PAIRS, UP_PAIRS = (RW_T + 1) // 2, (NA_T + RET_T) // 2, FF_T // 2

        @block.sync
        def _(sp):
            sp.dma_start(x_in, x[0].rearrange("(t p) d -> p t d", p=P)).then_inc(s["x_in"], 16)
            sp.dma_start(cst[:], cst_d).then_inc(s["consts_in"], 16)
            for name, v in (("g1", pre_mix_g), ("g2", pre_mlp_g), ("mup", rw_mu_prev), ("mun", rw_mu_next),
                            ("w0", rw_w0.rearrange("l d c -> l (d c)")), ("a0", rw_a0.rearrange("l d c -> l (d c)")),
                            ("kk", rw_k_k), ("ka", rw_k_a), ("rk", rw_r_k.rearrange("l h c -> l (h c)")),
                            ("lg", rw_lnx_g), ("lb", rw_lnx_b)):
                a, b = VEC[name]
                sp.dma_start(vstage[a:b, :], v.rearrange("l (t p) -> (l t) p", p=P)).then_inc(s["vec_in"], 16)

            def fetch(c, i, src, wait=True):
                if wait:
                    sp.wait_ge(s["lo_done"], 4 * i + c - RAW + 1)
                dst = raw[:, c % RAW, :]
                if len(src.shape) == 3:
                    dst = dst.rearrange("p (k c) -> p k c", k=KT)
                sp.dma_start(dst, src).then_inc(raw_in[c % RAW], 16)

            w_in_v = w_in[0].rearrange("(k p) c -> p k c", p=P)
            w_up_v = w_up[0].rearrange("(k p) c -> p k c", p=P)
            w_out_v = w_out[0].rearrange("(k p) c -> p k c", p=P)
            w_down_v = w_down[0].rearrange("(k p) c -> p k c", p=P)

            def columns(view, tile):
                return view[:, :, ds(tile * P, P)]

            def rows(view, tile):
                return view[:, ds(tile, 1), :].rearrange("p k c -> p (k c)")

            for n in range(RAW):
                fetch(n, 0, columns(w_in_v, NA_T + n), wait=False)
            with sp.Fori(0, (RW_T - 5) // 4) as i:
                for k in range(4):
                    fetch(4 + k, i, columns(w_in_v, i * 4 + (NA_T + 4 + k)))
            fetch(RW_T - 1, 0, columns(w_in_v, NA_T + RW_T - 1))
            with sp.Fori(0, NA_T // 4) as i:
                for k in range(4):
                    fetch(RW_T + k, i, columns(w_in_v, i * 4 + k))
            sp.wait_ge(s["y_rw_ready"], 1)
            for i in range(ROWS):
                half = GRID_W * (i % 2)
                for r in range(ROWS):
                    src = bass.AP(tensor=na_rpb.tensor, offset=(r - i + 7) * 31 + WIN - 1 - (GRID_W - 1),
                                  ap=[[1, GRID_W], [15 * 31, NA_HEADS], [1, GRID_W]])
                    dst = bias[half:half + GRID_W, :, i // 2, r * GRID_W:(r + 1) * GRID_W]
                    sp.dma_start(dst, src).then_inc(s["bias_in"], 16)
            sp.dma_start(flip, decay_d[:, RET_CT * 3 * P:]).then_inc(s["flip_in"], 16)
            sp.dma_start(decay.rearrange("p h x -> p (h x)"), decay_d[:, 0:RET_CT * 3 * P]).then_inc(s["decay_in"], 16)
            with sp.Fori(0, RET_T // 4) as i:
                for k in range(4):
                    fetch(RW_T + NA_T + k, i, columns(w_in_v, i * 4 + (RW_T + NA_T + k)))
            with sp.Fori(0, KT // 4) as i:
                for k in range(4):
                    fetch(OUT_FIRST + k, i, rows(w_out_v, i * 4 + k))
            sp.wait_ge(s["y_na_lo"], NA_T // 3)
            sp.wait_ge(s["y_lo"], RW_CT + RET_CT)
            sp.dma_start(x1, x[0].rearrange("(t p) d -> p t d", p=P)).then_inc(s["x_again"], 16)
            sp.dma_start(gains, post_mix_g.broadcast_to([P, D])).then_inc(s["gain_in"], 16)
            with sp.Fori(0, FF_T // 4) as i:
                for k in range(4):
                    fetch(UP_FIRST + k, i, columns(w_up_v, i * 4 + k))
            sp.wait_ge(s["x1_ready"], TT)
            sp.dma_start(gains, post_mlp_g.broadcast_to([P, D])).then_inc(s["gain_in"], 16)
            with sp.Fori(0, FF_T // 4) as i:
                for k in range(4):
                    fetch(DOWN_FIRST + k, i, rows(w_down_v, i * 4 + k))
            for t in range(TT):
                sp.wait_ge(s["o_ready"], t + 1)
                sp.dma_start(out[0, t * P:(t + 1) * P, :], o_sb[:, t]).then_inc(s["out_written"], 16)
            sp.wait_ge(s["out_written"], 16 * TT)

        @block.gpsimd
        def _(pool):
            step = [0]

            def nxt(ins):
                link(pool, step, "pool_step", ins)

            for _ in range(2):
                pool.sem_inc(s["relu_free"], 1)
            pool.wait_ge(s["h_lo"], KT)
            pool.dma_start(w2s, rw_w2.rearrange("l d r c -> (l d r) c")).then_inc(s["lora_in"], 16)
            pool.dma_start(a2s, rw_a2.rearrange("l d r c -> (l d r) c")).then_inc(s["lora_in"], 16)

            pool.wait_ge(s["lora_free"], 2 * RW_CT)
            pool.wait_ge(s["kk_ready"], 1)
            pool.memset(abd, 0.0).then_inc(s["rw_cleared"], 1)
            with pool.Fori(0, RW_CT) as i:
                k_i = tile_of(zk, i)
                for d in range(2):
                    stand(pool, "kd_scaled", i * 2 + d + 1, "pool_passed")
                    pool.tensor_tensor(kd[:, d], kd[:, d], k_i, ALU.mult).then_inc(s["pool_step"], 1)
                    if d == 1:
                        stand(pool, "tilde_ready", i * 2 + 1, "pool_passed")
                    rate_i = rate[:, d, ds(i, 1), :].rearrange("p a t -> p (a t)")
                    pool.tensor_tensor(bn, tile_of(kkn, i), rate_i, ALU.mult).then_inc(s["kb_ready"], 1)
                pool.wait_ge(s["pool_step"], i * 2 + 2)
                pool.tensor_tensor(tmp, kd[:, 0], kd[:, 1], ALU.add).then_inc(s["kd_summed"], 1)
                stand(pool, "vb_done", i, "pool_passed")
                pool.tensor_copy(vst, tile_of(zv, i)).then_inc(s["v_copied"], 1)
                stand(pool, "kd_summed", i + 1, "pool_passed")
                stand(pool, "tilde_ready", i * 2 + 2, "pool_passed")
                pool.memset(xbd, 0.0).then_inc(s["x_clear"], 1)
                for n in (1, 2):
                    stand(pool, "s_ready", i * 3 + n, "pool_passed")
                    for d in range(2):
                        c = n if d == 0 else NC - 1 - n
                        last = pool.tensor_scalar(state_dec[:, d], state[:, d], ec[:, d, c:c + 1], None, ALU.mult)
                    last.then_inc(s["dec_ready"], 1)

            pool.wait_ge(s["ln_ms"], 1)
            pool.dma_start(g2s, rw_g2[0]).then_inc(s["g2_in"], 16)

            pool.wait_ge(s["bias_in"], 16 * ROWS * ROWS)
            win = const("win").unsqueeze(1).broadcast_to([P, TT * ROWS, GRID_W])
            for h in range(NA_HEADS):
                b_h = bias[:, h].rearrange("p t (r c) -> p (t r) c", c=GRID_W)
                pool.tensor_tensor(b_h, b_h, win, ALU.add).then_inc(s["bias_ready"], 1)

            pool.wait_ge(s["bank_free"], RW_PAIRS + NR_PAIRS)
            with pool.Fori(0, NA_T // 3) as i:
                stand(pool, "sc_done", i, "pool_passed")
                pool.tensor_copy(k_s, tile_of(znr, i + NA_T // 3)).then_inc(s["k_copied"], 1)
            pool.wait_ge(s["silu_sig"], 1)
            g_all = znr[:, NA_T + 3 * RET_CT:NA_T + 4 * RET_CT]
            pool.tensor_tensor(g_all, g_all, silu_s, ALU.mult).then_inc(s["silu_ready"], 1)
            pool.wait_ge(s["y_na_lo"], NA_T // 3)
            with pool.Fori(0, RET_CT) as i:
                pool.wait_ge(s["qk_ready"], 2 * i)
                for n in range(2):
                    pool.tensor_tensor(qk_cos[:, n], znr[:, ds(i + (NA_T + n * RET_CT), 1), :].rearrange("p a t -> p (a t)"),
                                       const("cos"), ALU.mult).then_inc(s["rot_in"], 1)
                pool.wait_ge(s["vt_done"], i)
                pool.tensor_copy(v_cp, znr[:, ds(i + (NA_T + 2 * RET_CT), 1), :].rearrange("p a t -> p (a t)")).then_inc(
                    s["rot_in"], 1)

            with pool.Fori(0, UP_PAIRS // 2) as i:
                for k in range(2):
                    pool.wait_ge(s["bank_free"], i * 2 + (RW_PAIRS + NR_PAIRS + k + 1))
                    dst = u[:, ds(i * 4 + 2 * k, 2), :].rearrange("p a t -> p (a t)")
                    pool.tensor_tensor(dst, relu_t[:, k], relu_t[:, k], ALU.mult).then_inc(s["relu_free"], 1)

        @block.vector
        def _(dve):
            step = [0]

            def nxt(ins):
                link(dve, step, "dve_step", ins)

            dve.memset(zpad[:, 0], 0.0).then_inc(s["pad_free"], 1)
            dve.memset(zpad[:, 1], 0.0).then_inc(s["pad_free"], 1)
            dve.wait_ge(s["ss_done"], TT)
            dve.tensor_scalar(small[:, 2:4], small[:, 0:2], 1.0 / D, EPS, ALU.mult, ALU.add).then_inc(s["ms_done"], 1)
            dve.wait_ge(s["sq_done"], 1)
            dve.reciprocal(small[:, 6:8], small[:, 4:6]).then_inc(s["rs_done"], 1)
            dve.wait_ge(s["rs_done"], 1)
            for t in range(TT):
                dve.tensor_scalar(x_n[:, t], x_in[:, t], small[:, 6 + t:7 + t], None, ALU.mult).then_inc(s["xn_ready"], 1)
            dve.wait_ge(s["vec_t"], 1)
            dve.tensor_copy(vec[:], bank[1][:, 0:VEC_N]).then_inc(s["vec_ready"], 1)
            dve.wait_ge(s["vec_ready"], 1)
            nxt(dve.tensor_scalar(small[:, 64:64 + RW_T], vect("mup"), -1.0, 1.0, ALU.mult, ALU.add))
            dve.tensor_tensor(small[:, 64:64 + RW_T], small[:, 64:64 + RW_T], vect("mun"), ALU.subtract).then_inc(
                s["coef_ready"], 1)
            dve.tensor_scalar(small[:, 32:32 + RW_CT], vect("ka"), -1.0, 1.0, ALU.mult, ALU.add)
            dve.tensor_scalar(small[:, 48:48 + RW_CT], vect("kk"), -1.0, None, ALU.mult).then_inc(s["coef_ready"], 1)

            def split_h(gain):
                for k in range(KT):
                    dve.wait_ge(s["h_hi"], gain[1] + k + 1)
                    dve.scalar_tensor_tensor(act_lo[:, k], bank[2 + k % 6][:, 0:T], vect(gain[0])[:, k:k + 1],
                                             act_hi[:, k].bitcast(F32), ALU.mult, ALU.subtract).then_inc(s["h_lo"], 1)

            split_h(("g1", 0))

            def lo(c, i):
                dve.wait_ge(s["hi_done"], 4 * i + c + 1)
                if not (isinstance(i, int) and 4 * i + c < 2):
                    dve.wait_ge(s["gemm_done"], 4 * i + c - 1)
                dve.tensor_tensor(w_lo[:, c % 2], raw[:, c % RAW], w_hi[:, c % 2].bitcast(F32),
                                  ALU.subtract).then_inc(s["lo_done"], 1)

            def shift(k, i):
                n = 2 if not (isinstance(i, int) and 2 * i + k == RW_PAIRS - 1) else 1
                dve.wait_ge(s["bank_free"], 2 * i + k + 1)
                for mu, at in (("mup", 0), ("mun", 2)):
                    for j in range(n):
                        ct = 4 * i + 2 * k + j
                        z = zs[:, ds(ct, 1), :].rearrange("p a t -> p (a t)")
                        last = dve.scalar_tensor_tensor(z, zpad[:, k % 2, j, at:at + T], vect(mu)[:, ds(ct, 1)], z,
                                                        ALU.mult, ALU.add)
                        if at == 0:
                            last.then_inc(s["zs_ready"], 1)
                    if at == 0:
                        dve.wait_ge(s["zs_ready"], 2 * (2 * i + k) + n)
                last.then_inc(s["pad_free"], 1)

            stream(dve, 0, RW_T, lo, shift)

            dve.wait_ge(s["kk_root"], 3)
            nxt(dve.tensor_scalar(kk_ss, kk_ss, 1e-12, None, ALU.max))
            nxt(dve.reciprocal(kk_ss, kk_ss))
            dve.tensor_tensor(kkn, kkn, kk_ss, ALU.mult).then_inc(s["kk_ready"], 1)
            dve.wait_ge(s["kk_ready"], 1)
            dve.wait_ge(s["lora_free"], 2 * RW_CT)
            dve.wait_ge(s["rw_cleared"], 1)

            base = step[0]
            with dve.Fori(0, RW_CT) as i:
                kk_i, r_i, v_i = tile_of(kkn, i), tile_of(zr, i), tile_of(zv, i)
                y_i = chunks(tile_of(zk, i))
                for d in range(2):
                    s_i = sig_w[:, d, ds(i, 1), :].rearrange("p a t -> p (a t)")
                    if d == 1:
                        dve.wait_ge(s["exp_ready"], 6 * i + 3)
                    dve.tensor_tensor_scan(cs, keep, s_i, 0.0, ALU.mult, ALU.add).then_inc(s["cum_ready"], 1)
                    dve.wait_ge(s["cum_ready"], 5 * i + 2 * d + 1)
                    if d == 0:
                        dve.tensor_tensor(ce, cs, s_i, ALU.subtract).then_inc(s["cum_ready"], 1)
                    else:
                        dve.tensor_tensor(chunks(ce), chunks(cs)[:, :, C - 1:C].broadcast_to([P, NC, C]), chunks(cs),
                                          ALU.subtract).then_inc(s["cum_ready"], 1)
                        dve.wait_ge(s["cum_ready"], 5 * i + 4)
                        dve.tensor_tensor(cs, ce, s_i, ALU.add).then_inc(s["cum_ready"], 1)
                    dve.wait_ge(s["exp_ready"], 6 * i + 3 * d + 3)
                    dve.wait_ge(s["kb_ready"], 2 * i + d + 1)
                    last_t = C - 1 if d == 0 else 0
                    dve.tensor_copy(ec[:, d], chunks(e_inc)[:, :, last_t])
                    a_, k_ = ar[:, d], bk[:, d]
                    dve.tensor_tensor(a_[:, :, 0:C], chunks(kk_i), chunks(e_exc), ALU.mult)
                    dve.tensor_tensor(a_[:, :, C:2 * C], chunks(r_i), chunks(e_inc), ALU.mult)
                    dve.tensor_tensor(a_[C:P, :, 2 * C:3 * C], chunks(kk_i)[C:P], chunks(e_exc)[C:P], ALU.mult)
                    dve.scalar_tensor_tensor(k_[:, :, 0:C], chunks(bn), -1.0, chunks(e_inv), ALU.mult, ALU.mult)
                    dve.tensor_tensor(k_[:, :, C:2 * C], chunks(kd[:, d]), chunks(e_inv), ALU.mult)
                    dve.scalar_tensor_tensor(k_[C:P, :, 2 * C:3 * C], chunks(bn)[C:P], -1.0, chunks(e_inv)[C:P],
                                             ALU.mult, ALU.mult).then_inc(s["tilde_ready"], 1)
                dve.wait_ge(s["kd_summed"], i + 1)
                dve.scalar_tensor_tensor(tmp, tmp, vect("rk")[:, ds(i, 1)], r_i, ALU.mult, ALU.mult).then_inc(
                    s["bonus_in"], 1)
                dve.wait_ge(s["vb_done"], i + 1)
                uv_d = uv.rearrange("p (d c) e v -> p d c e v", d=2)
                v_ps = bank[5][:, 0:T].rearrange("p (c v) -> p c v", v=C)
                for d in range(2):
                    dve.tensor_copy(uv_d[C:P, d, :, 0, :], v_ps[C:P])
                    dve.tensor_copy(uv_d[0:C, d, :, 1, :], v_ps[0:C]).then_inc(s["vb_ready"], 1)
                dve.tensor_tensor(r_i, bank[5][:, T:2 * T], v_i, ALU.mult).then_inc(s["vb_ready"], 1)
                for d in range(2):
                    dve.wait_ge(s["bm_done"], 2 * i + d + 1)
                    for e in range(2):
                        dve.tensor_tensor(bms[:, (2 * d + e) * NC:(2 * d + e + 1) * NC],
                                          bank[2 * d + e].rearrange("p (c t) -> p c t", t=P),
                                          bm_mask[:, d, e].unsqueeze(1).broadcast_to([P, NC, P]),
                                          ALU.mult).then_inc(s["bm_ready"], 1)
                dve.wait_ge(s["a_done"], i + 1)
                a_ps = bank[4].rearrange("p (d c j) -> p d c j", d=2, c=NC)
                for e in range(2):
                    h = slice(e * C, e * C + C)
                    for d in range(2):
                        last = dve.tensor_tensor(abd[h, d * NC:(d + 1) * NC, h], a_ps[h, d],
                                                 lower[h, d].unsqueeze(1).broadcast_to([C, NC, C]), ALU.mult)
                last.then_inc(s["a_ready"], 1)
                dve.wait_ge(s["bm_ready"], 4 * i + 4)
                for e in range(2):
                    h = slice(e * C, e * C + C)
                    for d in range(2):
                        last = dve.tensor_tensor(p1s[h, d * NC:(d + 1) * NC],
                                                 bms[h, (2 * d + e) * NC:(2 * d + e + 1) * NC, h],
                                                 off[h, 0].unsqueeze(1).broadcast_to([C, NC, C]), ALU.mult)
                last.then_inc(s["dve_step"], 1)
                dve.wait_ge(s["dve_step"], i + (base + 1))
                twice = [P, 2 * NC, 2, C]
                dve.tensor_tensor(zd, p1s.unsqueeze(2).broadcast_to(twice),
                                  eye.unsqueeze(1).unsqueeze(1).broadcast_to(twice), ALU.add).then_inc(s["zd_ready"], 1)
                q_ps = bank[5].rearrange("p (n t) -> p n t", t=C)
                for n in range(len(LEVELS)):
                    dve.wait_ge(s["p1_done"], 5 * i + n + 1)
                    dve.tensor_tensor(p1s, bank[4].rearrange("p (n t) -> p n t", t=C),
                                      off[:, n + 1].unsqueeze(1).broadcast_to([P, 2 * NC, C]),
                                      ALU.mult).then_inc(s["p1_ready"], 1)
                    dve.wait_ge(s["q_done"], 5 * i + n + 1)
                    if n < len(LEVELS) - 1:
                        dve.tensor_tensor(zd, q_ps.unsqueeze(2).broadcast_to(twice), zd, ALU.add).then_inc(
                            s["zd_ready"], 1)
                    else:
                        for e in range(2):
                            h = slice(e * C, e * C + C)
                            last = dve.tensor_tensor(abd[h, :, h], q_ps[h], zd[h, :, 0], ALU.add)
                        last.then_inc(s["z_ready"], 1)
                for n in range(NC):
                    gy = [bank[n % 2 + 4 * e][:, 0:2 * C].rearrange("p (d v) -> p d v", d=2) for e in range(2)]
                    both = slice(n, 2 * NC - n, 2 * NC - 1 - 2 * n)
                    dve.wait_ge(s["gy_done"], 4 * i + n + 1)
                    dve.tensor_copy(gs[C:P], gy[1][C:P]).then_inc(s["g_high"], 1)
                    dve.wait_ge(s["u_done"], 4 * i + n + 1)
                    dve.tensor_copy(uv[C:P, both, 1], bank[2][C:P, 0:2 * C].rearrange("p (d v) -> p d v", d=2)).then_inc(
                        s["u_high"], 1)
                    if n < NC - 1:
                        dve.wait_ge(s["s_done"], 3 * i + n + 1)
                        if n:
                            dve.wait_ge(s["dec_ready"], 2 * i + n)
                        for d in range(2):
                            c = n if d == 0 else NC - 1 - n
                            new = bank[3][:, d * C:(d + 1) * C]
                            if n == 0:
                                last = dve.tensor_scalar(state[:, d], new, ec[:, d, c:c + 1], None, ALU.mult)
                            else:
                                last = dve.scalar_tensor_tensor(state[:, d], new, ec[:, d, c:c + 1], state_dec[:, d],
                                                                ALU.mult, ALU.add)
                        last.then_inc(s["s_ready"], 1)
                    if n >= 2:
                        dve.wait_ge(s["y_done"], 4 * i + n + 1)
                        dve.wait_ge(s["y_copied"], 2 * i + 2)
                        order = slice(NC - 1 - n, n + 1, 2 * n - NC + 1)
                        dve.tensor_tensor(y_i[0:C, order], gy[1][0:C], y_i[0:C, order], ALU.add)
                        dve.tensor_tensor(y_i[C:P, order], gy[0][C:P], y_i[C:P, order], ALU.add).then_inc(
                            s["y_added"], 1)
            step[0] = base + RW_CT

            dve.wait_ge(s["y_added"], 2 * RW_CT)
            y = zk.rearrange("p i (c v) -> p (i c) v", v=C)
            N = RW_CT * NC
            mean, rstd = small[:, 96:96 + N], small[:, 128:128 + N]
            wide = [P, N, C]
            nxt(dve.tensor_reduce(mean, y, AX_X, ALU.add))
            nxt(dve.tensor_scalar(mean, mean, -1.0 / C, None, ALU.mult))
            nxt(dve.tensor_tensor(y, y, mean.unsqueeze(2).broadcast_to(wide), ALU.add))
            nxt(dve.tensor_tensor(ysq, y, y, ALU.mult))
            nxt(dve.tensor_reduce(rstd, ysq, AX_X, ALU.add))
            dve.tensor_scalar(rstd, rstd, 1.0 / C, LNX_EPS, ALU.mult, ALU.add).then_inc(s["ln_ms"], 1)
            dve.wait_ge(s["ln_root"], 1)
            nxt(dve.reciprocal(rstd, rstd))
            dve.tensor_tensor(y, y, rstd.unsqueeze(2).broadcast_to(wide), ALU.mult).then_inc(s["ln_ready"], 1)
            for t in range(RW_CT):
                dve.wait_ge(s["yt_done"], t // 2 + 1)
                nxt(dve.tensor_scalar(y_rw[:, t], bank[5 + t // 2][:, (t % 2) * T:(t % 2 + 1) * T],
                                      vect("lg")[:, t:t + 1], vect("lb")[:, t:t + 1], ALU.mult, ALU.add))
            nxt(dve.tensor_tensor(y_rw, y_rw, zr, ALU.add))
            dve.wait_ge(s["gate_ready"], 3)
            dve.tensor_tensor(y_rw, y_rw, gate, ALU.mult).then_inc(s["y_rw_ready"], 1)

            stream(dve, RW_T, NA_T + RET_T, lo)

            for k in range(RW_CT):
                dve.wait_ge(s["y_rw_hi"], k + 1)
                dve.tensor_tensor(act_lo[:, NA_T // 3 + k], y_rw[:, k], act_hi[:, NA_T // 3 + k].bitcast(F32),
                                  ALU.subtract).then_inc(s["y_lo"], 1)
            base = step[0]
            with dve.Fori(0, NA_T // 3) as i:
                dve.wait_ge(s["sc_done"], i)
                dve.tensor_scalar(q_s, tile_of(znr, i), NA_HD ** -0.5, None, ALU.mult).then_inc(s["q_ready"], 1)
                dve.wait_ge(s["sc_done"], i + 1)
                top = small[:, 160:164]
                dve.tensor_reduce(top.rearrange("p (e t) -> p e t", e=2), scores, AX_X, ALU.max).then_inc(s["dve_step"], 1)
                dve.wait_ge(s["dve_step"], i + (base + 1))
                dve.tensor_scalar(top, top, -1.0, None, ALU.mult).then_inc(s["mx_ready"], 1)
                dve.wait_ge(s["p_ready"], 4 * i + 4)
                dve.reciprocal(small[:, 168:172], small[:, 164:168]).then_inc(s["rinv_ready"], 1)
                for e in range(2):
                    dve.wait_ge(s["pt_done"], 1 * i + 1)
                    dve.tensor_copy(pts[:, e], bank[4 + e].rearrange("p (a b q) -> p a b q", a=2, b=2)).then_inc(
                        s["pt_ready"], 1)
                dve.wait_ge(s["y_na_hi"], i + 1)
                dve.tensor_tensor(tile_of(act_lo, i), bank[7][:, 0:T], tile_of(act_hi, i).bitcast(F32),
                                  ALU.subtract).then_inc(s["y_na_lo"], 1)

            step[0] = base + NA_T // 3

            with dve.Fori(0, RET_CT) as i:
                dve.wait_ge(s["rot_done"], i + 1)
                dve.wait_ge(s["rot_in"], 3 * i + 2)
                dve.wait_ge(s["st_done"], i)
                sin2 = const("sin").unsqueeze(1).broadcast_to([P, 2, T])
                dve.tensor_tensor(qk, bank[2].rearrange("p (a t) -> p a t", a=2), sin2, ALU.mult).then_inc(
                    s["qk_ready"], 1)
                dve.wait_ge(s["qk_ready"], 2 * i + 1)
                dve.tensor_tensor(qk, qk, qk_cos, ALU.add).then_inc(s["qk_ready"], 1)
                dve.wait_ge(s["st_done"], i + 1)
                dve.wait_ge(s["ro_done"], i)
                dec_i = decay[:, ds(i, 1), :].rearrange("p a x -> p (a x)")
                for m in range(TT):
                    last = dve.tensor_tensor(sts[:, m], bank[3][:, m * T:(m + 1) * T],
                                             dec_i[:, P - m * P:P - m * P + T], ALU.mult)
                last.then_inc(s["st_ready"], 1)
            ss = small[:, 176:176 + RET_CT * TT]
            dve.wait_ge(s["ro_ready"], 3 * RET_CT)
            dve.tensor_scalar(ss, ss, 1.0 / P, EPS, ALU.mult, ALU.add).then_inc(s["ret_ms"], 1)
            dve.wait_ge(s["ret_root"], 1)
            dve.reciprocal(ss, ss).then_inc(s["ret_rs"], 1)
            dve.wait_ge(s["ret_rs"], 1)
            o_flat = o_all.rearrange("p h t v -> p (h t) v")
            dve.tensor_tensor(o_flat, o_flat, ss.unsqueeze(2).broadcast_to([P, RET_CT * TT, P]), ALU.mult).then_inc(
                s["on_ready"], 1)
            dve.wait_ge(s["silu_ready"], 1)
            for h in range(RET_CT):
                k = (NA_W + RW_W) // P + h
                dve.wait_ge(s["ont_done"], h + 1)
                if h >= 2:
                    dve.wait_ge(s["y_ret_hi"], h - 1)
                dve.tensor_tensor(y_f[:, h % 2], bank[2 + h][:, 0:T], znr[:, NA_T + 3 * RET_CT + h],
                                  ALU.mult).then_inc(s["yf_ready"], 1)
                dve.wait_ge(s["y_ret_hi"], h + 1)
                dve.tensor_tensor(act_lo[:, k], y_f[:, h % 2], act_hi[:, k].bitcast(F32),
                                  ALU.subtract).then_inc(s["y_lo"], 1)

            stream(dve, OUT_FIRST, KT, lo)

            dve.wait_ge(s["yss_done"], TT)
            rs = small[:, 192:194]
            dve.tensor_scalar(rs, rs, 1.0 / D, EPS, ALU.mult, ALU.add).then_inc(s["yms_done"], 1)
            dve.wait_ge(s["yroot_done"], 1)
            dve.reciprocal(rs, rs).then_inc(s["yrs_done"], 1)
            dve.wait_ge(s["yrs_done"], 1)
            dve.wait_ge(s["x_again"], 16)
            dve.wait_ge(s["gain_in"], 16)
            for t in range(TT):
                y_t = psum[:, 4 * t:4 * t + 4].rearrange("p b n -> p (b n)")
                nxt(dve.scalar_tensor_tensor(y_sb[:, t], y_t, rs[:, t:t + 1], gains, ALU.mult, ALU.mult))
                dve.tensor_tensor(x1[:, t], x1[:, t], y_sb[:, t], ALU.add).then_inc(s["x1_ready"], 1)
            dve.wait_ge(s["hss_done"], TT)
            h2 = small[:, 208:210]
            dve.tensor_scalar(h2, h2, 1.0 / D, EPS, ALU.mult, ALU.add).then_inc(s["yms_done"], 1)
            dve.wait_ge(s["yroot_done"], 2)
            dve.reciprocal(h2, h2).then_inc(s["yrs_done"], 1)
            dve.wait_ge(s["yrs_done"], 2)
            for t in range(TT):
                dve.tensor_scalar(y_sb[:, t], x1[:, t], h2[:, t:t + 1], None, ALU.mult).then_inc(s["xn_ready"], 1)
            split_h(("g2", KT))

            stream(dve, UP_FIRST, FF_T, lo)

            def lo_down(c, i):
                lo(c, i)
                m = c - DOWN_FIRST
                dve.wait_ge(s["uhi_done"], 4 * i + m + 1)
                dve.tensor_tensor(u_lo[:, c % 2], u[:, ds(4 * i + m, 1), :].rearrange("p a t -> p (a t)"),
                                  u_hi[:, c % 2].bitcast(F32), ALU.subtract).then_inc(s["ulo_done"], 1)

            stream(dve, DOWN_FIRST, FF_T, lo_down)

            dve.wait_ge(s["yss_done"], 2 * TT)
            dve.tensor_scalar(rs, rs, 1.0 / D, EPS, ALU.mult, ALU.add).then_inc(s["yms_done"], 1)
            dve.wait_ge(s["yroot_done"], 3)
            dve.reciprocal(rs, rs).then_inc(s["yrs_done"], 1)
            dve.wait_ge(s["yrs_done"], 3)
            dve.wait_ge(s["gain_in"], 32)
            for t in range(TT):
                y_t = psum[:, 4 * t:4 * t + 4].rearrange("p b n -> p (b n)")
                nxt(dve.scalar_tensor_tensor(o_sb[:, t], y_t, rs[:, t:t + 1], gains, ALU.mult, ALU.mult))
                dve.tensor_tensor(o_sb[:, t], x1[:, t], o_sb[:, t], ALU.add).then_inc(s["o_ready"], 1)

        @block.scalar
        def _(act):
            def norm_sums(src, junk_, sums, name, waits):
                for t in range(TT):
                    act.wait_ge(*waits(t))
                    act.activation(junk_[:, t], src[:, t], ACT.Square, accum_out=sums[:, t:t + 1]).then_inc(s[name], 1)

            norm_sums(x_in, x_n, small[:, 0:2], "ss_done", lambda t: (s["x_in"], 16))
            act.wait_ge(s["ms_done"], 1)
            act.activation(small[:, 4:6], small[:, 2:4], ACT.Sqrt).then_inc(s["sq_done"], 1)
            act.wait_ge(s["vec_ready"], 1)

            def split_h(gain):
                for k in range(KT):
                    act.wait_ge(s["xt_done"], gain[1] + k + 1)
                    act.activation(act_hi[:, k], bank[2 + k % 6][:, 0:T], ACT.Copy,
                                   scale=vect(gain[0])[:, k:k + 1]).then_inc(s["h_hi"], 1)

            split_h(("g1", 0))
            act.wait_ge(s["coef_ready"], 2)

            def hi(c, i):
                raw_landed(act, c, i)
                if not (isinstance(i, int) and 4 * i + c < 2):
                    act.wait_ge(s["gemm_done"], 4 * i + c - 1)
                act.activation(w_hi[:, c % 2], raw[:, c % RAW], ACT.Copy).then_inc(s["hi_done"], 1)

            def to_zs(k, i):
                n = 2 if not (isinstance(i, int) and 2 * i + k == RW_PAIRS - 1) else 1
                act.wait_ge(s["gemm_done"], 4 * i + 2 * k + n)
                act.wait_ge(s["pad_free"], 2 * i + k + 1)
                ps = bank[k % 2][:, 0:n * T]
                act.activation(zpad[:, k % 2, 0:n, 1:T + 1], ps.rearrange("p (a t) -> p a t", a=n), ACT.Copy)
                for j in range(n):
                    ct = 4 * i + 2 * k + j
                    last = act.activation(zs[:, ds(ct, 1), :].rearrange("p a t -> p (a t)"), ps[:, j * T:(j + 1) * T],
                                          ACT.Copy, scale=small[:, ds(ct + 64, 1)])
                last.then_inc(s["bank_free"], 1)

            stream(act, 0, RW_T, hi, to_zs)

            act.wait_ge(s["pad_free"], 2 + RW_PAIRS)
            act.activation(z_wd, z_wd, ACT.Tanh).then_inc(s["kk_raw"], 1)
            act.activation(z_gd, z_gd, ACT.Sigmoid)
            for t in range(RW_CT):
                act.activation(kkn[:, t], zk[:, t], ACT.Copy, scale=small[:, 48 + t:49 + t]).then_inc(s["kk_raw"], 1)
            act.wait_ge(s["kk_raw"], 1 + RW_CT)
            act.activation(kk_sq, kkn, ACT.Square).then_inc(s["kk_sqd"], 1)
            for n, (dst, bias_name) in enumerate(((sig_w, "w0"), (rate, "a0"))):
                for d in range(2):
                    for t in range(RW_CT):
                        f = (n * 2 + d) * (RW_CT // 2) + t // 2
                        if t % 2 == 0:
                            act.wait_ge(s["lora_done"], f + 1)
                        last = act.activation(dst[:, d, t], bank[2 + f % 6][:, (t % 2) * T:(t % 2 + 1) * T], ACT.Sigmoid,
                                              bias=vect(bias_name)[:, d * RW_CT + t:d * RW_CT + t + 1])
                        if t % 2:
                            last.then_inc(s["lora_free"], 1)
            act.wait_ge(s["lora_free"], 2 * RW_CT)
            act.sem_inc(s["gates_ready"], 2)
            for n in range(3):
                act.wait_ge(s["kk_summed"], n + 1)
                act.activation(kk_ss[:, 2 * n:2 * n + 2].rearrange("p a t -> p (a t)"), bank[2 + n], ACT.Sqrt).then_inc(
                    s["kk_root"], 1)

            act.wait_ge(s["kk_ready"], 1)
            with act.Fori(0, RW_CT) as i:
                stand(act, "z_ready", i, "act_passed")
                for d in range(2):
                    act.activation(kd[:, d], rate[:, d, ds(i, 1), :].rearrange("p a t -> p (a t)"), ACT.Identity,
                                   bias=small[:, ds(i + 32, 1)], scale=vect("ka")[:, ds(i, 1)]).then_inc(
                        s["kd_scaled"], 1)
                for d in range(2):
                    act.wait_ge(s["cum_ready"], 5 * i + 3 * d + 2)
                    if d == 1:
                        act.wait_ge(s["tilde_ready"], 2 * i + 1)
                    act.activation(e_inc, cs, ACT.Exp, scale=-DECAY).then_inc(s["exp_ready"], 1)
                    act.activation(e_exc, ce, ACT.Exp, scale=-DECAY).then_inc(s["exp_ready"], 1)
                    act.activation(e_inv, cs, ACT.Exp, scale=DECAY).then_inc(s["exp_ready"], 1)
                act.wait_ge(s["bkt_done"], i + 1)
                for e in range(2):
                    act.activation(bkt[:, e], bank[6 + e].rearrange("p (n k) -> p n k", k=C), ACT.Copy).then_inc(
                        s["bkt_ready"], 1)
                act.wait_ge(s["x_clear"], i + 1)
                t_ps = psum[:, 6:8].rearrange("p b (n t) -> p (b n) t", t=P)
                for n in range(len(LEVELS)):
                    act.wait_ge(s["t_done"], 5 * i + n + 1)
                    for e in range(2):
                        h = slice(e * C, e * C + C)
                        act.activation(xbd[h, :, h], t_ps[h, :, h], ACT.Copy).then_inc(s["x_ready"], 1)
                for n in range(NC):
                    gy = [bank[n % 2 + 4 * e][:, 0:2 * C].rearrange("p (d v) -> p d v", d=2) for e in range(2)]
                    both = slice(n, 2 * NC - n, 2 * NC - 1 - 2 * n)
                    act.wait_ge(s["gy_done"], 4 * i + n + 1)
                    act.activation(gs[0:C], gy[0][0:C], ACT.Copy).then_inc(s["g_low"], 1)
                    act.wait_ge(s["u_done"], 4 * i + n + 1)
                    act.activation(uv[0:C, both, 0], bank[2][0:C, 0:2 * C].rearrange("p (d v) -> p d v", d=2),
                                   ACT.Copy).then_inc(s["u_low"], 1)
                    if n < 2:
                        act.wait_ge(s["y_done"], 4 * i + n + 1)
                        y_i = chunks(tile_of(zk, i))
                        order = slice(n, NC - n, NC - 1 - 2 * n)
                        act.activation(y_i[0:C, order], gy[1][0:C], ACT.Copy)
                        act.activation(y_i[C:P, order], gy[0][C:P], ACT.Copy).then_inc(s["y_copied"], 1)
            act.wait_ge(s["ln_ms"], 1)
            rstd = small[:, 128:128 + RW_CT * NC]
            act.activation(rstd, rstd, ACT.Sqrt).then_inc(s["ln_root"], 1)
            for n in range(3):
                act.wait_ge(s["gate_done"], n + 1)
                act.activation(gate[:, 2 * n:2 * n + 2].rearrange("p a t -> p (a t)"), bank[2 + n], ACT.Copy).then_inc(
                    s["gate_ready"], 1)
            act.wait_ge(s["y_rw_ready"], 1)

            def to_znr(k, i):
                act.wait_ge(s["gemm_done"], 4 * i + (RW_T + 2 * k + 2))
                act.activation(znr[:, ds(4 * i + 2 * k, 2), :].rearrange("p a t -> p (a t)"), bank[(k + RW_PAIRS) % 2],
                               ACT.Copy).then_inc(s["bank_free"], 1)

            stream(act, RW_T, NA_T + RET_T, hi, to_znr)

            for t in range(RW_CT):
                act.activation(act_hi[:, NA_T // 3 + t], y_rw[:, t], ACT.Copy).then_inc(s["y_rw_hi"], 1)
            act.wait_ge(s["bank_free"], RW_PAIRS + NR_PAIRS)
            act.activation(silu_s, znr[:, NA_T + 3 * RET_CT:NA_T + 4 * RET_CT], ACT.Sigmoid).then_inc(s["silu_sig"], 1)
            for t in range(TT):
                act.wait_ge(s["vna_done"], t + 1)
                act.activation(v_na[:, t], bank[2 + t], ACT.Copy).then_inc(s["vna_ready"], 1)
            with act.Fori(0, NA_T // 3) as i:
                act.wait_ge(s["mx_ready"], i + 1)
                for e in range(2):
                    for t in range(TT):
                        n = 2 * e + t
                        act.activation(sx[:, e, t], scores[:, e, t], ACT.Exp, bias=small[:, 160 + n:161 + n],
                                       accum_out=small[:, 164 + n:165 + n]).then_inc(s["p_ready"], 1)
                act.wait_ge(s["rinv_ready"], i + 1)
                act.wait_ge(s["o_done"], i + 1)
                for e in range(2):
                    for t in range(TT):
                        n = 2 * e + t
                        act.activation(yq[:, t, e * C:(e + 1) * C], bank[6][:, (2 * t + e) * C:(2 * t + e + 1) * C],
                                       ACT.Copy, scale=small[:, 168 + n:169 + n]).then_inc(s["yq_ready"], 1)
                act.wait_ge(s["yqt_done"], i + 1)
                act.activation(tile_of(act_hi, i), bank[7][:, 0:T], ACT.Copy).then_inc(s["y_na_hi"], 1)
            act.wait_ge(s["silu_ready"], 1)
            with act.Fori(0, RET_CT) as i:
                act.wait_ge(s["vt_done"], i + 1)
                act.wait_ge(s["ro_done"], i)
                act.activation(v_tok, bank[4][:, 0:T].rearrange("p (t v) -> p t v", t=TT), ACT.Copy).then_inc(
                    s["v_tok_ready"], 1)
                act.wait_ge(s["ro_done"], i + 1)
                act.wait_ge(s["ro_ready"], 3 * i)
                act.activation(o_all[:, ds(i, 1)].rearrange("p a t v -> p (a t v)"), bank[5][:, 0:T], ACT.Copy).then_inc(
                    s["ro_ready"], 1)
                for t in range(TT):
                    act.activation(junk[:, t], bank[5][:, t * P:(t + 1) * P], ACT.Square,
                                   accum_out=small[:, ds(2 * i + (176 + t), 1)]).then_inc(s["ro_ready"], 1)
            ss = small[:, 176:176 + RET_CT * TT]
            act.wait_ge(s["ret_ms"], 1)
            act.activation(ss, ss, ACT.Sqrt).then_inc(s["ret_root"], 1)
            for h in range(RET_CT):
                act.wait_ge(s["yf_ready"], h + 1)
                act.activation(act_hi[:, (NA_W + RW_W) // P + h], y_f[:, h % 2], ACT.Copy).then_inc(s["y_ret_hi"], 1)

            stream(act, OUT_FIRST, KT, hi)

            def out_sums(k):
                act.wait_ge(s["gemm_done"], k)
                for t in range(TT):
                    act.activation(y_sb[:, t], psum[:, 4 * t:4 * t + 4].rearrange("p b n -> p (b n)"), ACT.Square,
                                   accum_out=small[:, 192 + t:193 + t]).then_inc(s["yss_done"], 1)

            out_sums(UP_FIRST)
            act.wait_ge(s["yms_done"], 1)
            act.activation(small[:, 192:194], small[:, 192:194], ACT.Sqrt).then_inc(s["yroot_done"], 1)
            norm_sums(x1, y_sb, small[:, 208:210], "hss_done", lambda t: (s["x1_ready"], t + 1))
            act.wait_ge(s["yms_done"], 2)
            act.activation(small[:, 208:210], small[:, 208:210], ACT.Sqrt).then_inc(s["yroot_done"], 1)
            split_h(("g2", KT))

            def to_relu(k, i):
                act.wait_ge(s["gemm_done"], 4 * i + (UP_FIRST + 2 * k + 2))
                act.wait_ge(s["relu_free"], 2 * i + k + 1)
                act.activation(relu_t[:, k % 2], bank[(k + RW_PAIRS + NR_PAIRS) % 2], ACT.Relu).then_inc(
                    s["bank_free"], 1)

            stream(act, UP_FIRST, FF_T, hi, to_relu)
            act.wait_ge(s["relu_free"], 2 + UP_PAIRS)

            def hi_down(c, i):
                hi(c, i)
                act.activation(u_hi[:, c % 2], u[:, ds(4 * i + (c - DOWN_FIRST), 1), :].rearrange("p a t -> p (a t)"),
                               ACT.Copy).then_inc(s["uhi_done"], 1)

            stream(act, DOWN_FIRST, FF_T, hi_down)
            out_sums(DOWN_FIRST + FF_T)
            act.wait_ge(s["yms_done"], 3)
            act.activation(small[:, 192:194], small[:, 192:194], ACT.Sqrt).then_inc(s["yroot_done"], 1)

        @block.tensor
        def _(pe):
            def turned(src, first):
                for k in range(KT):
                    if k >= 6:
                        pe.wait_ge(s["h_lo"], first + k - 5)
                    for t in range(TT):
                        if k == 0:
                            pe.wait_ge(s["xn_ready"], TT * (first // KT) + t + 1)
                        last = pe.transpose(bank[2 + k % 6][:, t * P:(t + 1) * P], src[:, t, k * P:(k + 1) * P], ident)
                    last.then_inc(s["xt_done"], 1)

            pe.wait_ge(s["consts_in"], 16)
            pe.wait_ge(s["vec_in"], 16 * len(VEC))
            pe.transpose(bank[1][:, 0:VEC_N], vstage[0:VEC_N, :], ident[0:VEC_N, 0:VEC_N]).then_inc(s["vec_t"], 1)
            turned(x_n, 0)
            pe.wait_ge(s["h_lo"], KT)
            pe.wait_ge(s["vec_ready"], 1)

            def split_ready(c, i):
                pe.wait_ge(s["hi_done"], 4 * i + c + 1)
                pe.wait_ge(s["lo_done"], 4 * i + c + 1)

            def columns(c, i, k, pairs, wait=True):
                split_ready(c, i)
                q = pairs + k // 2
                if k % 2 == 0 and wait:
                    pe.wait_ge(s["bank_free"], 2 * i + q - 1)
                dst = bank[q % 2][:, (k % 2) * T:(k % 2 + 1) * T]
                for kt in range(KT):
                    wh = w_hi[:, c % 2, kt * P:(kt + 1) * P]
                    pe.matmul(dst, wh, act_hi[:, kt], start=kt == 0, stop=False)
                    pe.matmul(dst, wh, act_lo[:, kt], start=False, stop=False)
                    last = pe.matmul(dst, w_lo[:, c % 2, kt * P:(kt + 1) * P], act_hi[:, kt], start=False,
                                     stop=kt == KT - 1)
                last.then_inc(s["gemm_done"], 1)

            for k in range(4):
                columns(k, 0, k, 0, wait=False)
            with pe.Fori(0, (RW_T - 5) // 4) as i:
                for k in range(4):
                    columns(4 + k, i, 4 + k, 0)
            columns(RW_T - 1, 0, RW_T - 1, 0)

            pe.wait_ge(s["kk_raw"], 1)
            pe.wait_ge(s["lora_in"], 32)
            for n, (w_s, z_s) in enumerate(((w2s, z_wd), (a2s, z_ad))):
                for d in range(2):
                    for t in range(RW_CT):
                        f = (n * 2 + d) * (RW_CT // 2) + t // 2
                        if t % 2 == 0 and f >= 6:
                            pe.wait_ge(s["lora_free"], f - 5)
                        h = slice(d * C, (d + 1) * C)
                        last = pe.matmul(bank[2 + f % 6][:, (t % 2) * T:(t % 2 + 1) * T], w_s[h, t * P:(t + 1) * P],
                                         z_s[h, :], start=True, stop=True)
                        if t % 2:
                            last.then_inc(s["lora_done"], 1)
            pe.wait_ge(s["kk_sqd"], 1)
            for n in range(3):
                pe.wait_ge(s["lora_free"], 7 + n)
                pe.matmul(bank[2 + n], ones, kk_sq[:, 2 * n:2 * n + 2].rearrange("p a t -> p (a t)"), start=True,
                          stop=True).then_inc(s["kk_summed"], 1)
            pe.wait_ge(s["kk_root"], 3)
            pe.wait_ge(s["bank_free"], RW_PAIRS)

            with pe.Fori(0, RW_CT) as i:
                for d in range(2):
                    pe.wait_ge(s["tilde_ready"], 2 * i + d + 1)
                    for e in range(2):
                        h = slice(e * C, e * C + C)
                        for c in range(NC):
                            last = pe.matmul(bank[2 * d + e][:, c * P:(c + 1) * P], bk[h, d, c, e * C:e * C + P],
                                             ar[h, d, c, e * C:e * C + P], start=True, stop=True)
                    last.then_inc(s["bm_done"], 1)
                    for e in range(2):
                        h = slice(e * C, e * C + C)
                        for c in range(NC):
                            last = pe.transpose(bank[6 + e][:, (d * NC + c) * C:(d * NC + c + 1) * C],
                                                bk[h, d, c, e * C:e * C + P], ident[h, h])
                last.then_inc(s["bkt_done"], 1)
                for d in range(2):
                    for c in range(NC):
                        for e in range(2):
                            h = slice(e * C, e * C + C)
                            last = pe.matmul(bank[4][h, (d * NC + c) * C:(d * NC + c + 1) * C], ar[h, d, c, 0:C],
                                             bk[h, d, c, 0:C], start=True, stop=True)
                last.then_inc(s["a_done"], 1)
                pe.wait_ge(s["v_copied"], i + 1)
                pe.wait_ge(s["bonus_in"], i + 1)
                pe.matmul(bank[5][:, T:2 * T], ones, tmp, start=True, stop=True)
                for c in range(NC):
                    for e in range(2):
                        h, o = slice(e * C, e * C + C), slice((1 - e) * C, (2 - e) * C)
                        last = pe.matmul(bank[5][o, c * C:(c + 1) * C], vst[h, c * C:(c + 1) * C], ident[h, h],
                                         start=True, stop=True)
                last.then_inc(s["vb_done"], 1)
                pe.wait_ge(s["a_ready"], i + 1)
                for n in range(len(LEVELS)):
                    pe.wait_ge(s["zd_ready"], 5 * i + n + 1)
                    for m in range(2 * NC):
                        last = pe.matmul(bank[4][:, m * C:(m + 1) * C], abd[:, m], zd[:, m, 0], start=True, stop=True)
                    last.then_inc(s["p1_done"], 1)
                    if n == 0:
                        pe.wait_ge(s["bkt_ready"], 2 * i + 2)
                    for m in range(2 * NC):
                        last = pe.transpose(bank[6 + m // NC][:, (m % NC) * P:(m % NC + 1) * P],
                                            zd[:, m].rearrange("p a t -> p (a t)"), ident)
                    last.then_inc(s["t_done"], 1)
                    pe.wait_ge(s["p1_ready"], 5 * i + n + 1)
                    pe.wait_ge(s["x_ready"], 10 * i + 2 * n + 2)
                    for m in range(2 * NC):
                        last = pe.matmul(bank[5][:, m * C:(m + 1) * C], xbd[:, m], p1s[:, m], start=True, stop=True)
                    last.then_inc(s["q_done"], 1)
                pe.wait_ge(s["z_ready"], i + 1)
                for n in range(NC):
                    gy = [bank[n % 2 + 4 * e][:, 0:2 * C].rearrange("p (d v) -> p d v", d=2) for e in range(2)]
                    if n == 2:
                        pe.wait_ge(s["y_copied"], 2 * i + 1)
                    if n == 3:
                        pe.wait_ge(s["y_copied"], 2 * i + 2)
                    cd = (n, NC - 1 - n)
                    at = (0, 1) if n < 2 else (1, 0)
                    for d in range(2):
                        for e in range(2):
                            o = slice((1 - e) * C, (2 - e) * C)
                            last = pe.matmul(gy[e][:, at[d]], bms[o, (2 * d + e) * NC + cd[d]], uv[o, d * NC + cd[d], e],
                                             start=d == 0, stop=n == 0, skip_group_check=True)
                    if n:
                        last.then_inc(s["v_part"], 1)
                        pe.wait_ge(s["v_part"], 3 * i + n)
                        pe.wait_ge(s["s_ready"], 3 * i + n)
                        for d in range(2):
                            for e in range(2):
                                h = slice(e * C, e * C + C)
                                last = pe.matmul(gy[e][:, at[d]], ar[h, d, cd[d], e * C:e * C + P], state[h, d],
                                                 start=False, stop=True, skip_group_check=True)
                    last.then_inc(s["gy_done"], 1)
                    pe.wait_ge(s["g_low"], 4 * i + n + 1)
                    pe.wait_ge(s["g_high"], 4 * i + n + 1)
                    for d in range(2):
                        last = pe.matmul(bank[2][:, d * C:(d + 1) * C], abd[:, d * NC + cd[d]], gs[:, at[d]], start=True,
                                         stop=True)
                    last.then_inc(s["u_done"], 1)
                    pe.wait_ge(s["u_low"], 4 * i + n + 1)
                    pe.wait_ge(s["u_high"], 4 * i + n + 1)
                    if n < NC - 1:
                        for d in range(2):
                            for e in range(2):
                                last = pe.matmul(bank[3][e * C:(e + 1) * C, d * C:(d + 1) * C], bkt[:, e, d * NC + cd[d]],
                                                 uv[:, d * NC + cd[d], e], start=True, stop=True)
                        last.then_inc(s["s_done"], 1)
                    for d in range(2):
                        for e in range(2):
                            h = slice(e * C, e * C + C)
                            last = pe.matmul(gy[e][:, at[d]], bms[h, (2 * d + e) * NC + cd[d]], uv[h, d * NC + cd[d], e],
                                             start=False, stop=True, skip_group_check=True)
                    last.then_inc(s["y_done"], 1)

            pe.wait_ge(s["g2_in"], 16)
            for n in range(3):
                for t in range(2 * n, 2 * n + 2):
                    last = pe.matmul(bank[2 + n][:, (t % 2) * T:(t % 2 + 1) * T], g2s[:, t * P:(t + 1) * P], z_gd,
                                     start=True, stop=True)
                last.then_inc(s["gate_done"], 1)
            pe.wait_ge(s["ln_ready"], 1)
            for t in range(RW_CT):
                for c in range(NC):
                    for e in range(2):
                        h, o = slice(e * C, e * C + C), slice((1 - e) * C, (2 - e) * C)
                        at = (t % 2) * T + c * C
                        last = pe.matmul(bank[5 + t // 2][h, at:at + C], zk[o, t, c * C:(c + 1) * C], ident[o, o],
                                         start=True, stop=True)
                if t % 2:
                    last.then_inc(s["yt_done"], 1)

            for k in range(2):
                columns(RW_T + k, 0, k, RW_PAIRS)
            for k in range(2, 4):
                columns(RW_T + k, 0, k, RW_PAIRS)
            with pe.Fori(0, (NA_T + RET_T) // 4 - 1) as i:
                for k in range(4):
                    columns(RW_T + 4 + k, i, k + 4, RW_PAIRS)

            pe.wait_ge(s["bank_free"], RW_PAIRS + NR_PAIRS)
            for t in range(TT):
                for n in range(NA_W // P):
                    last = pe.transpose(bank[2 + t][:, n * P:(n + 1) * P], znr[:, 2 * NA_W // P + n, t * P:(t + 1) * P],
                                        ident)
                last.then_inc(s["vna_done"], 1)
            pe.wait_ge(s["vna_ready"], TT)
            pe.wait_ge(s["bias_ready"], NA_HEADS)
            pe.wait_ge(s["flip_in"], 16)
            with pe.Fori(0, NA_T // 3) as i:
                pe.wait_ge(s["k_copied"], i + 1)
                pe.wait_ge(s["q_ready"], i + 1)
                for e in range(2):
                    h = slice(e * C, e * C + C)
                    pe.matmul(bank[2 + e], flip, bias[:, ds(i * 2 + e, 1), :, :].rearrange("p h t k -> p (h t k)"),
                              start=True, stop=False)
                    for t in range(TT):
                        last = pe.matmul(bank[2 + e][:, t * T:(t + 1) * T], q_s[h, t * P:(t + 1) * P], k_s[h, :],
                                         start=False, stop=t == TT - 1)
                last.then_inc(s["sc_done"], 1)
                pe.wait_ge(s["p_ready"], 4 * i + 4)
                pe.wait_ge(s["pt_ready"], 2 * i)
                for e in range(2):
                    for kt in range(TT):
                        for t in range(TT):
                            last = pe.transpose(bank[4 + e][:, (2 * kt + t) * P:(2 * kt + t + 1) * P],
                                                sx[:, e, t, kt * P:(kt + 1) * P], ident)
                last.then_inc(s["pt_done"], 1)
                pe.wait_ge(s["pt_ready"], 2 * i + 2)
                pe.wait_ge(s["yq_ready"], 4 * i)
                for t in range(TT):
                    for e in range(2):
                        for kt in range(TT):
                            last = pe.matmul(bank[6][:, (2 * t + e) * C:(2 * t + e + 1) * C], pts[:, e, kt, t],
                                             v_na[:, kt, ds(i * P + e * C, C)], start=kt == 0, stop=kt == TT - 1)
                last.then_inc(s["o_done"], 1)
                pe.wait_ge(s["yq_ready"], 4 * i + 4)
                pe.wait_ge(s["y_na_lo"], i)
                for t in range(TT):
                    last = pe.transpose(bank[7][:, t * P:(t + 1) * P], yq[:, t], ident)
                last.then_inc(s["yqt_done"], 1)

            pe.wait_ge(s["y_na_lo"], NA_T // 3)
            with pe.Fori(0, RET_CT) as i:
                pe.wait_ge(s["qk_ready"], 2 * i)
                for n in range(2):
                    last = pe.matmul(bank[2][:, n * T:(n + 1) * T], turn,
                                     znr[:, ds(i + (NA_T + n * RET_CT), 1), :].rearrange("p a t -> p (a t)"),
                                     start=True, stop=True)
                last.then_inc(s["rot_done"], 1)
                pe.wait_ge(s["rot_in"], 3 * i + 3)
                pe.wait_ge(s["v_tok_ready"], i)
                for t in range(TT):
                    last = pe.transpose(bank[4][:, t * P:(t + 1) * P], v_cp[:, t * P:(t + 1) * P], ident)
                last.then_inc(s["vt_done"], 1)
                pe.wait_ge(s["qk_ready"], 2 * i + 2)
                pe.wait_ge(s["st_ready"], i)
                for m in range(TT):
                    last = pe.matmul(bank[3][:, m * T:(m + 1) * T], qk[:, 1, m * P:(m + 1) * P], qk[:, 0], start=True,
                                     stop=True)
                last.then_inc(s["st_done"], 1)
                pe.wait_ge(s["st_ready"], i + 1)
                pe.wait_ge(s["v_tok_ready"], i + 1)
                pe.wait_ge(s["ro_ready"], 3 * i)
                for t in range(TT):
                    for m in range(TT):
                        last = pe.matmul(bank[5][:, t * P:(t + 1) * P], sts[:, m, t * P:(t + 1) * P], v_tok[:, m],
                                         start=m == 0, stop=m == TT - 1)
                last.then_inc(s["ro_done"], 1)
            pe.wait_ge(s["on_ready"], 1)
            for h in range(RET_CT):
                for t in range(TT):
                    last = pe.transpose(bank[2 + h][:, t * P:(t + 1) * P], o_all[:, h, t], ident)
                last.then_inc(s["ont_done"], 1)

            def rows(c, i, lhs_hi, lhs_lo, first=False, final=False):
                split_ready(c, i)
                for t in range(TT):
                    h = slice(t * P, (t + 1) * P)
                    for lhs, w, a, z in ((lhs_hi, w_hi, first, False), (lhs_hi, w_lo, False, False),
                                         (lhs_lo, w_hi, False, final)):
                        for b in range(4):
                            last = pe.matmul(bank[4 * t + b], lhs[:, h], w[:, c % 2, b * 512:(b + 1) * 512],
                                             start=a, stop=z)
                last.then_inc(s["gemm_done"], 1)

            pe.wait_ge(s["y_lo"], RW_CT + RET_CT)
            for n in range(KT):
                rows(OUT_FIRST + n, 0, act_hi[:, n], act_lo[:, n], n == 0, n == KT - 1)

            turned(y_sb, KT)
            pe.wait_ge(s["h_lo"], 2 * KT)
            with pe.Fori(0, FF_T // 4) as i:
                for k in range(4):
                    columns(UP_FIRST + k, i, k, RW_PAIRS + NR_PAIRS)

            pe.wait_ge(s["bank_free"], RW_PAIRS + NR_PAIRS + UP_PAIRS)

            def down(c, i, **ends):
                m = c - DOWN_FIRST
                pe.wait_ge(s["uhi_done"], 4 * i + m + 1)
                pe.wait_ge(s["ulo_done"], 4 * i + m + 1)
                rows(c, i, u_hi[:, c % 2], u_lo[:, c % 2], **ends)

            down(DOWN_FIRST, 0, first=True)
            with pe.Fori(0, (FF_T - 1) // 4) as i:
                for k in range(4):
                    down(DOWN_FIRST + 1 + k, i)
            for n in range(FF_T - 3, FF_T):
                down(DOWN_FIRST + n, 0, final=n == FF_T - 1)


_INS = ("x", "pre_mix_g", "w_in", "na_rpb", "rw_mu_prev", "rw_mu_next", "rw_w0", "rw_w2", "rw_a0", "rw_a2", "rw_k_k",
        "rw_k_a", "rw_r_k", "rw_g2", "rw_lnx_g", "rw_lnx_b", "w_out", "post_mix_g", "pre_mlp_g", "w_up", "w_down",
        "post_mlp_g")


def kernel(**inputs):
    import concourse.bacc as bacc
    from concourse.bass_utils import run_bass_kernel_spmd

    nc = bacc.Bacc("TRN2", target_bir_lowering=False, num_devices=1)
    tables, decays = constants()
    arrays = {f"in_{n}": np.ascontiguousarray(inputs[n]) for n in _INS}
    arrays["in_tables"], arrays["in_decays"] = tables, decays
    args = [nc.dram_tensor(n, a.shape, mybir.dt.from_np(a.dtype), kind="ExternalInput").ap() for n, a in arrays.items()]
    args.append(nc.dram_tensor("out_x", (1, T, D), F32, kind="ExternalOutput").ap())
    layer(nc, *args)
    r = run_bass_kernel_spmd(nc, [arrays], core_ids=[0])
    return r.results[0]["out_x"]
```

```python
from contextlib import ExitStack
import math

import numpy as np

import concourse.bass as bass
from concourse import mybir

ALU = mybir.AluOpType
ACT = mybir.ActivationFunctionType
F32 = mybir.dt.float32
F32R = mybir.dt.float32r
AX_X = mybir.AxisListType.X
ds = bass.ds

P = 128
T = 256
TT = T // P
D = 2048
KT = D // P
NA_W, RW_W, RET_W = D // 4, 3 * D // 8, 3 * D // 8
NA_HEADS, NA_HD = NA_W // 64, 64
GRID_W, ROWS, WIN = 64, T // 64, 16
NA_T, RW_CT, RET_CT = 3 * NA_W // P, RW_W // P, RET_W // P
RW_T = 3 * RW_CT + 3
RET_T = 4 * RET_CT
W_IN_T = NA_T + RW_T + RET_T
FF = 4 * D
FF_T = FF // P
C = 64
NC = T // C
LEVELS = [2, 4, 8, 16, 32]
EPS, LNX_EPS = 1e-6, 64e-5
DECAY = math.exp(-0.5)

UNIT = 2048
RAW = 4
OUT_FIRST = W_IN_T
UP_FIRST = OUT_FIRST + KT
DOWN_FIRST = UP_FIRST + FF_T

VEC = {}
_at = 0
for _n, _w in (("g1", KT), ("g2", KT), ("mup", RW_T), ("mun", RW_T), ("w0", 2 * RW_CT), ("a0", 2 * RW_CT),
               ("kk", RW_CT), ("ka", RW_CT), ("rk", RW_CT), ("lg", RW_CT), ("lb", RW_CT)):
    VEC[_n] = (_at, _at + _w)
    _at += _w
VEC_N = _at
CST = {}
_at = 0
for _n, _w in (("ident", P), ("ones", P), ("turn", P), ("cos", T), ("sin", T), ("bm", 4 * P), ("lower", 2 * C),
               ("off", (len(LEVELS) + 1) * C), ("eye", C), ("keep", T), ("win", GRID_W)):
    CST[_n] = (_at, _at + _w)
    _at += _w
CST_N = _at


def constants():
    c = np.zeros((P, CST_N), np.float32)

    def put(name, a):
        c[:, CST[name][0]:CST[name][1]] = a.reshape(P, -1)

    put("ident", np.eye(P, dtype=np.float32))
    half = np.arange(P) // C
    put("ones", (half[:, None] == half[None]).astype(np.float32))
    turn = np.zeros((P, P), np.float32)
    for j in range(0, P, 2):
        turn[j + 1, j], turn[j, j + 1] = -1.0, 1.0
    put("turn", turn)
    theta = np.float32(1.0) / np.float32(10000.0) ** np.linspace(0.0, 1.0, P // 2, dtype=np.float32)
    ang = np.arange(T, dtype=np.float32)[:, None] * theta[None].astype(np.float32)
    put("cos", np.repeat(np.cos(ang).T, 2, axis=0))
    put("sin", np.repeat(np.sin(ang).T, 2, axis=0))
    j, t = np.arange(C)[:, None], np.arange(C)[None]
    strict = [(j < t), (j > t)]
    incl = [(j <= t), (j >= t)]
    bm = np.zeros((P, 2, 2, P), np.float32)
    for d in range(2):
        a_r = np.concatenate([strict[d], incl[d]], 1)
        bm[:, d, 0] = np.concatenate([a_r, a_r], 0)
        r_a = np.concatenate([incl[d], strict[d]], 1)
        bm[:, d, 1] = np.concatenate([r_a, r_a], 0)
    put("bm", bm)
    low = np.stack([strict[d].T for d in range(2)], 1).astype(np.float32)
    put("lower", np.concatenate([low, low], 0))
    off = np.stack([(j // (2 * m) == t // (2 * m)) & (j // m != t // m) for m in [1] + LEVELS], 1)
    put("off", np.concatenate([off, off], 0).astype(np.float32))
    put("eye", np.concatenate([np.eye(C), np.eye(C)], 0).astype(np.float32))
    keep = np.ones((P, T), np.float32)
    keep[:, 0::C] = 0.0
    put("keep", keep)
    col = np.arange(GRID_W)
    start = np.clip(col - WIN // 2, 0, GRID_W - WIN)
    seen = (col[None] >= start[:, None]) & (col[None] < start[:, None] + WIN)
    win = np.where(seen, 0.0, -1e30).astype(np.float32)
    put("win", np.concatenate([win[::-1], win[::-1]], 0))
    lg = np.log(1.0 - 2.0 ** (-5.0 - np.arange(RET_CT)))
    dist = np.abs(np.arange(3 * P)[None] - P - np.arange(P)[:, None])
    decay = np.exp(dist[:, None, :] * lg[None, :, None]) * P ** -0.5
    flip = np.zeros((P, P), np.float32)
    for p in range(P):
        flip[p, p // GRID_W * GRID_W + GRID_W - 1 - p % GRID_W] = 1.0
    return c, np.concatenate([decay.astype(np.float32).reshape(P, -1), flip], 1)


def layer(nc, x, pre_mix_g, w_in, na_rpb, rw_mu_prev, rw_mu_next, rw_w0, rw_w2, rw_a0, rw_a2, rw_k_k, rw_k_a,
          rw_r_k, rw_g2, rw_lnx_g, rw_lnx_b, w_out, post_mix_g, pre_mlp_g, w_up, w_down, post_mlp_g,
          cst_d, decay_d, out):
    with ExitStack() as ctx:
        def sb(name, shape, dt=F32):
            return ctx.enter_context(nc.sbuf_tensor(name, shape, dt))

        def sem(name):
            return ctx.enter_context(nc.semaphore(name))

        raw = sb("raw", [P, RAW, UNIT])
        w_hi = sb("w_hi", [P, 2, UNIT], F32R)
        w_lo = sb("w_lo", [P, 2, UNIT], F32R)
        act_hi = sb("act_hi", [P, KT, T], F32R)
        act_lo = sb("act_lo", [P, KT, T], F32R)
        u_hi = sb("u_hi", [P, 2, T], F32R)
        u_lo = sb("u_lo", [P, 2, T], F32R)
        cst = sb("cst", [P, CST_N])
        vec = sb("vec", [P, VEC_N])
        small = sb("small", [P, 256])
        ARENA = 24640
        arena = sb("arena", [P, ARENA])
        psum = ctx.enter_context(nc.psum_tensor("psum", [P, 8, 512], F32))
        bank = [psum[:, b] for b in range(8)]
        scores = psum[:, 2:4].rearrange("p e (t k) -> p e t k", t=TT)

        def const(name):
            return cst[:, CST[name][0]:CST[name][1]]

        def vect(name):
            return vec[:, VEC[name][0]:VEC[name][1]]

        ident, ones, turn = const("ident"), const("ones"), const("turn")
        bm_mask = const("bm").rearrange("p (d e t) -> p d e t", d=2, e=2)
        lower = const("lower").rearrange("p (d j) -> p d j", d=2)
        off = const("off").rearrange("p (m t) -> p m t", t=C)
        eye = const("eye")
        keep = const("keep")

        def cut(at, *shape):
            n = int(np.prod(shape))
            assert at + n <= ARENA, (at, n)
            v = arena[:, at:at + n]
            names = "abcd"[:len(shape)]
            if len(shape) == 1:
                return v
            return v.rearrange(f"p ({' '.join(names)}) -> p {' '.join(names)}",
                               **{k: s for k, s in zip(names[1:], shape[1:])})

        zs = cut(0, RW_T, T)
        zr, zk, zv = zs[:, 0:RW_CT], zs[:, RW_CT:2 * RW_CT], zs[:, 2 * RW_CT:3 * RW_CT]
        z_wd, z_ad, z_gd = (zs[:, 3 * RW_CT + n] for n in range(3))
        a0_ = RW_T * T
        sig_w = cut(a0_, 2, RW_CT, T)
        rate = cut(a0_ + 3072, 2, RW_CT, T)
        kkn = cut(a0_ + 6144, RW_CT, T)
        L = a0_ + 7680
        x_in = cut(L, TT, D)
        x_n = cut(L + 4096, TT, D)
        zpad = cut(L + 8192, 2, 2, T + 2)
        vstage = cut(L + 9300, P)
        w2s = cut(L, RW_W)
        a2s = cut(L + RW_W, RW_W)
        kk_ss = cut(L + 2 * RW_W, RW_CT, T)
        kk_sq = cut(L + 4 * RW_W, RW_CT, T)
        cs = cut(L, T)
        ce = cut(L + 256, T)
        e_inc = cut(L + 512, T)
        e_exc = cut(L + 768, T)
        e_inv = cut(L + 1024, T)
        kd = cut(L + 1280, 2, T)
        bn = cut(L + 1792, T)
        tmp = cut(L + 2048, T)
        zd = cut(L, 2 * NC, C)
        zt = cut(L + 1024, 2 * NC, C)
        p1s = cut(L + 1536, 2 * NC, C)
        bk = cut(L + 2304, 2, NC, 3 * C)
        gs = cut(L + 3840, 2, C)
        state = cut(L + 3968, 2, C)
        state_dec = cut(L + 4096, 2, C)
        vst = cut(L + 4224, T)
        ar, bms, az, bkt, uv, ec = [], [], [], [], [], []
        for q, (mem, at) in enumerate(((arena, L + 4480), (raw[:].rearrange("p r n -> p (r n)"), 0))):
            ar.append(mem[:, at:at + 1536].rearrange("p (d c n) -> p d c n", d=2, c=NC))
            bms.append(mem[:, at + 1536:at + 3584].rearrange("p (n t) -> p n t", t=P))
            az.append(mem[:, at + 3584:at + 4096].rearrange("p (n t) -> p n t", t=C))
            bkt.append(mem[:, at + 4096:at + 5120].rearrange("p (e n k) -> p e n k", e=2, k=C))
            uv.append(mem[:, at + 5120:at + 6144].rearrange("p (n e v) -> p n e v", e=2, v=C))
            ec.append(small[:, 16 + 8 * q:24 + 8 * q].rearrange("p (d c) -> p d c", d=2))
        gate = cut(a0_, RW_CT, T)
        g2s = cut(a0_ + 3072, RW_W)
        ysq = cut(L, RW_CT * NC, C)
        y_rw = cut(a0_ + 6144, RW_CT, T)
        znr = cut(0, NA_T + RET_T, T)
        o_all = cut(9216, RET_CT, TT, P)
        v_cp = cut(10752, T)
        v_tok = cut(11008, TT, P)
        bias = cut(L, NA_HEADS, TT, T)
        decay = cut(L + 4096, RET_CT, 3 * P)
        W_ = L + 6400
        v_na = cut(W_, TT, NA_W)
        q_s = cut(W_ + 1024, T)
        k_s = cut(W_ + 1280, T)
        sx = cut(W_ + 1536, 2, TT, T)
        pts = cut(W_ + 2560, 2, TT, TT, P)
        yq = cut(W_ + 3584, TT, P)
        flip = cut(W_ + 3840, P)
        silu_s = cut(9216, RET_CT, T)
        qk = cut(W_, 2, T)
        qk_cos = cut(W_ + 512, 2, T)
        sts = cut(W_ + 1024, TT, T)
        y_f = cut(W_ + 1536, 2, T)
        junk = cut(W_ + 2048, TT, P)
        u = cut(0, FF_T, T)
        x1 = cut(16384, TT, D)
        gains = cut(20480, D)
        relu_t = cut(22528, 2, 512)
        o_sb = cut(0, TT, D)
        y_sb = cut(0, TT, D)

        s = {n: sem(n) for n in (
            "x_in", "consts_in", "vec_in", "lora_in", "g2_in", "bias_in", "flip_in", "decay_in", "gain_in", "x_again", "out_written",
            "ss_done", "ms_done", "sq_done", "rs_done", "xn_ready", "xt_done", "h_hi", "h_lo",
            "vec_t", "vec_ready", "coef_ready",
            "hi_done", "lo_done", "gemm_done", "bank_free", "pad_free", "zs_ready",
            "gates_ready", "lora_done", "lora_free", "kk_raw", "kk_sqd", "kk_summed", "kk_root", "kk_ready",
            "cum_ready", "exp_ready", "kb_ready", "bonus_in", "kd_scaled", "kd_summed", "pool_passed", "act_passed", "v_copied", "tilde_ready", "bm_done", "a_done",
            "bkt_done", "vb_done", "bm_ready", "a_ready", "bkt_ready", "vb_ready", "zd_ready", "t_done", "zt_ready", "p0_ready", "pe_passed", 
            "p1_done", "v_part", "p1_ready", "q_done", "z_ready", "gy_done", "g_low", "g_high", "u_done", "u_low", "u_high",
            "s_done", "s_ready", "dec_ready", "y_done", "y_copied", "y_added", 
            "ln_ms", "ln_root", "ln_ready", "gate_done", "gate_ready", "yt_done", "y_rw_ready",
            "bias_ready", "vna_done", "vna_ready", "k_copied", "q_ready", "sc_done", "mx_ready", "p_ready", "rinv_ready",
            "pt_done", "pt_ready", "o_done", "yq_ready", "yqt_done", "y_na_hi", "y_na_lo",
            "silu_sig", "silu_ready", "rot_in", "rot_done", "qk_ready", "vt_done", "v_tok_ready", "st_done", "st_ready",
            "ro_done", "ro_ready", "ret_ms", "ret_root", "ret_rs", "on_ready", "ont_done", "yf_ready", "y_ret_hi",
            "y_rw_hi", "y_lo", "out_acc", "yss_done", "yms_done", "yroot_done", "yrs_done", "x1_ready", "hss_done",
            "relu_free", "uhi_done", "ulo_done", "down_done", "o_ready",
            "act_step", "dve_step", "pool_step")}
        raw_in = [sem(f"raw_in{r}") for r in range(RAW)]
        block = ctx.enter_context(nc.Block())

        def stream(eng, first, count, convert, drain=None):
            quads = count // 4
            convert(first, 0)
            convert(first + 1, 0)
            with eng.Fori(0, quads - 1) as i:
                for pair in range(2):
                    convert(first + 2 * pair + 2, i)
                    convert(first + 2 * pair + 3, i)
                    if drain:
                        drain(pair, i)
            rest = [first + n for n in range(4 * quads - 2, count)]
            pairs = list(range(2 * quads - 2, (count + 1) // 2))
            while rest or pairs:
                for n in rest[:2]:
                    convert(n, 0)
                rest = rest[2:]
                if pairs and drain:
                    drain(pairs[0], 0)
                pairs = pairs[1:]

        def raw_landed(eng, c, i):
            eng.wait_ge(raw_in[c % RAW], 16 * (i + c // RAW + 1))

        def link(eng, counter, name, ins):
            counter[0] += 1
            ins.then_inc(s[name], 1)
            eng.wait_ge(s[name], counter[0])

        def stand(eng, name, value, passed):
            eng.wait_ge(s[name], value)
            eng.sem_inc(s[passed], 1)

        def tile_of(view, i):
            return view[:, ds(i, 1), :].rearrange("p a t -> p (a t)")

        def rw_tiles(eng, prepare, level, chunk):
            def turn(t, p, first=False, last=False):
                pieces = [chunk(t - 1, 1 - p, n) for n in range(NC)] if not first else [None] * NC
                if last:
                    for n in range(NC):
                        for piece in pieces[n]:
                            piece()
                    return
                prepare(t, p, pieces[0], pieces[1])
                for n in range(len(LEVELS)):
                    level(t, p, n, pieces[2 + n] if n < NC - 2 else None)

            turn(0, 0, first=True)
            with eng.Fori(0, (RW_CT - 2) // 2) as i:
                turn(2 * i + 1, 1)
                turn(2 * i + 2, 0)
            turn(RW_CT - 1, 1)
            turn(RW_CT, 0, last=True)

        def chunks(view):
            return view.rearrange("p (c t) -> p c t", t=C)

        RW_PAIRS, NR_PAIRS, UP_PAIRS = (RW_T + 1) // 2, (NA_T + RET_T) // 2, FF_T // 2

        @block.sync
        def _(sp):
            sp.dma_start(x_in, x[0].rearrange("(t p) d -> p t d", p=P)).then_inc(s["x_in"], 16)
            sp.dma_start(cst[:], cst_d).then_inc(s["consts_in"], 16)
            for name, v in (("g1", pre_mix_g), ("g2", pre_mlp_g), ("mup", rw_mu_prev), ("mun", rw_mu_next),
                            ("w0", rw_w0.rearrange("l d c -> l (d c)")), ("a0", rw_a0.rearrange("l d c -> l (d c)")),
                            ("kk", rw_k_k), ("ka", rw_k_a), ("rk", rw_r_k.rearrange("l h c -> l (h c)")),
                            ("lg", rw_lnx_g), ("lb", rw_lnx_b)):
                a, b = VEC[name]
                sp.dma_start(vstage[a:b, :], v.rearrange("l (t p) -> (l t) p", p=P)).then_inc(s["vec_in"], 16)

            def fetch(c, i, src, wait=True):
                if wait:
                    sp.wait_ge(s["lo_done"], 4 * i + c - RAW + 1)
                dst = raw[:, c % RAW, :]
                if len(src.shape) == 3:
                    dst = dst.rearrange("p (k c) -> p k c", k=KT)
                sp.dma_start(dst, src).then_inc(raw_in[c % RAW], 16)

            w_in_v = w_in[0].rearrange("(k p) c -> p k c", p=P)
            w_up_v = w_up[0].rearrange("(k p) c -> p k c", p=P)
            w_out_v = w_out[0].rearrange("(k p) c -> p k c", p=P)
            w_down_v = w_down[0].rearrange("(k p) c -> p k c", p=P)

            def columns(view, tile):
                return view[:, :, ds(tile * P, P)]

            def rows(view, tile):
                return view[:, ds(tile, 1), :].rearrange("p k c -> p (k c)")

            for n in range(RAW):
                fetch(n, 0, columns(w_in_v, NA_T + n), wait=False)
            with sp.Fori(0, (RW_T - 5) // 4) as i:
                for k in range(4):
                    fetch(4 + k, i, columns(w_in_v, i * 4 + (NA_T + 4 + k)))
            fetch(RW_T - 1, 0, columns(w_in_v, NA_T + RW_T - 1))
            sp.wait_ge(s["y_added"], 2 * RW_CT)
            with sp.Fori(0, NA_T // 4) as i:
                for k in range(4):
                    fetch(RW_T + k, i, columns(w_in_v, i * 4 + k))
            sp.wait_ge(s["y_rw_ready"], 1)
            for i in range(ROWS):
                half = GRID_W * (i % 2)
                for r in range(ROWS):
                    src = bass.AP(tensor=na_rpb.tensor, offset=(r - i + 7) * 31 + WIN - 1 - (GRID_W - 1),
                                  ap=[[1, GRID_W], [15 * 31, NA_HEADS], [1, GRID_W]])
                    dst = bias[half:half + GRID_W, :, i // 2, r * GRID_W:(r + 1) * GRID_W]
                    sp.dma_start(dst, src).then_inc(s["bias_in"], 16)
            sp.dma_start(flip, decay_d[:, RET_CT * 3 * P:]).then_inc(s["flip_in"], 16)
            sp.dma_start(decay.rearrange("p h x -> p (h x)"), decay_d[:, 0:RET_CT * 3 * P]).then_inc(s["decay_in"], 16)
            with sp.Fori(0, RET_T // 4) as i:
                for k in range(4):
                    fetch(RW_T + NA_T + k, i, columns(w_in_v, i * 4 + (RW_T + NA_T + k)))
            with sp.Fori(0, KT // 4) as i:
                for k in range(4):
                    fetch(OUT_FIRST + k, i, rows(w_out_v, i * 4 + k))
            sp.wait_ge(s["y_na_lo"], NA_T // 3)
            sp.wait_ge(s["y_lo"], RW_CT + RET_CT)
            sp.dma_start(x1, x[0].rearrange("(t p) d -> p t d", p=P)).then_inc(s["x_again"], 16)
            sp.dma_start(gains, post_mix_g.broadcast_to([P, D])).then_inc(s["gain_in"], 16)
            with sp.Fori(0, FF_T // 4) as i:
                for k in range(4):
                    fetch(UP_FIRST + k, i, columns(w_up_v, i * 4 + k))
            sp.wait_ge(s["x1_ready"], TT)
            sp.dma_start(gains, post_mlp_g.broadcast_to([P, D])).then_inc(s["gain_in"], 16)
            with sp.Fori(0, FF_T // 4) as i:
                for k in range(4):
                    fetch(DOWN_FIRST + k, i, rows(w_down_v, i * 4 + k))
            for t in range(TT):
                sp.wait_ge(s["o_ready"], t + 1)
                sp.dma_start(out[0, t * P:(t + 1) * P, :], o_sb[:, t]).then_inc(s["out_written"], 16)
            sp.wait_ge(s["out_written"], 16 * TT)

        @block.gpsimd
        def _(pool):
            step = [0]

            def nxt(ins):
                link(pool, step, "pool_step", ins)

            for _ in range(2):
                pool.sem_inc(s["relu_free"], 1)
            pool.wait_ge(s["h_lo"], KT)
            pool.dma_start(w2s, rw_w2.rearrange("l d r c -> (l d r) c")).then_inc(s["lora_in"], 16)
            pool.dma_start(a2s, rw_a2.rearrange("l d r c -> (l d r) c")).then_inc(s["lora_in"], 16)

            pool.wait_ge(s["lora_free"], 2 * RW_CT)
            pool.wait_ge(s["kk_ready"], 1)

            def prepare(t, p, first, second):
                k_i = tile_of(zk, t)
                for d in range(2):
                    stand(pool, "kd_scaled", 2 * t + (d + 1), "pool_passed")
                    pool.tensor_tensor(kd[:, d], kd[:, d], k_i, ALU.mult).then_inc(s["pool_step"], 1)
                    if d == 1:
                        stand(pool, "tilde_ready", 2 * t + 1, "pool_passed")
                    pool.tensor_tensor(bn, tile_of(kkn, t), tile_of(rate[:, d], t), ALU.mult).then_inc(s["kb_ready"], 1)
                for piece in second or ():
                    piece()
                pool.wait_ge(s["pool_step"], 2 * t + 2)
                pool.tensor_tensor(tmp, kd[:, 0], kd[:, 1], ALU.add).then_inc(s["kd_summed"], 1)
                stand(pool, "vb_done", t, "pool_passed")
                pool.tensor_copy(vst, tile_of(zv, t)).then_inc(s["v_copied"], 1)

            def level(t, p, n, pieces):
                for piece in pieces or ():
                    piece()

            def chunk(b, q, n):
                def decay_state():
                    stand(pool, "s_ready", 3 * b + n, "pool_passed")
                    for d in range(2):
                        c = n if d == 0 else NC - 1 - n
                        last = pool.tensor_scalar(state_dec[:, d], state[:, d], ec[q][:, d, c:c + 1], None, ALU.mult)
                    last.then_inc(s["dec_ready"], 1)
                return [decay_state] if n in (1, 2) else []

            rw_tiles(pool, prepare, level, chunk)

            pool.wait_ge(s["ln_ms"], 1)
            pool.dma_start(g2s, rw_g2[0]).then_inc(s["g2_in"], 16)

            pool.wait_ge(s["bias_in"], 16 * ROWS * ROWS)
            win = const("win").unsqueeze(1).broadcast_to([P, TT * ROWS, GRID_W])
            for h in range(NA_HEADS):
                b_h = bias[:, h].rearrange("p t (r c) -> p (t r) c", c=GRID_W)
                pool.tensor_tensor(b_h, b_h, win, ALU.add).then_inc(s["bias_ready"], 1)

            pool.wait_ge(s["bank_free"], RW_PAIRS + NR_PAIRS)
            with pool.Fori(0, NA_T // 3) as i:
                stand(pool, "sc_done", i, "pool_passed")
                pool.tensor_copy(k_s, tile_of(znr, i + NA_T // 3)).then_inc(s["k_copied"], 1)
            pool.wait_ge(s["silu_sig"], 1)
            g_all = znr[:, NA_T + 3 * RET_CT:NA_T + 4 * RET_CT]
            pool.tensor_tensor(g_all, g_all, silu_s, ALU.mult).then_inc(s["silu_ready"], 1)
            pool.wait_ge(s["y_na_lo"], NA_T // 3)
            with pool.Fori(0, RET_CT) as i:
                pool.wait_ge(s["qk_ready"], 2 * i)
                for n in range(2):
                    pool.tensor_tensor(qk_cos[:, n], znr[:, ds(i + (NA_T + n * RET_CT), 1), :].rearrange("p a t -> p (a t)"),
                                       const("cos"), ALU.mult).then_inc(s["rot_in"], 1)
                pool.wait_ge(s["vt_done"], i)
                pool.tensor_copy(v_cp, znr[:, ds(i + (NA_T + 2 * RET_CT), 1), :].rearrange("p a t -> p (a t)")).then_inc(
                    s["rot_in"], 1)

            with pool.Fori(0, UP_PAIRS // 2) as i:
                for k in range(2):
                    pool.wait_ge(s["bank_free"], i * 2 + (RW_PAIRS + NR_PAIRS + k + 1))
                    dst = u[:, ds(i * 4 + 2 * k, 2), :].rearrange("p a t -> p (a t)")
                    pool.tensor_tensor(dst, relu_t[:, k], relu_t[:, k], ALU.mult).then_inc(s["relu_free"], 1)

        @block.vector
        def _(dve):
            step = [0]

            def nxt(ins):
                link(dve, step, "dve_step", ins)

            dve.memset(zpad[:, 0], 0.0).then_inc(s["pad_free"], 1)
            dve.memset(zpad[:, 1], 0.0).then_inc(s["pad_free"], 1)
            dve.wait_ge(s["ss_done"], TT)
            dve.tensor_scalar(small[:, 2:4], small[:, 0:2], 1.0 / D, EPS, ALU.mult, ALU.add).then_inc(s["ms_done"], 1)
            dve.wait_ge(s["sq_done"], 1)
            dve.reciprocal(small[:, 6:8], small[:, 4:6]).then_inc(s["rs_done"], 1)
            dve.wait_ge(s["rs_done"], 1)
            for t in range(TT):
                dve.tensor_scalar(x_n[:, t], x_in[:, t], small[:, 6 + t:7 + t], None, ALU.mult).then_inc(s["xn_ready"], 1)
            dve.wait_ge(s["vec_t"], 1)
            dve.tensor_copy(vec[:], bank[1][:, 0:VEC_N]).then_inc(s["vec_ready"], 1)
            dve.wait_ge(s["vec_ready"], 1)
            nxt(dve.tensor_scalar(small[:, 64:64 + RW_T], vect("mup"), -1.0, 1.0, ALU.mult, ALU.add))
            dve.tensor_tensor(small[:, 64:64 + RW_T], small[:, 64:64 + RW_T], vect("mun"), ALU.subtract).then_inc(
                s["coef_ready"], 1)
            dve.tensor_scalar(small[:, 32:32 + RW_CT], vect("ka"), -1.0, 1.0, ALU.mult, ALU.add)
            dve.tensor_scalar(small[:, 48:48 + RW_CT], vect("kk"), -1.0, None, ALU.mult).then_inc(s["coef_ready"], 1)

            def split_h(gain):
                for k in range(KT):
                    dve.wait_ge(s["h_hi"], gain[1] + k + 1)
                    dve.scalar_tensor_tensor(act_lo[:, k], bank[2 + k % 6][:, 0:T], vect(gain[0])[:, k:k + 1],
                                             act_hi[:, k].bitcast(F32), ALU.mult, ALU.subtract).then_inc(s["h_lo"], 1)

            split_h(("g1", 0))

            def lo(c, i):
                dve.wait_ge(s["hi_done"], 4 * i + c + 1)
                if not (isinstance(i, int) and 4 * i + c < 2):
                    dve.wait_ge(s["gemm_done"], 4 * i + c - 1)
                dve.tensor_tensor(w_lo[:, c % 2], raw[:, c % RAW], w_hi[:, c % 2].bitcast(F32),
                                  ALU.subtract).then_inc(s["lo_done"], 1)

            def shift(k, i):
                n = 2 if not (isinstance(i, int) and 2 * i + k == RW_PAIRS - 1) else 1
                dve.wait_ge(s["bank_free"], 2 * i + k + 1)
                for mu, at in (("mup", 0), ("mun", 2)):
                    for j in range(n):
                        ct = 4 * i + 2 * k + j
                        z = zs[:, ds(ct, 1), :].rearrange("p a t -> p (a t)")
                        last = dve.scalar_tensor_tensor(z, zpad[:, k % 2, j, at:at + T], vect(mu)[:, ds(ct, 1)], z,
                                                        ALU.mult, ALU.add)
                        if at == 0:
                            last.then_inc(s["zs_ready"], 1)
                    if at == 0:
                        dve.wait_ge(s["zs_ready"], 2 * (2 * i + k) + n)
                last.then_inc(s["pad_free"], 1)

            stream(dve, 0, RW_T, lo, shift)

            dve.wait_ge(s["kk_root"], 3)
            nxt(dve.tensor_scalar(kk_ss, kk_ss, 1e-12, None, ALU.max))
            nxt(dve.reciprocal(kk_ss, kk_ss))
            dve.tensor_tensor(kkn, kkn, kk_ss, ALU.mult).then_inc(s["kk_ready"], 1)
            dve.wait_ge(s["kk_ready"], 1)
            dve.wait_ge(s["lora_free"], 2 * RW_CT)

            def turn_z(t, n, d):
                dve.wait_ge(s["zd_ready"], 10 * t + (2 * n + d + 1))
                half = slice(d * NC, (d + 1) * NC)
                dve.transpose(zt[:, half].rearrange("p n t -> p (n t)"), zd[:, half].rearrange("p n t -> p (n t)")).then_inc(
                    s["zt_ready"], 1)

            def prepare(t, p, first, second):
                kk_i, r_i, v_i = tile_of(kkn, t), tile_of(zr, t), tile_of(zv, t)
                dve.wait_ge(s["z_ready"], 2 * t)
                for d in range(2):
                    s_i = tile_of(sig_w[:, d], t)
                    if d == 1:
                        dve.wait_ge(s["exp_ready"], 6 * t + 3)
                    dve.tensor_tensor_scan(cs, keep, s_i, 0.0, ALU.mult, ALU.add).then_inc(s["cum_ready"], 1)
                    dve.wait_ge(s["cum_ready"], 5 * t + (2 * d + 1))
                    if d == 0:
                        dve.tensor_tensor(ce, cs, s_i, ALU.subtract).then_inc(s["cum_ready"], 1)
                    else:
                        dve.tensor_tensor(chunks(ce), chunks(cs)[:, :, C - 1:C].broadcast_to([P, NC, C]), chunks(cs),
                                          ALU.subtract).then_inc(s["cum_ready"], 1)
                        dve.wait_ge(s["cum_ready"], 5 * t + 4)
                        dve.tensor_tensor(cs, ce, s_i, ALU.add).then_inc(s["cum_ready"], 1)
                    beside = (first, second)[d]
                    if beside:
                        beside[0]()
                        beside[1]()
                    dve.wait_ge(s["exp_ready"], 6 * t + (3 * d + 3))
                    dve.wait_ge(s["kb_ready"], 2 * t + (d + 1))
                    last_t = C - 1 if d == 0 else 0
                    dve.tensor_copy(ec[p][:, d], chunks(e_inc)[:, :, last_t])
                    a_, k_ = ar[p][:, d], bk[:, d]
                    dve.tensor_tensor(a_[:, :, 0:C], chunks(kk_i), chunks(e_exc), ALU.mult)
                    dve.tensor_tensor(a_[:, :, C:2 * C], chunks(r_i), chunks(e_inc), ALU.mult)
                    dve.tensor_tensor(a_[C:P, :, 2 * C:3 * C], chunks(kk_i)[C:P], chunks(e_exc)[C:P], ALU.mult)
                    dve.scalar_tensor_tensor(k_[:, :, 0:C], chunks(bn), -1.0, chunks(e_inv), ALU.mult, ALU.mult)
                    dve.tensor_tensor(k_[:, :, C:2 * C], chunks(kd[:, d]), chunks(e_inv), ALU.mult)
                    dve.scalar_tensor_tensor(k_[C:P, :, 2 * C:3 * C], chunks(bn)[C:P], -1.0, chunks(e_inv)[C:P],
                                             ALU.mult, ALU.mult).then_inc(s["tilde_ready"], 1)
                    if beside:
                        beside[2]()
                dve.wait_ge(s["kd_summed"], t + 1)
                dve.scalar_tensor_tensor(tmp, tmp, vect("rk")[:, ds(t, 1)], r_i, ALU.mult, ALU.mult).then_inc(
                    s["bonus_in"], 1)
                for d in range(2):
                    dve.wait_ge(s["bm_done"], 2 * t + (d + 1))
                    for e in range(2):
                        dve.tensor_tensor(bms[p][:, (2 * d + e) * NC:(2 * d + e + 1) * NC],
                                          bank[4 + 2 * d + e].rearrange("p (c t) -> p c t", t=P),
                                          bm_mask[:, d, e].unsqueeze(1).broadcast_to([P, NC, P]),
                                          ALU.mult).then_inc(s["bm_ready"], 1)
                dve.wait_ge(s["a_done"], t + 1)
                a_ps = bank[2].rearrange("p (d c j) -> p d c j", d=2, c=NC)
                for e in range(2):
                    h = slice(e * C, e * C + C)
                    for d in range(2):
                        last = dve.tensor_tensor(az[p][h, d * NC:(d + 1) * NC], a_ps[h, d],
                                                 lower[h, d].unsqueeze(1).broadcast_to([C, NC, C]), ALU.mult)
                last.then_inc(s["a_ready"], 1)
                dve.wait_ge(s["bm_ready"], 4 * t + 4)
                for d in range(2):
                    for e in range(2):
                        h = slice(e * C, e * C + C)
                        last = dve.tensor_tensor(p1s[h, d * NC:(d + 1) * NC],
                                                 bms[p][h, (2 * d + e) * NC:(2 * d + e + 1) * NC, h],
                                                 off[h, 0].unsqueeze(1).broadcast_to([C, NC, C]), ALU.mult)
                    last.then_inc(s["p0_ready"], 1)
                for d in range(2):
                    dve.wait_ge(s["p0_ready"], 2 * t + (d + 1))
                    dve.tensor_tensor(zd[:, d * NC:(d + 1) * NC], p1s[:, d * NC:(d + 1) * NC],
                                      eye.unsqueeze(1).broadcast_to([P, NC, C]), ALU.add).then_inc(s["zd_ready"], 1)
                    turn_z(t, 0, d)
                dve.wait_ge(s["vb_done"], t + 1)
                uv_d = uv[p].rearrange("p (d c) e v -> p d c e v", d=2)
                v_ps = bank[2][:, 0:T].rearrange("p (c v) -> p c v", v=C)
                for d in range(2):
                    dve.tensor_copy(uv_d[C:P, d, :, 0, :], v_ps[C:P])
                    dve.tensor_copy(uv_d[0:C, d, :, 1, :], v_ps[0:C]).then_inc(s["vb_ready"], 1)
                dve.tensor_tensor(r_i, bank[2][:, T:2 * T], v_i, ALU.mult).then_inc(s["vb_ready"], 1)

            def level(t, p, n, pieces):
                for d in range(2):
                    half = slice(d * NC, (d + 1) * NC)
                    if pieces:
                        pieces[d]()
                    dve.wait_ge(s["p1_done"], 10 * t + (2 * n + d + 1))
                    dve.tensor_tensor(p1s[:, half], bank[4 + d][:, 0:T].rearrange("p (n t) -> p n t", t=C),
                                      off[:, n + 1].unsqueeze(1).broadcast_to([P, NC, C]),
                                      ALU.mult).then_inc(s["p1_ready"], 1)
                for d in range(2):
                    half = slice(d * NC, (d + 1) * NC)
                    q_ps = bank[4 + d][:, T:2 * T].rearrange("p (n t) -> p n t", t=C)
                    dve.wait_ge(s["q_done"], 10 * t + (2 * n + d + 1))
                    if n < len(LEVELS) - 1:
                        dve.tensor_tensor(zd[:, half], q_ps, zd[:, half], ALU.add).then_inc(s["zd_ready"], 1)
                        turn_z(t, n + 1, d)
                    else:
                        dve.tensor_tensor(az[p][:, half], q_ps, zd[:, half], ALU.add).then_inc(s["z_ready"], 1)
                    if pieces:
                        pieces[2 + d]()

            def chunk(b, q, n):
                gy = [bank[e][:, 0:2 * C].rearrange("p (d v) -> p d v", d=2) for e in range(2)]
                both = slice(n, 2 * NC - n, 2 * NC - 1 - 2 * n)

                def g():
                    dve.wait_ge(s["gy_done"], 4 * b + (n + 1))
                    dve.tensor_copy(gs[C:P], gy[1][C:P]).then_inc(s["g_high"], 1)

                def u():
                    dve.wait_ge(s["u_done"], 4 * b + (n + 1))
                    dve.tensor_copy(uv[q][C:P, both, 1], bank[3][C:P, 0:2 * C].rearrange("p (d v) -> p d v", d=2)).then_inc(
                        s["u_high"], 1)

                def new_state():
                    if n == NC - 1:
                        return
                    dve.wait_ge(s["s_done"], 3 * b + (n + 1))
                    if n:
                        dve.wait_ge(s["dec_ready"], 2 * b + n)
                    for d in range(2):
                        c = n if d == 0 else NC - 1 - n
                        new = bank[3][:, d * C:(d + 1) * C]
                        if n == 0:
                            last = dve.tensor_scalar(state[:, d], new, ec[q][:, d, c:c + 1], None, ALU.mult)
                        else:
                            last = dve.scalar_tensor_tensor(state[:, d], new, ec[q][:, d, c:c + 1], state_dec[:, d],
                                                            ALU.mult, ALU.add)
                    last.then_inc(s["s_ready"], 1)

                def add_y():
                    if n < 2:
                        return
                    dve.wait_ge(s["y_done"], 4 * b + (n + 1))
                    dve.wait_ge(s["y_copied"], 2 * b + 2)
                    y_i = chunks(tile_of(zk, b))
                    order = slice(NC - 1 - n, n + 1, 2 * n - NC + 1)
                    dve.tensor_tensor(y_i[0:C, order], gy[1][0:C], y_i[0:C, order], ALU.add)
                    dve.tensor_tensor(y_i[C:P, order], gy[0][C:P], y_i[C:P, order], ALU.add).then_inc(s["y_added"], 1)

                return g, u, new_state, add_y

            rw_tiles(dve, prepare, level, chunk)

            dve.wait_ge(s["y_added"], 2 * RW_CT)
            y = zk.rearrange("p i (c v) -> p (i c) v", v=C)
            N = RW_CT * NC
            mean, rstd = small[:, 96:96 + N], small[:, 128:128 + N]
            wide = [P, N, C]
            nxt(dve.tensor_reduce(mean, y, AX_X, ALU.add))
            nxt(dve.tensor_scalar(mean, mean, -1.0 / C, None, ALU.mult))
            nxt(dve.tensor_tensor(y, y, mean.unsqueeze(2).broadcast_to(wide), ALU.add))
            nxt(dve.tensor_tensor(ysq, y, y, ALU.mult))
            nxt(dve.tensor_reduce(rstd, ysq, AX_X, ALU.add))
            dve.tensor_scalar(rstd, rstd, 1.0 / C, LNX_EPS, ALU.mult, ALU.add).then_inc(s["ln_ms"], 1)
            dve.wait_ge(s["ln_root"], 1)
            nxt(dve.reciprocal(rstd, rstd))
            dve.tensor_tensor(y, y, rstd.unsqueeze(2).broadcast_to(wide), ALU.mult).then_inc(s["ln_ready"], 1)
            for t in range(RW_CT):
                dve.wait_ge(s["yt_done"], t // 2 + 1)
                nxt(dve.tensor_scalar(y_rw[:, t], bank[5 + t // 2][:, (t % 2) * T:(t % 2 + 1) * T],
                                      vect("lg")[:, t:t + 1], vect("lb")[:, t:t + 1], ALU.mult, ALU.add))
            nxt(dve.tensor_tensor(y_rw, y_rw, zr, ALU.add))
            dve.wait_ge(s["gate_ready"], 3)
            dve.tensor_tensor(y_rw, y_rw, gate, ALU.mult).then_inc(s["y_rw_ready"], 1)

            stream(dve, RW_T, NA_T + RET_T, lo)

            for k in range(RW_CT):
                dve.wait_ge(s["y_rw_hi"], k + 1)
                dve.tensor_tensor(act_lo[:, NA_T // 3 + k], y_rw[:, k], act_hi[:, NA_T // 3 + k].bitcast(F32),
                                  ALU.subtract).then_inc(s["y_lo"], 1)
            base = step[0]
            with dve.Fori(0, NA_T // 3) as i:
                dve.wait_ge(s["sc_done"], i)
                dve.tensor_scalar(q_s, tile_of(znr, i), NA_HD ** -0.5, None, ALU.mult).then_inc(s["q_ready"], 1)
                dve.wait_ge(s["sc_done"], i + 1)
                top = small[:, 160:164]
                dve.tensor_reduce(top.rearrange("p (e t) -> p e t", e=2), scores, AX_X, ALU.max).then_inc(s["dve_step"], 1)
                dve.wait_ge(s["dve_step"], i + (base + 1))
                dve.tensor_scalar(top, top, -1.0, None, ALU.mult).then_inc(s["mx_ready"], 1)
                dve.wait_ge(s["p_ready"], 4 * i + 4)
                dve.reciprocal(small[:, 168:172], small[:, 164:168]).then_inc(s["rinv_ready"], 1)
                for e in range(2):
                    dve.wait_ge(s["pt_done"], 1 * i + 1)
                    dve.tensor_copy(pts[:, e], bank[4 + e].rearrange("p (a b q) -> p a b q", a=2, b=2)).then_inc(
                        s["pt_ready"], 1)
                dve.wait_ge(s["y_na_hi"], i + 1)
                dve.tensor_tensor(tile_of(act_lo, i), bank[7][:, 0:T], tile_of(act_hi, i).bitcast(F32),
                                  ALU.subtract).then_inc(s["y_na_lo"], 1)

            step[0] = base + NA_T // 3

            with dve.Fori(0, RET_CT) as i:
                dve.wait_ge(s["rot_done"], i + 1)
                dve.wait_ge(s["rot_in"], 3 * i + 2)
                dve.wait_ge(s["st_done"], i)
                sin2 = const("sin").unsqueeze(1).broadcast_to([P, 2, T])
                dve.tensor_tensor(qk, bank[2].rearrange("p (a t) -> p a t", a=2), sin2, ALU.mult).then_inc(
                    s["qk_ready"], 1)
                dve.wait_ge(s["qk_ready"], 2 * i + 1)
                dve.tensor_tensor(qk, qk, qk_cos, ALU.add).then_inc(s["qk_ready"], 1)
                dve.wait_ge(s["st_done"], i + 1)
                dve.wait_ge(s["ro_done"], i)
                dec_i = decay[:, ds(i, 1), :].rearrange("p a x -> p (a x)")
                for m in range(TT):
                    last = dve.tensor_tensor(sts[:, m], bank[3][:, m * T:(m + 1) * T],
                                             dec_i[:, P - m * P:P - m * P + T], ALU.mult)
                last.then_inc(s["st_ready"], 1)
            ss = small[:, 176:176 + RET_CT * TT]
            dve.wait_ge(s["ro_ready"], 3 * RET_CT)
            dve.tensor_scalar(ss, ss, 1.0 / P, EPS, ALU.mult, ALU.add).then_inc(s["ret_ms"], 1)
            dve.wait_ge(s["ret_root"], 1)
            dve.reciprocal(ss, ss).then_inc(s["ret_rs"], 1)
            dve.wait_ge(s["ret_rs"], 1)
            o_flat = o_all.rearrange("p h t v -> p (h t) v")
            dve.tensor_tensor(o_flat, o_flat, ss.unsqueeze(2).broadcast_to([P, RET_CT * TT, P]), ALU.mult).then_inc(
                s["on_ready"], 1)
            dve.wait_ge(s["silu_ready"], 1)
            for h in range(RET_CT):
                k = (NA_W + RW_W) // P + h
                dve.wait_ge(s["ont_done"], h + 1)
                if h >= 2:
                    dve.wait_ge(s["y_ret_hi"], h - 1)
                dve.tensor_tensor(y_f[:, h % 2], bank[2 + h][:, 0:T], znr[:, NA_T + 3 * RET_CT + h],
                                  ALU.mult).then_inc(s["yf_ready"], 1)
                dve.wait_ge(s["y_ret_hi"], h + 1)
                dve.tensor_tensor(act_lo[:, k], y_f[:, h % 2], act_hi[:, k].bitcast(F32),
                                  ALU.subtract).then_inc(s["y_lo"], 1)

            stream(dve, OUT_FIRST, KT, lo)

            dve.wait_ge(s["yss_done"], TT)
            rs = small[:, 192:194]
            dve.tensor_scalar(rs, rs, 1.0 / D, EPS, ALU.mult, ALU.add).then_inc(s["yms_done"], 1)
            dve.wait_ge(s["yroot_done"], 1)
            dve.reciprocal(rs, rs).then_inc(s["yrs_done"], 1)
            dve.wait_ge(s["yrs_done"], 1)
            dve.wait_ge(s["x_again"], 16)
            dve.wait_ge(s["gain_in"], 16)
            for t in range(TT):
                y_t = psum[:, 4 * t:4 * t + 4].rearrange("p b n -> p (b n)")
                nxt(dve.scalar_tensor_tensor(y_sb[:, t], y_t, rs[:, t:t + 1], gains, ALU.mult, ALU.mult))
                dve.tensor_tensor(x1[:, t], x1[:, t], y_sb[:, t], ALU.add).then_inc(s["x1_ready"], 1)
            dve.wait_ge(s["hss_done"], TT)
            h2 = small[:, 208:210]
            dve.tensor_scalar(h2, h2, 1.0 / D, EPS, ALU.mult, ALU.add).then_inc(s["yms_done"], 1)
            dve.wait_ge(s["yroot_done"], 2)
            dve.reciprocal(h2, h2).then_inc(s["yrs_done"], 1)
            dve.wait_ge(s["yrs_done"], 2)
            for t in range(TT):
                dve.tensor_scalar(y_sb[:, t], x1[:, t], h2[:, t:t + 1], None, ALU.mult).then_inc(s["xn_ready"], 1)
            split_h(("g2", KT))

            stream(dve, UP_FIRST, FF_T, lo)

            def lo_down(c, i):
                lo(c, i)
                m = c - DOWN_FIRST
                dve.wait_ge(s["uhi_done"], 4 * i + m + 1)
                dve.tensor_tensor(u_lo[:, c % 2], u[:, ds(4 * i + m, 1), :].rearrange("p a t -> p (a t)"),
                                  u_hi[:, c % 2].bitcast(F32), ALU.subtract).then_inc(s["ulo_done"], 1)

            stream(dve, DOWN_FIRST, FF_T, lo_down)

            dve.wait_ge(s["yss_done"], 2 * TT)
            dve.tensor_scalar(rs, rs, 1.0 / D, EPS, ALU.mult, ALU.add).then_inc(s["yms_done"], 1)
            dve.wait_ge(s["yroot_done"], 3)
            dve.reciprocal(rs, rs).then_inc(s["yrs_done"], 1)
            dve.wait_ge(s["yrs_done"], 3)
            dve.wait_ge(s["gain_in"], 32)
            for t in range(TT):
                y_t = psum[:, 4 * t:4 * t + 4].rearrange("p b n -> p (b n)")
                nxt(dve.scalar_tensor_tensor(o_sb[:, t], y_t, rs[:, t:t + 1], gains, ALU.mult, ALU.mult))
                dve.tensor_tensor(o_sb[:, t], x1[:, t], o_sb[:, t], ALU.add).then_inc(s["o_ready"], 1)

        @block.scalar
        def _(act):
            def norm_sums(src, junk_, sums, name, waits):
                for t in range(TT):
                    act.wait_ge(*waits(t))
                    act.activation(junk_[:, t], src[:, t], ACT.Square, accum_out=sums[:, t:t + 1]).then_inc(s[name], 1)

            norm_sums(x_in, x_n, small[:, 0:2], "ss_done", lambda t: (s["x_in"], 16))
            act.wait_ge(s["ms_done"], 1)
            act.activation(small[:, 4:6], small[:, 2:4], ACT.Sqrt).then_inc(s["sq_done"], 1)
            act.wait_ge(s["vec_ready"], 1)

            def split_h(gain):
                for k in range(KT):
                    act.wait_ge(s["xt_done"], gain[1] + k + 1)
                    act.activation(act_hi[:, k], bank[2 + k % 6][:, 0:T], ACT.Copy,
                                   scale=vect(gain[0])[:, k:k + 1]).then_inc(s["h_hi"], 1)

            split_h(("g1", 0))
            act.wait_ge(s["coef_ready"], 2)

            def hi(c, i):
                raw_landed(act, c, i)
                if not (isinstance(i, int) and 4 * i + c < 2):
                    act.wait_ge(s["gemm_done"], 4 * i + c - 1)
                act.activation(w_hi[:, c % 2], raw[:, c % RAW], ACT.Copy).then_inc(s["hi_done"], 1)

            def to_zs(k, i):
                n = 2 if not (isinstance(i, int) and 2 * i + k == RW_PAIRS - 1) else 1
                act.wait_ge(s["gemm_done"], 4 * i + 2 * k + n)
                act.wait_ge(s["pad_free"], 2 * i + k + 1)
                ps = bank[k % 2][:, 0:n * T]
                act.activation(zpad[:, k % 2, 0:n, 1:T + 1], ps.rearrange("p (a t) -> p a t", a=n), ACT.Copy)
                for j in range(n):
                    ct = 4 * i + 2 * k + j
                    last = act.activation(zs[:, ds(ct, 1), :].rearrange("p a t -> p (a t)"), ps[:, j * T:(j + 1) * T],
                                          ACT.Copy, scale=small[:, ds(ct + 64, 1)])
                last.then_inc(s["bank_free"], 1)

            stream(act, 0, RW_T, hi, to_zs)

            act.wait_ge(s["pad_free"], 2 + RW_PAIRS)
            act.activation(z_wd, z_wd, ACT.Tanh).then_inc(s["kk_raw"], 1)
            act.activation(z_gd, z_gd, ACT.Sigmoid)
            for t in range(RW_CT):
                act.activation(kkn[:, t], zk[:, t], ACT.Copy, scale=small[:, 48 + t:49 + t]).then_inc(s["kk_raw"], 1)
            act.wait_ge(s["kk_raw"], 1 + RW_CT)
            act.activation(kk_sq, kkn, ACT.Square).then_inc(s["kk_sqd"], 1)
            for n, (dst, bias_name) in enumerate(((sig_w, "w0"), (rate, "a0"))):
                for d in range(2):
                    for t in range(RW_CT):
                        f = (n * 2 + d) * (RW_CT // 2) + t // 2
                        if t % 2 == 0:
                            act.wait_ge(s["lora_done"], f + 1)
                        last = act.activation(dst[:, d, t], bank[2 + f % 6][:, (t % 2) * T:(t % 2 + 1) * T], ACT.Sigmoid,
                                              bias=vect(bias_name)[:, d * RW_CT + t:d * RW_CT + t + 1])
                        if t % 2:
                            last.then_inc(s["lora_free"], 1)
            act.wait_ge(s["lora_free"], 2 * RW_CT)
            act.sem_inc(s["gates_ready"], 2)
            for n in range(3):
                act.wait_ge(s["kk_summed"], n + 1)
                act.activation(kk_ss[:, 2 * n:2 * n + 2].rearrange("p a t -> p (a t)"), bank[2 + n], ACT.Sqrt).then_inc(
                    s["kk_root"], 1)

            act.wait_ge(s["kk_ready"], 1)

            def prepare(t, p, first, second):
                stand(act, "z_ready", 2 * t, "act_passed")
                for d in range(2):
                    act.activation(kd[:, d], tile_of(rate[:, d], t), ACT.Identity, bias=small[:, ds(t + 32, 1)],
                                   scale=vect("ka")[:, ds(t, 1)]).then_inc(s["kd_scaled"], 1)
                for d in range(2):
                    act.wait_ge(s["cum_ready"], 5 * t + (3 * d + 2))
                    if d == 1:
                        act.wait_ge(s["tilde_ready"], 2 * t + 1)
                    act.activation(e_inc, cs, ACT.Exp, scale=-DECAY).then_inc(s["exp_ready"], 1)
                    act.activation(e_exc, ce, ACT.Exp, scale=-DECAY).then_inc(s["exp_ready"], 1)
                    act.activation(e_inv, cs, ACT.Exp, scale=DECAY).then_inc(s["exp_ready"], 1)
                    for piece in (first, second)[d] or ():
                        piece()
                act.wait_ge(s["bkt_done"], t + 1)
                for e in range(2):
                    act.activation(bkt[p][:, e], bank[4 + e].rearrange("p (n k) -> p n k", k=C), ACT.Copy).then_inc(
                        s["bkt_ready"], 1)

            def level(t, p, n, pieces):
                for piece in pieces or ():
                    piece()

            def chunk(b, q, n):
                gy = [bank[e][:, 0:2 * C].rearrange("p (d v) -> p d v", d=2) for e in range(2)]
                both = slice(n, 2 * NC - n, 2 * NC - 1 - 2 * n)

                def g():
                    act.wait_ge(s["gy_done"], 4 * b + (n + 1))
                    act.activation(gs[0:C], gy[0][0:C], ACT.Copy).then_inc(s["g_low"], 1)

                def u():
                    act.wait_ge(s["u_done"], 4 * b + (n + 1))
                    act.activation(uv[q][0:C, both, 0], bank[3][0:C, 0:2 * C].rearrange("p (d v) -> p d v", d=2),
                                   ACT.Copy).then_inc(s["u_low"], 1)

                def y():
                    if n >= 2:
                        return
                    act.wait_ge(s["y_done"], 4 * b + (n + 1))
                    y_i = chunks(tile_of(zk, b))
                    order = slice(n, NC - n, NC - 1 - 2 * n)
                    act.activation(y_i[0:C, order], gy[1][0:C], ACT.Copy)
                    act.activation(y_i[C:P, order], gy[0][C:P], ACT.Copy).then_inc(s["y_copied"], 1)

                return g, u, y

            rw_tiles(act, prepare, level, chunk)

            act.wait_ge(s["ln_ms"], 1)
            rstd = small[:, 128:128 + RW_CT * NC]
            act.activation(rstd, rstd, ACT.Sqrt).then_inc(s["ln_root"], 1)
            for n in range(3):
                act.wait_ge(s["gate_done"], n + 1)
                act.activation(gate[:, 2 * n:2 * n + 2].rearrange("p a t -> p (a t)"), bank[2 + n], ACT.Copy).then_inc(
                    s["gate_ready"], 1)
            act.wait_ge(s["y_rw_ready"], 1)

            def to_znr(k, i):
                act.wait_ge(s["gemm_done"], 4 * i + (RW_T + 2 * k + 2))
                act.activation(znr[:, ds(4 * i + 2 * k, 2), :].rearrange("p a t -> p (a t)"), bank[(k + RW_PAIRS) % 2],
                               ACT.Copy).then_inc(s["bank_free"], 1)

            stream(act, RW_T, NA_T + RET_T, hi, to_znr)

            for t in range(RW_CT):
                act.activation(act_hi[:, NA_T // 3 + t], y_rw[:, t], ACT.Copy).then_inc(s["y_rw_hi"], 1)
            act.wait_ge(s["bank_free"], RW_PAIRS + NR_PAIRS)
            act.activation(silu_s, znr[:, NA_T + 3 * RET_CT:NA_T + 4 * RET_CT], ACT.Sigmoid).then_inc(s["silu_sig"], 1)
            for t in range(TT):
                act.wait_ge(s["vna_done"], t + 1)
                act.activation(v_na[:, t], bank[2 + t], ACT.Copy).then_inc(s["vna_ready"], 1)
            with act.Fori(0, NA_T // 3) as i:
                act.wait_ge(s["mx_ready"], i + 1)
                for e in range(2):
                    for t in range(TT):
                        n = 2 * e + t
                        act.activation(sx[:, e, t], scores[:, e, t], ACT.Exp, bias=small[:, 160 + n:161 + n],
                                       accum_out=small[:, 164 + n:165 + n]).then_inc(s["p_ready"], 1)
                act.wait_ge(s["rinv_ready"], i + 1)
                act.wait_ge(s["o_done"], i + 1)
                for e in range(2):
                    for t in range(TT):
                        n = 2 * e + t
                        act.activation(yq[:, t, e * C:(e + 1) * C], bank[6][:, (2 * t + e) * C:(2 * t + e + 1) * C],
                                       ACT.Copy, scale=small[:, 168 + n:169 + n]).then_inc(s["yq_ready"], 1)
                act.wait_ge(s["yqt_done"], i + 1)
                act.activation(tile_of(act_hi, i), bank[7][:, 0:T], ACT.Copy).then_inc(s["y_na_hi"], 1)
            act.wait_ge(s["silu_ready"], 1)
            with act.Fori(0, RET_CT) as i:
                act.wait_ge(s["vt_done"], i + 1)
                act.wait_ge(s["ro_done"], i)
                act.activation(v_tok, bank[4][:, 0:T].rearrange("p (t v) -> p t v", t=TT), ACT.Copy).then_inc(
                    s["v_tok_ready"], 1)
                act.wait_ge(s["ro_done"], i + 1)
                act.wait_ge(s["ro_ready"], 3 * i)
                act.activation(o_all[:, ds(i, 1)].rearrange("p a t v -> p (a t v)"), bank[5][:, 0:T], ACT.Copy).then_inc(
                    s["ro_ready"], 1)
                for t in range(TT):
                    act.activation(junk[:, t], bank[5][:, t * P:(t + 1) * P], ACT.Square,
                                   accum_out=small[:, ds(2 * i + (176 + t), 1)]).then_inc(s["ro_ready"], 1)
            ss = small[:, 176:176 + RET_CT * TT]
            act.wait_ge(s["ret_ms"], 1)
            act.activation(ss, ss, ACT.Sqrt).then_inc(s["ret_root"], 1)
            for h in range(RET_CT):
                act.wait_ge(s["yf_ready"], h + 1)
                act.activation(act_hi[:, (NA_W + RW_W) // P + h], y_f[:, h % 2], ACT.Copy).then_inc(s["y_ret_hi"], 1)

            stream(act, OUT_FIRST, KT, hi)

            def out_sums(k):
                act.wait_ge(s["gemm_done"], k)
                for t in range(TT):
                    act.activation(y_sb[:, t], psum[:, 4 * t:4 * t + 4].rearrange("p b n -> p (b n)"), ACT.Square,
                                   accum_out=small[:, 192 + t:193 + t]).then_inc(s["yss_done"], 1)

            out_sums(UP_FIRST)
            act.wait_ge(s["yms_done"], 1)
            act.activation(small[:, 192:194], small[:, 192:194], ACT.Sqrt).then_inc(s["yroot_done"], 1)
            norm_sums(x1, y_sb, small[:, 208:210], "hss_done", lambda t: (s["x1_ready"], t + 1))
            act.wait_ge(s["yms_done"], 2)
            act.activation(small[:, 208:210], small[:, 208:210], ACT.Sqrt).then_inc(s["yroot_done"], 1)
            split_h(("g2", KT))

            def to_relu(k, i):
                act.wait_ge(s["gemm_done"], 4 * i + (UP_FIRST + 2 * k + 2))
                act.wait_ge(s["relu_free"], 2 * i + k + 1)
                act.activation(relu_t[:, k % 2], bank[(k + RW_PAIRS + NR_PAIRS) % 2], ACT.Relu).then_inc(
                    s["bank_free"], 1)

            stream(act, UP_FIRST, FF_T, hi, to_relu)
            act.wait_ge(s["relu_free"], 2 + UP_PAIRS)

            def hi_down(c, i):
                hi(c, i)
                act.activation(u_hi[:, c % 2], u[:, ds(4 * i + (c - DOWN_FIRST), 1), :].rearrange("p a t -> p (a t)"),
                               ACT.Copy).then_inc(s["uhi_done"], 1)

            stream(act, DOWN_FIRST, FF_T, hi_down)
            out_sums(DOWN_FIRST + FF_T)
            act.wait_ge(s["yms_done"], 3)
            act.activation(small[:, 192:194], small[:, 192:194], ACT.Sqrt).then_inc(s["yroot_done"], 1)

        @block.tensor
        def _(pe):
            def turned(src, first):
                for k in range(KT):
                    if k >= 6:
                        pe.wait_ge(s["h_lo"], first + k - 5)
                    for t in range(TT):
                        if k == 0:
                            pe.wait_ge(s["xn_ready"], TT * (first // KT) + t + 1)
                        last = pe.transpose(bank[2 + k % 6][:, t * P:(t + 1) * P], src[:, t, k * P:(k + 1) * P], ident)
                    last.then_inc(s["xt_done"], 1)

            pe.wait_ge(s["consts_in"], 16)
            pe.wait_ge(s["vec_in"], 16 * len(VEC))
            pe.transpose(bank[1][:, 0:VEC_N], vstage[0:VEC_N, :], ident[0:VEC_N, 0:VEC_N]).then_inc(s["vec_t"], 1)
            turned(x_n, 0)
            pe.wait_ge(s["h_lo"], KT)
            pe.wait_ge(s["vec_ready"], 1)

            def split_ready(c, i):
                pe.wait_ge(s["hi_done"], 4 * i + c + 1)
                pe.wait_ge(s["lo_done"], 4 * i + c + 1)

            def columns(c, i, k, pairs, wait=True):
                split_ready(c, i)
                q = pairs + k // 2
                if k % 2 == 0 and wait:
                    pe.wait_ge(s["bank_free"], 2 * i + q - 1)
                dst = bank[q % 2][:, (k % 2) * T:(k % 2 + 1) * T]
                for kt in range(KT):
                    wh = w_hi[:, c % 2, kt * P:(kt + 1) * P]
                    pe.matmul(dst, wh, act_hi[:, kt], start=kt == 0, stop=False)
                    pe.matmul(dst, wh, act_lo[:, kt], start=False, stop=False)
                    last = pe.matmul(dst, w_lo[:, c % 2, kt * P:(kt + 1) * P], act_hi[:, kt], start=False,
                                     stop=kt == KT - 1)
                last.then_inc(s["gemm_done"], 1)

            for k in range(4):
                columns(k, 0, k, 0, wait=False)
            with pe.Fori(0, (RW_T - 5) // 4) as i:
                for k in range(4):
                    columns(4 + k, i, 4 + k, 0)
            columns(RW_T - 1, 0, RW_T - 1, 0)

            pe.wait_ge(s["kk_raw"], 1)
            pe.wait_ge(s["lora_in"], 32)
            for n, (w_s, z_s) in enumerate(((w2s, z_wd), (a2s, z_ad))):
                for d in range(2):
                    for t in range(RW_CT):
                        f = (n * 2 + d) * (RW_CT // 2) + t // 2
                        if t % 2 == 0 and f >= 6:
                            pe.wait_ge(s["lora_free"], f - 5)
                        h = slice(d * C, (d + 1) * C)
                        last = pe.matmul(bank[2 + f % 6][:, (t % 2) * T:(t % 2 + 1) * T], w_s[h, t * P:(t + 1) * P],
                                         z_s[h, :], start=True, stop=True)
                        if t % 2:
                            last.then_inc(s["lora_done"], 1)
            pe.wait_ge(s["kk_sqd"], 1)
            for n in range(3):
                pe.wait_ge(s["lora_free"], 7 + n)
                pe.matmul(bank[2 + n], ones, kk_sq[:, 2 * n:2 * n + 2].rearrange("p a t -> p (a t)"), start=True,
                          stop=True).then_inc(s["kk_summed"], 1)
            pe.wait_ge(s["kk_root"], 3)
            pe.wait_ge(s["bank_free"], RW_PAIRS)

            def prepare(t, p, first, second):
                for piece in first or ():
                    piece()
                for d in range(2):
                    stand(pe, "tilde_ready", 2 * t + (d + 1), "pe_passed")
                    for e in range(2):
                        h = slice(e * C, e * C + C)
                        for c in range(NC):
                            last = pe.matmul(bank[4 + 2 * d + e][:, c * P:(c + 1) * P], bk[h, d, c, e * C:e * C + P],
                                             ar[p][h, d, c, e * C:e * C + P], start=True, stop=True)
                    last.then_inc(s["bm_done"], 1)
                    if second and d == 0:
                        second[0]()
                        second[1]()
                if second:
                    second[2]()
                stand(pe, "vb_ready", 3 * t, "pe_passed")
                for d in range(2):
                    for c in range(NC):
                        for e in range(2):
                            h = slice(e * C, e * C + C)
                            last = pe.matmul(bank[2][h, (d * NC + c) * C:(d * NC + c + 1) * C], ar[p][h, d, c, 0:C],
                                             bk[h, d, c, 0:C], start=True, stop=True)
                last.then_inc(s["a_done"], 1)
                stand(pe, "bm_ready", 4 * t + 2, "pe_passed")
                for d in range(2):
                    for e in range(2):
                        h = slice(e * C, e * C + C)
                        for c in range(NC):
                            last = pe.transpose(bank[4 + e][:, (d * NC + c) * C:(d * NC + c + 1) * C],
                                                bk[h, d, c, e * C:e * C + P], ident[h, h])
                last.then_inc(s["bkt_done"], 1)
                stand(pe, "v_copied", t + 1, "pe_passed")
                stand(pe, "bonus_in", t + 1, "pe_passed")
                stand(pe, "a_ready", t + 1, "pe_passed")
                pe.matmul(bank[2][:, T:2 * T], ones, tmp, start=True, stop=True)
                for c in range(NC):
                    for e in range(2):
                        h, o = slice(e * C, e * C + C), slice((1 - e) * C, (2 - e) * C)
                        last = pe.matmul(bank[2][o, c * C:(c + 1) * C], vst[h, c * C:(c + 1) * C], ident[h, h],
                                         start=True, stop=True)
                last.then_inc(s["vb_done"], 1)
                stand(pe, "bkt_ready", 2 * t + 2, "pe_passed")
                stand(pe, "bm_ready", 4 * t + 4, "pe_passed")

            def level(t, p, n, pieces):
                for d in range(2):
                    if pieces:
                        pieces[d]()
                    stand(pe, "zd_ready", 10 * t + (2 * n + d + 1), "pe_passed")
                    for m in range(NC):
                        for e in range(2):
                            h = slice(e * C, e * C + C)
                            last = pe.matmul(bank[4 + d][h, m * C:(m + 1) * C], az[p][h, d * NC + m],
                                             zd[h, d * NC + m], start=True, stop=True)
                    last.then_inc(s["p1_done"], 1)
                for d in range(2):
                    stand(pe, "zt_ready", 10 * t + (2 * n + d + 1), "pe_passed")
                    stand(pe, "p1_ready", 10 * t + (2 * n + d + 1), "pe_passed")
                    for m in range(NC):
                        for e in range(2):
                            h = slice(e * C, e * C + C)
                            last = pe.matmul(bank[4 + d][h, T + m * C:T + (m + 1) * C], zt[h, d * NC + m],
                                             p1s[h, d * NC + m], start=True, stop=True)
                    last.then_inc(s["q_done"], 1)
                    if pieces and d == 0:
                        pieces[2]()

            def chunk(b, q, n):
                gy = [bank[e][:, 0:2 * C].rearrange("p (d v) -> p d v", d=2) for e in range(2)]
                cd = (n, NC - 1 - n)
                at = (0, 1) if n < 2 else (1, 0)

                def g():
                    if n in (0, 3):
                        stand(pe, "y_added", 2 * b + n // 3, "pe_passed")
                    else:
                        stand(pe, "y_copied", 2 * b + n, "pe_passed")
                    if n == 0:
                        stand(pe, "z_ready", 2 * b + 2, "pe_passed")
                    for d in range(2):
                        for e in range(2):
                            h, o = slice(e * C, e * C + C), slice((1 - e) * C, (2 - e) * C)
                            last = pe.matmul(gy[e][h, at[d]], bms[q][o, (2 * d + e) * NC + cd[d], h],
                                             uv[q][o, d * NC + cd[d], e], start=d == 0, stop=n == 0,
                                             skip_group_check=True)
                    if n:
                        last.then_inc(s["v_part"], 1)
                        stand(pe, "s_ready", 3 * b + n, "pe_passed")
                        stand(pe, "v_part", 3 * b + n, "pe_passed")
                        for d in range(2):
                            for e in range(2):
                                h = slice(e * C, e * C + C)
                                last = pe.matmul(gy[e][h, at[d]], ar[q][h, d, cd[d], 2 * e * C:2 * e * C + C], state[h, d],
                                                 start=False, stop=True, skip_group_check=True)
                    last.then_inc(s["gy_done"], 1)

                def u():
                    stand(pe, "g_low", 4 * b + (n + 1), "pe_passed")
                    stand(pe, "g_high", 4 * b + (n + 1), "pe_passed")
                    for d in range(2):
                        for e in range(2):
                            h = slice(e * C, e * C + C)
                            last = pe.matmul(bank[3][h, d * C:(d + 1) * C], az[q][h, d * NC + cd[d]], gs[h, at[d]],
                                             start=True, stop=True)
                    last.then_inc(s["u_done"], 1)
                    if n:
                        for d in range(2):
                            for e in range(2):
                                h, o = slice(e * C, e * C + C), slice((1 - e) * C, (2 - e) * C)
                                pe.matmul(gy[e][o, at[d]], ar[q][h, d, cd[d], C:2 * C], state[h, d], start=d == 0,
                                          stop=False, skip_group_check=True)

                def state_and_y():
                    stand(pe, "u_low", 4 * b + (n + 1), "pe_passed")
                    stand(pe, "u_high", 4 * b + (n + 1), "pe_passed")
                    if n < NC - 1:
                        for d in range(2):
                            for e in range(2):
                                last = pe.matmul(bank[3][e * C:(e + 1) * C, d * C:(d + 1) * C],
                                                 bkt[q][:, e, d * NC + cd[d]], uv[q][:, d * NC + cd[d], e],
                                                 start=True, stop=True)
                        last.then_inc(s["s_done"], 1)
                    for d in range(2):
                        for e in range(2):
                            o = slice((1 - e) * C, (2 - e) * C)
                            last = pe.matmul(gy[e][o, at[d]], bms[q][:, (2 * d + e) * NC + cd[d], o],
                                             uv[q][:, d * NC + cd[d], e], start=n == 0 and d == 0, stop=True,
                                             skip_group_check=True)
                    last.then_inc(s["y_done"], 1)

                return g, u, state_and_y

            rw_tiles(pe, prepare, level, chunk)

            pe.wait_ge(s["g2_in"], 16)
            for n in range(3):
                for t in range(2 * n, 2 * n + 2):
                    last = pe.matmul(bank[2 + n][:, (t % 2) * T:(t % 2 + 1) * T], g2s[:, t * P:(t + 1) * P], z_gd,
                                     start=True, stop=True)
                last.then_inc(s["gate_done"], 1)
            pe.wait_ge(s["ln_ready"], 1)
            for t in range(RW_CT):
                for c in range(NC):
                    for e in range(2):
                        h, o = slice(e * C, e * C + C), slice((1 - e) * C, (2 - e) * C)
                        at = (t % 2) * T + c * C
                        last = pe.matmul(bank[5 + t // 2][h, at:at + C], zk[o, t, c * C:(c + 1) * C], ident[o, o],
                                         start=True, stop=True)
                if t % 2:
                    last.then_inc(s["yt_done"], 1)

            for k in range(2):
                columns(RW_T + k, 0, k, RW_PAIRS)
            for k in range(2, 4):
                columns(RW_T + k, 0, k, RW_PAIRS)
            with pe.Fori(0, (NA_T + RET_T) // 4 - 1) as i:
                for k in range(4):
                    columns(RW_T + 4 + k, i, k + 4, RW_PAIRS)

            pe.wait_ge(s["bank_free"], RW_PAIRS + NR_PAIRS)
            for t in range(TT):
                for n in range(NA_W // P):
                    last = pe.transpose(bank[2 + t][:, n * P:(n + 1) * P], znr[:, 2 * NA_W // P + n, t * P:(t + 1) * P],
                                        ident)
                last.then_inc(s["vna_done"], 1)
            pe.wait_ge(s["vna_ready"], TT)
            pe.wait_ge(s["bias_ready"], NA_HEADS)
            pe.wait_ge(s["flip_in"], 16)
            with pe.Fori(0, NA_T // 3) as i:
                pe.wait_ge(s["k_copied"], i + 1)
                pe.wait_ge(s["q_ready"], i + 1)
                for e in range(2):
                    h = slice(e * C, e * C + C)
                    pe.matmul(bank[2 + e], flip, bias[:, ds(i * 2 + e, 1), :, :].rearrange("p h t k -> p (h t k)"),
                              start=True, stop=False)
                    for t in range(TT):
                        last = pe.matmul(bank[2 + e][:, t * T:(t + 1) * T], q_s[h, t * P:(t + 1) * P], k_s[h, :],
                                         start=False, stop=t == TT - 1)
                last.then_inc(s["sc_done"], 1)
                pe.wait_ge(s["p_ready"], 4 * i + 4)
                pe.wait_ge(s["pt_ready"], 2 * i)
                for e in range(2):
                    for kt in range(TT):
                        for t in range(TT):
                            last = pe.transpose(bank[4 + e][:, (2 * kt + t) * P:(2 * kt + t + 1) * P],
                                                sx[:, e, t, kt * P:(kt + 1) * P], ident)
                last.then_inc(s["pt_done"], 1)
                pe.wait_ge(s["pt_ready"], 2 * i + 2)
                pe.wait_ge(s["yq_ready"], 4 * i)
                for t in range(TT):
                    for e in range(2):
                        for kt in range(TT):
                            last = pe.matmul(bank[6][:, (2 * t + e) * C:(2 * t + e + 1) * C], pts[:, e, kt, t],
                                             v_na[:, kt, ds(i * P + e * C, C)], start=kt == 0, stop=kt == TT - 1)
                last.then_inc(s["o_done"], 1)
                pe.wait_ge(s["yq_ready"], 4 * i + 4)
                pe.wait_ge(s["y_na_lo"], i)
                for t in range(TT):
                    last = pe.transpose(bank[7][:, t * P:(t + 1) * P], yq[:, t], ident)
                last.then_inc(s["yqt_done"], 1)

            pe.wait_ge(s["y_na_lo"], NA_T // 3)
            with pe.Fori(0, RET_CT) as i:
                pe.wait_ge(s["qk_ready"], 2 * i)
                for n in range(2):
                    last = pe.matmul(bank[2][:, n * T:(n + 1) * T], turn,
                                     znr[:, ds(i + (NA_T + n * RET_CT), 1), :].rearrange("p a t -> p (a t)"),
                                     start=True, stop=True)
                last.then_inc(s["rot_done"], 1)
                pe.wait_ge(s["rot_in"], 3 * i + 3)
                pe.wait_ge(s["v_tok_ready"], i)
                for t in range(TT):
                    last = pe.transpose(bank[4][:, t * P:(t + 1) * P], v_cp[:, t * P:(t + 1) * P], ident)
                last.then_inc(s["vt_done"], 1)
                pe.wait_ge(s["qk_ready"], 2 * i + 2)
                pe.wait_ge(s["st_ready"], i)
                for m in range(TT):
                    last = pe.matmul(bank[3][:, m * T:(m + 1) * T], qk[:, 1, m * P:(m + 1) * P], qk[:, 0], start=True,
                                     stop=True)
                last.then_inc(s["st_done"], 1)
                pe.wait_ge(s["st_ready"], i + 1)
                pe.wait_ge(s["v_tok_ready"], i + 1)
                pe.wait_ge(s["ro_ready"], 3 * i)
                for t in range(TT):
                    for m in range(TT):
                        last = pe.matmul(bank[5][:, t * P:(t + 1) * P], sts[:, m, t * P:(t + 1) * P], v_tok[:, m],
                                         start=m == 0, stop=m == TT - 1)
                last.then_inc(s["ro_done"], 1)
            pe.wait_ge(s["on_ready"], 1)
            for h in range(RET_CT):
                for t in range(TT):
                    last = pe.transpose(bank[2 + h][:, t * P:(t + 1) * P], o_all[:, h, t], ident)
                last.then_inc(s["ont_done"], 1)

            def rows(c, i, lhs_hi, lhs_lo, first=False, final=False):
                split_ready(c, i)
                for t in range(TT):
                    h = slice(t * P, (t + 1) * P)
                    for lhs, w, a, z in ((lhs_hi, w_hi, first, False), (lhs_hi, w_lo, False, False),
                                         (lhs_lo, w_hi, False, final)):
                        for b in range(4):
                            last = pe.matmul(bank[4 * t + b], lhs[:, h], w[:, c % 2, b * 512:(b + 1) * 512],
                                             start=a, stop=z)
                last.then_inc(s["gemm_done"], 1)

            pe.wait_ge(s["y_lo"], RW_CT + RET_CT)
            for n in range(KT):
                rows(OUT_FIRST + n, 0, act_hi[:, n], act_lo[:, n], n == 0, n == KT - 1)

            turned(y_sb, KT)
            pe.wait_ge(s["h_lo"], 2 * KT)
            with pe.Fori(0, FF_T // 4) as i:
                for k in range(4):
                    columns(UP_FIRST + k, i, k, RW_PAIRS + NR_PAIRS)

            pe.wait_ge(s["bank_free"], RW_PAIRS + NR_PAIRS + UP_PAIRS)

            def down(c, i, **ends):
                m = c - DOWN_FIRST
                pe.wait_ge(s["uhi_done"], 4 * i + m + 1)
                pe.wait_ge(s["ulo_done"], 4 * i + m + 1)
                rows(c, i, u_hi[:, c % 2], u_lo[:, c % 2], **ends)

            down(DOWN_FIRST, 0, first=True)
            with pe.Fori(0, (FF_T - 1) // 4) as i:
                for k in range(4):
                    down(DOWN_FIRST + 1 + k, i)
            for n in range(FF_T - 3, FF_T):
                down(DOWN_FIRST + n, 0, final=n == FF_T - 1)


_INS = ("x", "pre_mix_g", "w_in", "na_rpb", "rw_mu_prev", "rw_mu_next", "rw_w0", "rw_w2", "rw_a0", "rw_a2", "rw_k_k",
        "rw_k_a", "rw_r_k", "rw_g2", "rw_lnx_g", "rw_lnx_b", "w_out", "post_mix_g", "pre_mlp_g", "w_up", "w_down",
        "post_mlp_g")


def kernel(**inputs):
    import concourse.bacc as bacc
    from concourse.bass_utils import run_bass_kernel_spmd

    nc = bacc.Bacc("TRN2", target_bir_lowering=False, num_devices=1)
    tables, decays = constants()
    arrays = {f"in_{n}": np.ascontiguousarray(inputs[n]) for n in _INS}
    arrays["in_tables"], arrays["in_decays"] = tables, decays
    args = [nc.dram_tensor(n, a.shape, mybir.dt.from_np(a.dtype), kind="ExternalInput").ap() for n, a in arrays.items()]
    args.append(nc.dram_tensor("out_x", (1, T, D), F32, kind="ExternalOutput").ap())
    layer(nc, *args)
    r = run_bass_kernel_spmd(nc, [arrays], core_ids=[0])
    return r.results[0]["out_x"]
```

```python
from contextlib import ExitStack
import math

import numpy as np

import concourse.bass as bass
from concourse import mybir

ALU = mybir.AluOpType
ACT = mybir.ActivationFunctionType
F32 = mybir.dt.float32
F32R = mybir.dt.float32r
AX_X = mybir.AxisListType.X
ds = bass.ds

P = 128
T = 256
TT = T // P
D = 2048
KT = D // P
NA_W, RW_W, RET_W = D // 4, 3 * D // 8, 3 * D // 8
NA_HEADS, NA_HD = NA_W // 64, 64
GRID_W, ROWS, WIN = 64, T // 64, 16
NA_T, RW_CT, RET_CT = 3 * NA_W // P, RW_W // P, RET_W // P
RW_T = 3 * RW_CT + 3
RET_T = 4 * RET_CT
W_IN_T = NA_T + RW_T + RET_T
FF = 4 * D
FF_T = FF // P
C = 64
NC = T // C
LEVELS = [2, 4, 8, 16, 32]
EPS, LNX_EPS = 1e-6, 64e-5
DECAY = math.exp(-0.5)

UNIT = 2048
RAW = 4
U_RING = 4
OUT_FIRST = W_IN_T
UP_FIRST = OUT_FIRST + KT
DOWN_FIRST = UP_FIRST + FF_T

VEC = {}
_at = 0
for _n, _w in (("g1", KT), ("g2", KT), ("mup", RW_T), ("mun", RW_T), ("w0", 2 * RW_CT), ("a0", 2 * RW_CT),
               ("kk", RW_CT), ("ka", RW_CT), ("rk", RW_CT), ("lg", RW_CT), ("lb", RW_CT)):
    VEC[_n] = (_at, _at + _w)
    _at += _w
VEC_N = _at
CST = {}
_at = 0
for _n, _w in (("ident", P), ("ones", P), ("turn", P), ("cos", T), ("sin", T), ("bm", 4 * P),
               ("off", (len(LEVELS) + 1) * C), ("eye", C), ("keep", T), ("win", GRID_W)):
    CST[_n] = (_at, _at + _w)
    _at += _w
CST_N = _at


def constants():
    c = np.zeros((P, CST_N), np.float32)

    def put(name, a):
        c[:, CST[name][0]:CST[name][1]] = a.reshape(P, -1)

    put("ident", np.eye(P, dtype=np.float32))
    half = np.arange(P) // C
    put("ones", (half[:, None] == half[None]).astype(np.float32))
    turn = np.zeros((P, P), np.float32)
    for j in range(0, P, 2):
        turn[j + 1, j], turn[j, j + 1] = -1.0, 1.0
    put("turn", turn)
    theta = np.float32(1.0) / np.float32(10000.0) ** np.linspace(0.0, 1.0, P // 2, dtype=np.float32)
    ang = np.arange(T, dtype=np.float32)[:, None] * theta[None].astype(np.float32)
    put("cos", np.repeat(np.cos(ang).T, 2, axis=0))
    put("sin", np.repeat(np.sin(ang).T, 2, axis=0))
    j, t = np.arange(C)[:, None], np.arange(C)[None]
    strict = [(j < t), (j > t)]
    incl = [(j <= t), (j >= t)]
    bm = np.zeros((P, 2, 2, P), np.float32)
    for d in range(2):
        a_r = np.concatenate([strict[d], incl[d]], 1)
        bm[:, d, 0] = np.concatenate([a_r, a_r], 0)
        r_a = np.concatenate([incl[d], strict[d]], 1)
        bm[:, d, 1] = np.concatenate([r_a, r_a], 0)
    put("bm", bm)
    off = np.stack([(j // (2 * m) == t // (2 * m)) & (j // m != t // m) for m in [1] + LEVELS], 1)
    put("off", np.concatenate([off, off], 0).astype(np.float32))
    put("eye", np.concatenate([np.eye(C), np.eye(C)], 0).astype(np.float32))
    keep = np.ones((P, T), np.float32)
    keep[:, 0::C] = 0.0
    put("keep", keep)
    col = np.arange(GRID_W)
    start = np.clip(col - WIN // 2, 0, GRID_W - WIN)
    seen = (col[None] >= start[:, None]) & (col[None] < start[:, None] + WIN)
    win = np.where(seen, 0.0, -1e30).astype(np.float32)
    put("win", np.concatenate([win[::-1], win[::-1]], 0))
    lg = np.log(1.0 - 2.0 ** (-5.0 - np.arange(RET_CT)))
    dist = np.abs(np.arange(3 * P)[None] - P - np.arange(P)[:, None])
    decay = np.exp(dist[:, None, :] * lg[None, :, None]) * P ** -0.5
    flip = np.zeros((P, P), np.float32)
    for p in range(P):
        flip[p, p // GRID_W * GRID_W + GRID_W - 1 - p % GRID_W] = 1.0
    return c, np.concatenate([decay.astype(np.float32).reshape(P, -1), flip], 1)


def layer(nc, x, pre_mix_g, w_in, na_rpb, rw_mu_prev, rw_mu_next, rw_w0, rw_w2, rw_a0, rw_a2, rw_k_k, rw_k_a,
          rw_r_k, rw_g2, rw_lnx_g, rw_lnx_b, w_out, post_mix_g, pre_mlp_g, w_up, w_down, post_mlp_g,
          cst_d, decay_d, out):
    with ExitStack() as ctx:
        def sb(name, shape, dt=F32):
            return ctx.enter_context(nc.sbuf_tensor(name, shape, dt))

        def sem(name):
            return ctx.enter_context(nc.semaphore(name))

        raw = sb("raw", [P, RAW, UNIT])
        w_hi = sb("w_hi", [P, 2, UNIT], F32R)
        w_lo = sb("w_lo", [P, 2, UNIT], F32R)
        act_hi = sb("act_hi", [P, KT, T], F32R)
        act_lo = sb("act_lo", [P, KT, T], F32R)
        u_hi = sb("u_hi", [P, U_RING, T], F32R)
        u_lo = sb("u_lo", [P, U_RING, T], F32R)
        cst = sb("cst", [P, CST_N])
        vec = sb("vec", [P, VEC_N])
        small = sb("small", [P, 256])
        ARENA = 23680
        arena = sb("arena", [P, ARENA])
        psum = ctx.enter_context(nc.psum_tensor("psum", [P, 8, 512], F32))
        bank = [psum[:, b] for b in range(8)]
        scores = psum[:, 2:4].rearrange("p e (t k) -> p e t k", t=TT)

        yt_bank = [bank[6], bank[7], bank[5]]
        gate_bank = [bank[2], bank[4], bank[5]]

        def const(name):
            return cst[:, CST[name][0]:CST[name][1]]

        def vect(name):
            return vec[:, VEC[name][0]:VEC[name][1]]

        ident, ones, turn_pairs = const("ident"), const("ones"), const("turn")
        bm_mask = const("bm").rearrange("p (d e t) -> p d e t", d=2, e=2)
        off = const("off").rearrange("p (m t) -> p m t", t=C)
        eye = const("eye")
        keep = const("keep")

        def cut(at, *shape):
            n = int(np.prod(shape))
            assert at + n <= ARENA, (at, n)
            v = arena[:, at:at + n]
            names = "abcd"[:len(shape)]
            if len(shape) == 1:
                return v
            return v.rearrange(f"p ({' '.join(names)}) -> p {' '.join(names)}",
                               **{k: s for k, s in zip(names[1:], shape[1:])})

        zs = cut(0, RW_T, T)
        zr, zk, zv = zs[:, 0:RW_CT], zs[:, RW_CT:2 * RW_CT], zs[:, 2 * RW_CT:3 * RW_CT]
        z_wd, z_ad, z_gd = (zs[:, 3 * RW_CT + n] for n in range(3))
        a0_ = RW_T * T
        sig_w = cut(a0_, 2, RW_CT, T)
        rate = cut(a0_ + 3072, 2, RW_CT, T)
        kkn = cut(a0_ + 6144, RW_CT, T)
        L = a0_ + 7680
        x_in = cut(L, TT, D)
        x_n = cut(L + 4096, TT, D)
        zpad = cut(L + 8192, 2, 2, T + 2)
        vstage = cut(L + 9300, P)
        w2s = cut(L, RW_W)
        a2s = cut(L + RW_W, RW_W)
        kk_ss = cut(L + 2 * RW_W, RW_CT, T)
        kk_sq = cut(L + 4 * RW_W, RW_CT, T)
        cs = cut(L, T)
        ce = cut(L + 256, T)
        e_inc = cut(L + 512, T)
        e_exc = cut(L + 768, T)
        e_inv = cut(L + 1024, T)
        kd = cut(L + 1280, 2, T)
        bn = cut(L + 1792, T)
        tmp = cut(L + 2048, T)
        late = raw[:].rearrange("p r n -> p (r n)")[:, 6144:7680].rearrange("p (w n t) -> p w n t", w=3, t=C)
        zd, zt, p1s = (late[:, w] for w in range(3))
        bk = cut(L + 2304, 2, NC, 3 * C)
        gs = cut(L + 3840, 2, C)
        state = cut(L + 3968, 2, C)
        state_dec = cut(L + 4096, 2, C)
        vst = cut(L + 4224, T)
        ar, bms, az, bkt, uv, ec = [], [], [], [], [], []
        for q, (mem, at) in enumerate(((raw[:].rearrange("p r n -> p (r n)"), 0), (arena, L + 4480))):
            ar.append(mem[:, at:at + 1536].rearrange("p (d c n) -> p d c n", d=2, c=NC))
            bms.append(mem[:, at + 1536:at + 3584].rearrange("p (n t) -> p n t", t=P))
            az.append(mem[:, at + 3584:at + 4096].rearrange("p (n t) -> p n t", t=C))
            bkt.append(mem[:, at + 4096:at + 5120].rearrange("p (e n k) -> p e n k", e=2, k=C))
            uv.append(mem[:, at + 5120:at + 6144].rearrange("p (n e v) -> p n e v", e=2, v=C))
            ec.append(small[:, 16 + 8 * q:24 + 8 * q].rearrange("p (d c) -> p d c", d=2))
        gate = cut(a0_, RW_CT, T)
        g2s = cut(a0_ + 3072, RW_W)
        ysq = cut(L, RW_CT * NC, C)
        y_rw = cut(a0_ + 6144, RW_CT, T)
        znr = cut(0, NA_T + RET_T, T)
        o_all = cut(9216, RET_CT, TT, P)
        v_cp = cut(10752, T)
        v_tok = cut(11008, TT, P)
        bias = cut(L, NA_HEADS, TT, T)
        decay = cut(L + 4096, RET_CT, 3 * P)
        W_ = L + 6400
        v_na = cut(W_, TT, NA_W)
        q_s = cut(W_ + 1024, T)
        k_s = cut(W_ + 1280, T)
        sx = cut(W_ + 1536, 2, TT, T)
        pts = cut(W_ + 2560, 2, TT, TT, P)
        yq = cut(W_ + 3584, TT, P)
        flip = cut(W_ + 3840, P)
        silu_s = cut(9216, RET_CT, T)
        V_ = a0_ + 6144
        qk = cut(V_, 2, T)
        qk_cos = cut(V_ + 512, 2, T)
        sts = cut(V_ + 1024, TT, T)
        junk = cut(W_ + 3968, TT, P)
        y_f = cut(W_, RET_CT, T)
        u = cut(0, FF_T, T)
        x1 = cut(16384, TT, D)
        gains = cut(20480, D)
        relu_t = cut(22528, 2, 512)
        o_sb = cut(0, TT, D)
        y_sb = cut(0, TT, D)

        s = {n: sem(n) for n in (
            "x_in", "x_in_next", "consts_in", "vec_in", "lora_in", "g2_in", "bias_in", "flip_in", "decay_in",
            "gain_in", "x_again", "out_written",
            "ss_done", "ms_done", "sq_done", "rs_done", "xn_ready", "xt_done", "h_hi", "h_lo",
            "vec_t", "vec_ready", "coef_ready",
            "hi_done", "lo_done", "gemm_done", "bank_free", "pad_free", "zs_ready",
            "lora_done", "lora_free", "kk_raw", "wd_ready", "half_done", "kk_sqd", "kk_summed", "kk_root", "kk_ready",
            "cum_ready", "exp_ready", "kb_ready", "bonus_in", "kd_scaled", "kd_summed", "pool_passed", "act_passed",
            "v_copied", "tilde_ready", "again_ready", "bm_done",
            "bkt_done", "vb_done", "bm_ready", "bkt_ready", "vb_ready", "zd_ready", "zt_ready", "p0_ready", "pe_passed", 
            "p1_done", "v_part", "p1_ready", "q_done", "z_ready", "gy_done", "g_low", "g_high", "u_done", "u_low", "u_high",
            "s_done", "s_ready", "dec_ready", "y_done", "y_copied", "y_added", 
            "ln_ms", "ln_root", "ln_ready", "gate_done", "gate_ready", "yt_done", "y_rw_ready",
            "bias_ready", "vna_done", "vna_ready", "k_copied", "q_ready", "sc_done", "mx_ready", "p_ready", "rinv_ready",
            "pt_done", "pt_ready", "o_done", "yq_ready", "yqt_done", "y_na_hi", "y_na_lo",
            "silu_sig", "silu_ready", "rot_in", "rot_done", "qk_ready", "vt_done", "v_tok_ready", "st_done", "st_ready",
            "ro_done", "ro_ready", "ret_ms", "ret_root", "ret_rs", "on_ready", "ont_done", "yf_ready", "y_ret_hi",
            "y_rw_hi", "y_lo", "yss_done", "yms_done", "yroot_done", "yrs_done", "x1_ready", "hss_done",
            "relu_free", "uhi_done", "ulo_done", "o_ready",
            "dve_step", "pool_step")}
        raw_in = [sem(f"raw_in{r}") for r in range(RAW)]
        block = ctx.enter_context(nc.Block())

        def stream(eng, first, count, convert, drain=None, begun=0, then=None):
            quads = count // 4
            for n in range(begun, 2):
                convert(first + n, 0)
            with eng.Fori(0, quads - 1) as i:
                for pair in range(2):
                    convert(first + 2 * pair + 2, i)
                    convert(first + 2 * pair + 3, i)
                    if drain:
                        drain(pair, i)
            rest = [first + n for n in range(4 * quads - 2, count)]
            pairs = list(range(2 * quads - 2, (count + 1) // 2))
            while rest or pairs:
                for n in rest[:2]:
                    convert(n, 0)
                rest = rest[2:]
                if then and len(pairs) == 1:
                    then()
                if pairs and drain:
                    drain(pairs[0], 0)
                pairs = pairs[1:]

        def raw_landed(eng, c, i):
            eng.wait_ge(raw_in[c % RAW], 16 * (i + c // RAW + 1))

        def link(eng, counter, name, ins):
            counter[0] += 1
            ins.then_inc(s[name], 1)
            eng.wait_ge(s[name], counter[0])

        def stand(eng, name, value, passed):
            eng.wait_ge(s[name], value)
            eng.sem_inc(s[passed], 1)

        def tile_of(view, i):
            return view[:, ds(i, 1), :].rearrange("p a t -> p (a t)")

        def rw_tiles(eng, tilde, products, level, chunk, closing=(), tail=()):
            def turn(t, p, first=False, last=False):
                pieces = [chunk(t - 1, 1 - p, n) for n in range(NC)] if not first else [()] * NC
                ahead = tilde(t + 1, 1 - p) if not last else closing
                products(t, p, pieces[0], pieces[1])
                for n in range(len(LEVELS)):
                    level(t, p, n, pieces[2 + n] if n < NC - 2 else (),
                          ahead[2 * (n - 2):2 * (n - 1)] if n >= 2 else ())

            run(tilde(0, 0))
            turn(0, 0, first=True)
            with eng.Fori(0, (RW_CT - 2) // 2) as i:
                turn(2 * i + 1, 1)
                turn(2 * i + 2, 0)
            turn(RW_CT - 1, 1, last=True)
            for n in range(NC):
                run(chunk(RW_CT - 1, 1, n))
                run(tail[n:n + 1])

        def run(pieces):
            for piece in pieces:
                piece()

        def mixers(eng, turn):
            with eng.Fori(0, NA_T // 3 - 1) as i:
                turn(i, True, True)
            turn(NA_T // 3 - 1, True)
            for i in range(NA_T // 3, RET_CT):
                turn(i, False)

        def chunks(view):
            return view.rearrange("p (c t) -> p c t", t=C)

        RW_PAIRS, NR_PAIRS, UP_PAIRS = (RW_T + 1) // 2, (NA_T + RET_T) // 2, FF_T // 2

        @block.sync
        def _(sp):
            for t in range(TT):
                sp.dma_start(x_in[:, t], x[0, t * P:(t + 1) * P]).then_inc(s[("x_in", "x_in_next")[t]], 16)
            sp.dma_start(cst[:], cst_d).then_inc(s["consts_in"], 16)
            for name, v in (("g1", pre_mix_g), ("g2", pre_mlp_g), ("mup", rw_mu_prev), ("mun", rw_mu_next),
                            ("w0", rw_w0.rearrange("l d c -> l (d c)")), ("a0", rw_a0.rearrange("l d c -> l (d c)")),
                            ("kk", rw_k_k), ("ka", rw_k_a), ("rk", rw_r_k.rearrange("l h c -> l (h c)")),
                            ("lg", rw_lnx_g), ("lb", rw_lnx_b)):
                a, b = VEC[name]
                sp.dma_start(vstage[a:b, :], v.rearrange("l (t p) -> (l t) p", p=P)).then_inc(s["vec_in"], 16)

            def fetch(c, i, src, wait=True):
                if wait:
                    sp.wait_ge(s["lo_done"], 4 * i + c - RAW + 1)
                dst = raw[:, c % RAW, :]
                if len(src.shape) == 3:
                    dst = dst.rearrange("p (k c) -> p k c", k=KT)
                sp.dma_start(dst, src).then_inc(raw_in[c % RAW], 16)

            w_in_v = w_in[0].rearrange("(k p) c -> p k c", p=P)
            w_up_v = w_up[0].rearrange("(k p) c -> p k c", p=P)
            w_out_v = w_out[0].rearrange("(k p) c -> p k c", p=P)
            w_down_v = w_down[0].rearrange("(k p) c -> p k c", p=P)

            def columns(view, tile):
                return view[:, :, ds(tile * P, P)]

            def rows(view, tile):
                return view[:, ds(tile, 1), :].rearrange("p k c -> p (k c)")

            for n in range(RAW):
                fetch(n, 0, columns(w_in_v, NA_T + n), wait=False)
            with sp.Fori(0, (RW_T - 5) // 4) as i:
                for k in range(4):
                    fetch(4 + k, i, columns(w_in_v, i * 4 + (NA_T + 4 + k)))
            fetch(RW_T - 1, 0, columns(w_in_v, NA_T + RW_T - 1))
            sp.wait_ge(s["z_ready"], 2 * RW_CT)
            sp.wait_ge(s["y_added"], 2 * RW_CT - 2)
            with sp.Fori(0, NA_T // 4) as i:
                for k in range(4):
                    fetch(RW_T + k, i, columns(w_in_v, i * 4 + k))
            sp.wait_ge(s["y_rw_ready"], 1)
            for i in range(ROWS):
                half = GRID_W * (i % 2)
                for r in range(ROWS):
                    src = bass.AP(tensor=na_rpb.tensor, offset=(r - i + 7) * 31 + WIN - 1 - (GRID_W - 1),
                                  ap=[[1, GRID_W], [15 * 31, NA_HEADS], [1, GRID_W]])
                    dst = bias[half:half + GRID_W, :, i // 2, r * GRID_W:(r + 1) * GRID_W]
                    sp.dma_start(dst, src).then_inc(s["bias_in"], 16)
            sp.dma_start(flip, decay_d[:, RET_CT * 3 * P:]).then_inc(s["flip_in"], 16)
            sp.dma_start(decay.rearrange("p h x -> p (h x)"), decay_d[:, 0:RET_CT * 3 * P]).then_inc(s["decay_in"], 16)
            with sp.Fori(0, RET_T // 4) as i:
                for k in range(4):
                    fetch(RW_T + NA_T + k, i, columns(w_in_v, i * 4 + (RW_T + NA_T + k)))
            with sp.Fori(0, KT // 4) as i:
                for k in range(4):
                    fetch(OUT_FIRST + k, i, rows(w_out_v, i * 4 + k))
            sp.wait_ge(s["y_na_lo"], NA_T // 3)
            sp.wait_ge(s["y_lo"], RW_CT + RET_CT)
            sp.dma_start(x1, x[0].rearrange("(t p) d -> p t d", p=P)).then_inc(s["x_again"], 16)
            sp.dma_start(gains, post_mix_g.broadcast_to([P, D])).then_inc(s["gain_in"], 16)
            with sp.Fori(0, FF_T // 4) as i:
                for k in range(4):
                    fetch(UP_FIRST + k, i, columns(w_up_v, i * 4 + k))
            sp.wait_ge(s["x1_ready"], TT)
            sp.dma_start(gains, post_mlp_g.broadcast_to([P, D])).then_inc(s["gain_in"], 16)
            with sp.Fori(0, FF_T // 4) as i:
                for k in range(4):
                    fetch(DOWN_FIRST + k, i, rows(w_down_v, i * 4 + k))
            for t in range(TT):
                sp.wait_ge(s["o_ready"], t + 1)
                sp.dma_start(out[0, t * P:(t + 1) * P, :], o_sb[:, t]).then_inc(s["out_written"], 16)
            sp.wait_ge(s["out_written"], 16 * TT)

        @block.gpsimd
        def _(pool):
            step = [0]

            def nxt(ins):
                link(pool, step, "pool_step", ins)

            for _ in range(2):
                pool.sem_inc(s["relu_free"], 1)
            pool.wait_ge(s["h_lo"], KT)
            pool.dma_start(w2s, rw_w2.rearrange("l d r c -> (l d r) c")).then_inc(s["lora_in"], 16)
            pool.dma_start(a2s, rw_a2.rearrange("l d r c -> (l d r) c")).then_inc(s["lora_in"], 16)

            pool.wait_ge(s["lora_free"], 2 * RW_CT)
            pool.wait_ge(s["kk_ready"], 1)

            def tilde(t, p):
                def bonus_and_keys():
                    k_i = tile_of(zk, t)
                    for d in range(2):
                        stand(pool, "kd_scaled", 2 * t + (d + 1), "pool_passed")
                        pool.tensor_tensor(kd[:, d], kd[:, d], k_i, ALU.mult).then_inc(s["pool_step"], 1)
                        stand(pool, "tilde_ready", 2 * t + d, "pool_passed")
                        pool.tensor_tensor(bn, tile_of(kkn, t), tile_of(rate[:, d], t), ALU.mult).then_inc(
                            s["kb_ready"], 1)
                    pool.wait_ge(s["pool_step"], 2 * t + 2)
                    stand(pool, "vb_done", t, "pool_passed")
                    pool.tensor_tensor(tmp, kd[:, 0], kd[:, 1], ALU.add).then_inc(s["kd_summed"], 1)
                    pool.tensor_copy(vst, tile_of(zv, t)).then_inc(s["v_copied"], 1)
                return [bonus_and_keys]

            def products(t, p, first, second):
                run(second)

            def level(t, p, n, pieces, ahead):
                run(pieces)
                run(ahead)

            def chunk(b, q, n):
                def decay_state():
                    stand(pool, "s_ready", 3 * b + n, "pool_passed")
                    for d in range(2):
                        c = n if d == 0 else NC - 1 - n
                        last = pool.tensor_scalar(state_dec[:, d], state[:, d], ec[q][:, d, c:c + 1], None, ALU.mult)
                    last.then_inc(s["dec_ready"], 1)
                return [decay_state] if n in (1, 2) else []

            def gate_weights():
                pool.wait_ge(s["kb_ready"], 2 * RW_CT)
                pool.dma_start(g2s, rw_g2[0]).then_inc(s["g2_in"], 16)

            rw_tiles(pool, tilde, products, level, chunk, closing=[gate_weights])

            pool.wait_ge(s["bias_in"], 16 * ROWS * ROWS)
            win = const("win").unsqueeze(1).broadcast_to([P, TT * ROWS, GRID_W])
            for h in range(NA_HEADS):
                b_h = bias[:, h].rearrange("p t (r c) -> p (t r) c", c=GRID_W)
                pool.tensor_tensor(b_h, b_h, win, ALU.add).then_inc(s["bias_ready"], 1)

            pool.wait_ge(s["bank_free"], RW_PAIRS + NR_PAIRS)

            def copy_k(i):
                pool.tensor_copy(k_s, tile_of(znr, i + NA_T // 3)).then_inc(s["k_copied"], 1)

            def turn(i, attend, more=False):
                pool.wait_ge(s["y_lo"], RW_CT)
                stand(pool, "qk_ready", 2 * i, "pool_passed")
                for n in range(2):
                    pool.tensor_tensor(qk_cos[:, n], tile_of(znr, i + (NA_T + n * RET_CT)), const("cos"),
                                       ALU.mult).then_inc(s["rot_in"], 1)
                stand(pool, "vt_done", i, "pool_passed")
                pool.tensor_copy(v_cp, tile_of(znr, i + (NA_T + 2 * RET_CT))).then_inc(s["rot_in"], 1)
                if more:
                    stand(pool, "sc_done", i + 1, "pool_passed")
                    copy_k(i + 1)

            copy_k(0)
            mixers(pool, turn)

            with pool.Fori(0, UP_PAIRS // 2) as i:
                for k in range(2):
                    pool.wait_ge(s["bank_free"], i * 2 + (RW_PAIRS + NR_PAIRS + k + 1))
                    dst = u[:, ds(i * 4 + 2 * k, 2), :].rearrange("p a t -> p (a t)")
                    pool.tensor_tensor(dst, relu_t[:, k], relu_t[:, k], ALU.mult).then_inc(s["relu_free"], 1)

        @block.vector
        def _(dve):
            step = [0]

            def nxt(ins):
                link(dve, step, "dve_step", ins)

            dve.memset(zpad[:, 0], 0.0).then_inc(s["pad_free"], 1)
            dve.memset(zpad[:, 1], 0.0).then_inc(s["pad_free"], 1)
            for t in range(TT):
                dve.wait_ge(s["ss_done"], t + 1)
                dve.tensor_scalar(small[:, 2 + t:3 + t], small[:, t:t + 1], 1.0 / D, EPS, ALU.mult, ALU.add).then_inc(
                    s["ms_done"], 1)
                dve.wait_ge(s["sq_done"], t + 1)
                dve.reciprocal(small[:, 6 + t:7 + t], small[:, 4 + t:5 + t]).then_inc(s["rs_done"], 1)
                dve.wait_ge(s["rs_done"], t + 1)
                dve.tensor_scalar(x_n[:, t], x_in[:, t], small[:, 6 + t:7 + t], None, ALU.mult).then_inc(s["xn_ready"], 1)
            dve.wait_ge(s["vec_t"], 1)
            dve.tensor_copy(vec[:], bank[1][:, 0:VEC_N]).then_inc(s["vec_ready"], 1)
            dve.wait_ge(s["vec_ready"], 1)
            nxt(dve.tensor_scalar(small[:, 64:64 + RW_T], vect("mup"), -1.0, 1.0, ALU.mult, ALU.add))
            dve.tensor_tensor(small[:, 64:64 + RW_T], small[:, 64:64 + RW_T], vect("mun"), ALU.subtract).then_inc(
                s["coef_ready"], 1)
            dve.tensor_scalar(small[:, 32:32 + RW_CT], vect("ka"), -1.0, 1.0, ALU.mult, ALU.add)
            dve.tensor_scalar(small[:, 48:48 + RW_CT], vect("kk"), -1.0, None, ALU.mult).then_inc(s["coef_ready"], 1)

            def split_h(gain):
                for k in range(KT):
                    dve.wait_ge(s["h_hi"], gain[1] + k + 1)
                    dve.scalar_tensor_tensor(act_lo[:, k], bank[2 + k % 6][:, 0:T], vect(gain[0])[:, k:k + 1],
                                             act_hi[:, k].bitcast(F32), ALU.mult, ALU.subtract).then_inc(s["h_lo"], 1)

            split_h(("g1", 0))

            def lo(c, i):
                dve.wait_ge(s["hi_done"], 4 * i + c + 1)
                if not (isinstance(i, int) and 4 * i + c < 2):
                    dve.wait_ge(s["gemm_done"], 4 * i + c - 1)
                dve.tensor_tensor(w_lo[:, c % 2], raw[:, c % RAW], w_hi[:, c % 2].bitcast(F32),
                                  ALU.subtract).then_inc(s["lo_done"], 1)

            def shift(k, i):
                n = 2 if not (isinstance(i, int) and 2 * i + k == RW_PAIRS - 1) else 1
                dve.wait_ge(s["bank_free"], 2 * i + k + 1)
                for mu, at in (("mup", 0), ("mun", 2)):
                    for j in range(n):
                        ct = 4 * i + 2 * k + j
                        z = zs[:, ds(ct, 1), :].rearrange("p a t -> p (a t)")
                        last = dve.scalar_tensor_tensor(z, zpad[:, k % 2, j, at:at + T], vect(mu)[:, ds(ct, 1)], z,
                                                        ALU.mult, ALU.add)
                        if at == 0:
                            last.then_inc(s["zs_ready"], 1)
                    if at == 0:
                        dve.wait_ge(s["zs_ready"], 2 * (2 * i + k) + n)
                last.then_inc(s["pad_free"], 1)

            stream(dve, 0, RW_T, lo, shift)

            dve.wait_ge(s["pad_free"], 2 + RW_PAIRS)
            for t in range(RW_CT):
                last = dve.tensor_scalar(kkn[:, t], zk[:, t], small[:, 48 + t:49 + t], None, ALU.mult)
            last.then_inc(s["kk_raw"], 1)
            dve.wait_ge(s["kk_raw"], 1)
            dve.tensor_tensor(kk_sq, kkn, kkn, ALU.mult).then_inc(s["kk_sqd"], 1)
            for n in range(3):
                third = kk_ss[:, 2 * n:2 * n + 2]
                dve.wait_ge(s["kk_root"], n + 1)
                nxt(dve.tensor_scalar(third, third, 1e-12, None, ALU.max))
                nxt(dve.reciprocal(third, third))
                last = dve.tensor_tensor(kkn[:, 2 * n:2 * n + 2], kkn[:, 2 * n:2 * n + 2], third, ALU.mult)
            last.then_inc(s["kk_ready"], 1)
            dve.wait_ge(s["kk_ready"], 1)
            dve.wait_ge(s["lora_free"], 2 * RW_CT)

            def transposed(dst, src, d, name):
                half = slice(d * NC, (d + 1) * NC)
                dve.transpose(dst[:, half].rearrange("p n t -> p (n t)"), src[:, half].rearrange("p n t -> p (n t)")).then_inc(
                    s[name], 1)

            def tilde(t, p):
                kk_i, r_i = tile_of(kkn, t), tile_of(zr, t)

                def sums(d):
                    s_i = tile_of(sig_w[:, d], t)
                    dve.wait_ge(s["exp_ready"], 6 * t + 3 * d)
                    dve.tensor_tensor_scan(cs, keep, s_i, 0.0, ALU.mult, ALU.add).then_inc(s["cum_ready"], 1)
                    dve.wait_ge(s["cum_ready"], 5 * t + (2 * d + 1))
                    if d == 0:
                        dve.tensor_tensor(ce, cs, s_i, ALU.subtract).then_inc(s["cum_ready"], 1)
                    else:
                        dve.tensor_tensor(chunks(ce), chunks(cs)[:, :, C - 1:C].broadcast_to([P, NC, C]), chunks(cs),
                                          ALU.subtract).then_inc(s["cum_ready"], 1)
                        dve.wait_ge(s["cum_ready"], 5 * t + 4)
                        dve.tensor_tensor(cs, ce, s_i, ALU.add).then_inc(s["cum_ready"], 1)

                def queries(d):
                    dve.wait_ge(s["exp_ready"], 6 * t + (3 * d + 3))
                    last_t = C - 1 if d == 0 else 0
                    dve.tensor_copy(ec[p][:, d], chunks(e_inc)[:, :, last_t])
                    a_ = ar[p][:, d]
                    dve.tensor_tensor(a_[:, :, 0:C], chunks(kk_i), chunks(e_exc), ALU.mult)
                    dve.tensor_tensor(a_[:, :, C:2 * C], chunks(r_i), chunks(e_inc), ALU.mult)

                def keys(d):
                    dve.wait_ge(s["kb_ready"], 2 * t + (d + 1))
                    k_ = bk[:, d]
                    dve.scalar_tensor_tensor(k_[:, :, 0:C], chunks(bn), -1.0, chunks(e_inv), ALU.mult, ALU.mult)
                    dve.tensor_tensor(k_[:, :, C:2 * C], chunks(kd[:, d]), chunks(e_inv), ALU.mult).then_inc(
                        s["tilde_ready"], 1)

                return [lambda d=d, part=part: part(d) for d in range(2) for part in (sums, queries, keys)]

            def products(t, p, first, second):
                r_i, v_i = tile_of(zr, t), tile_of(zv, t)
                dve.wait_ge(s["z_ready"], 2 * t)
                dve.wait_ge(s["kd_summed"], t + 1)
                dve.scalar_tensor_tensor(tmp, tmp, vect("rk")[:, ds(t, 1)], r_i, ALU.mult, ALU.mult).then_inc(
                    s["bonus_in"], 1)
                for d in range(2):
                    dve.wait_ge(s["bm_done"], 2 * t + (d + 1))
                    for e in range(2):
                        dve.tensor_tensor(bms[p][:, (2 * d + e) * NC:(2 * d + e + 1) * NC],
                                          bank[4 + 2 * d + e].rearrange("p (c t) -> p c t", t=P),
                                          bm_mask[:, d, e].unsqueeze(1).broadcast_to([P, NC, P]),
                                          ALU.mult).then_inc(s["bm_ready"], 1)
                    run(first[d:d + 1])
                for d in range(2):
                    dve.wait_ge(s["bm_ready"], 4 * t + (2 * d + 2))
                    for e in range(2):
                        h = slice(e * C, e * C + C)
                        last = dve.tensor_tensor(p1s[h, d * NC:(d + 1) * NC],
                                                 bms[p][h, (2 * d + e) * NC:(2 * d + e + 1) * NC, h],
                                                 off[h, 0].unsqueeze(1).broadcast_to([C, NC, C]), ALU.mult)
                    last.then_inc(s["p0_ready"], 1)
                for d in range(2):
                    dve.wait_ge(s["p0_ready"], 2 * t + (d + 1))
                    dve.tensor_tensor(zt[:, d * NC:(d + 1) * NC], p1s[:, d * NC:(d + 1) * NC],
                                      eye.unsqueeze(1).broadcast_to([P, NC, C]), ALU.add).then_inc(s["zt_ready"], 1)
                    dve.wait_ge(s["zt_ready"], 10 * t + (d + 1))
                    transposed(zd, zt, d, "zd_ready")
                run(first[2:])
                run(second[:2])
                dve.wait_ge(s["vb_done"], t + 1)
                uv_d = uv[p].rearrange("p (d c) e v -> p d c e v", d=2)
                v_ps = bank[2][:, 0:T].rearrange("p (c v) -> p c v", v=C)
                for d in range(2):
                    dve.tensor_copy(uv_d[C:P, d, :, 0, :], v_ps[C:P])
                    dve.tensor_copy(uv_d[0:C, d, :, 1, :], v_ps[0:C]).then_inc(s["vb_ready"], 1)
                dve.tensor_tensor(r_i, bank[2][:, T:2 * T], v_i, ALU.mult).then_inc(s["vb_ready"], 1)
                run(second[2:])

            def level(t, p, n, pieces, ahead):
                for d in range(2):
                    half = slice(d * NC, (d + 1) * NC)
                    run(pieces[d:d + 1])
                    dve.wait_ge(s["p1_done"], 10 * t + (2 * n + d + 1))
                    dve.tensor_tensor(p1s[:, half], bank[4 + d][:, 0:T].rearrange("p (n t) -> p n t", t=C),
                                      off[:, n + 1].unsqueeze(1).broadcast_to([P, NC, C]),
                                      ALU.mult).then_inc(s["p1_ready"], 1)
                run(ahead[:1])
                for d in range(2):
                    half = slice(d * NC, (d + 1) * NC)
                    q_ps = bank[4 + d][:, T:2 * T].rearrange("p (n t) -> p n t", t=C)
                    dve.wait_ge(s["q_done"], 10 * t + (2 * n + d + 1))
                    if n < len(LEVELS) - 1:
                        dve.tensor_tensor(zd[:, half], q_ps, zd[:, half], ALU.add).then_inc(s["zd_ready"], 1)
                        dve.wait_ge(s["zd_ready"], 10 * t + (2 * (n + 1) + d + 1))
                        transposed(zt, zd, d, "zt_ready")
                    else:
                        dve.tensor_tensor(az[p][:, half], q_ps, zt[:, half], ALU.add).then_inc(s["z_ready"], 1)
                    run(pieces[2 + d:3 + d])
                run(ahead[1:])

            def chunk(b, q, n):
                gy = [bank[e][:, 0:2 * C].rearrange("p (d v) -> p d v", d=2) for e in range(2)]
                both = slice(n, 2 * NC - n, 2 * NC - 1 - 2 * n)

                def g():
                    dve.wait_ge(s["gy_done"], 4 * b + (n + 1))
                    dve.tensor_copy(gs[C:P], gy[1][C:P]).then_inc(s["g_high"], 1)

                def u():
                    dve.wait_ge(s["u_done"], 4 * b + (n + 1))
                    dve.tensor_copy(uv[q][C:P, both, 1], bank[3][C:P, 0:2 * C].rearrange("p (d v) -> p d v", d=2)).then_inc(
                        s["u_high"], 1)

                def new_state():
                    if n == NC - 1:
                        return
                    dve.wait_ge(s["s_done"], 3 * b + (n + 1))
                    if n:
                        dve.wait_ge(s["dec_ready"], 2 * b + n)
                    for d in range(2):
                        c = n if d == 0 else NC - 1 - n
                        new = bank[3][:, d * C:(d + 1) * C]
                        if n == 0:
                            last = dve.tensor_scalar(state[:, d], new, ec[q][:, d, c:c + 1], None, ALU.mult)
                        else:
                            last = dve.scalar_tensor_tensor(state[:, d], new, ec[q][:, d, c:c + 1], state_dec[:, d],
                                                            ALU.mult, ALU.add)
                    last.then_inc(s["s_ready"], 1)

                def add_y():
                    if n < 2:
                        return
                    dve.wait_ge(s["y_done"], 4 * b + (n + 1))
                    dve.wait_ge(s["y_copied"], 2 * b + 2)
                    y_i = chunks(tile_of(zk, b))
                    order = slice(NC - 1 - n, n + 1, 2 * n - NC + 1)
                    dve.tensor_tensor(y_i[0:C, order], gy[1][0:C], y_i[0:C, order], ALU.add)
                    dve.tensor_tensor(y_i[C:P, order], gy[0][C:P], y_i[C:P, order], ALU.add).then_inc(s["y_added"], 1)

                return g, u, new_state, add_y

            def norm_steps(tiles, count):
                cols = slice(tiles.start * NC, tiles.stop * NC)
                y = zk.rearrange("p i (c v) -> p (i c) v", v=C)[:, cols]
                mean, rstd = small[:, 96:96 + N][:, cols], small[:, 128:128 + N][:, cols]
                sq = ysq[:, cols]
                wide = [P, (tiles.stop - tiles.start) * NC, C]

                def sums():
                    dve.wait_ge(s["y_added"], 2 * tiles.stop)
                    nxt(dve.tensor_reduce(mean, y, AX_X, ALU.add))

                def centre():
                    nxt(dve.tensor_scalar(mean, mean, -1.0 / C, None, ALU.mult))
                    nxt(dve.tensor_tensor(y, y, mean.unsqueeze(2).broadcast_to(wide), ALU.add))

                def squares():
                    nxt(dve.tensor_tensor(sq, y, y, ALU.mult))

                def variance():
                    nxt(dve.tensor_reduce(rstd, sq, AX_X, ALU.add))

                def mean_square():
                    dve.tensor_scalar(rstd, rstd, 1.0 / C, LNX_EPS, ALU.mult, ALU.add).then_inc(s["ln_ms"], 1)

                def scale():
                    dve.wait_ge(s["ln_root"], count)
                    nxt(dve.reciprocal(rstd, rstd))
                    dve.tensor_tensor(y, y, rstd.unsqueeze(2).broadcast_to(wide), ALU.mult).then_inc(s["ln_ready"], 1)

                return [sums, centre, squares, variance, mean_square, scale]

            N = RW_CT * NC
            rw_tiles(dve, tilde, products, level, chunk, closing=norm_steps(slice(0, RW_CT - 1), 1))
            run(norm_steps(slice(RW_CT - 1, RW_CT), 2))
            lo(RW_T, 0)
            lo(RW_T + 1, 0)
            for t in range(RW_CT):
                dve.wait_ge(s["yt_done"], t // 2 + 1)
                nxt(dve.tensor_scalar(y_rw[:, t], yt_bank[t // 2][:, (t % 2) * T:(t % 2 + 1) * T],
                                      vect("lg")[:, t:t + 1], vect("lb")[:, t:t + 1], ALU.mult, ALU.add))
            nxt(dve.tensor_tensor(y_rw, y_rw, zr, ALU.add))
            dve.wait_ge(s["gate_ready"], 3)
            dve.tensor_tensor(y_rw, y_rw, gate, ALU.mult).then_inc(s["y_rw_ready"], 1)

            stream(dve, RW_T, NA_T + RET_T, lo, begun=2)

            def scale_q(i):
                dve.wait_ge(s["sc_done"], i)
                dve.tensor_scalar(q_s, tile_of(znr, i), NA_HD ** -0.5, None, ALU.mult).then_inc(s["q_ready"], 1)

            dve.wait_ge(s["bank_free"], RW_PAIRS + NR_PAIRS)
            scale_q(0)
            for k in range(RW_CT):
                dve.wait_ge(s["y_rw_hi"], k + 1)
                dve.tensor_tensor(act_lo[:, NA_T // 3 + k], y_rw[:, k], act_hi[:, NA_T // 3 + k].bitcast(F32),
                                  ALU.subtract).then_inc(s["y_lo"], 1)
            dve.wait_ge(s["silu_sig"], 1)
            g_all = znr[:, NA_T + 3 * RET_CT:NA_T + 4 * RET_CT]
            dve.tensor_tensor(g_all, g_all, silu_s, ALU.mult).then_inc(s["silu_ready"], 1)
            base = step[0]

            def maxima(i):
                dve.wait_ge(s["sc_done"], i + 1)
                top = small[:, 160:164]
                dve.tensor_reduce(top.rearrange("p (e t) -> p e t", e=2), scores, AX_X, ALU.max).then_inc(
                    s["dve_step"], 1)
                dve.wait_ge(s["dve_step"], i + (base + 1))
                dve.tensor_scalar(top, top, -1.0, None, ALU.mult).then_inc(s["mx_ready"], 1)

            def turn(i, attend, more=False):
                if more:
                    scale_q(i + 1)
                dve.wait_ge(s["rot_done"], i + 1)
                dve.wait_ge(s["rot_in"], 3 * i + 2)
                dve.wait_ge(s["st_done"], i)
                sin2 = const("sin").unsqueeze(1).broadcast_to([P, 2, T])
                dve.tensor_tensor(qk, bank[0].rearrange("p (a t) -> p a t", a=2), sin2, ALU.mult).then_inc(
                    s["qk_ready"], 1)
                dve.wait_ge(s["qk_ready"], 2 * i + 1)
                dve.tensor_tensor(qk, qk, qk_cos, ALU.add).then_inc(s["qk_ready"], 1)
                if not attend:
                    lo(OUT_FIRST + i - NA_T // 3, 0)
                if attend:
                    dve.wait_ge(s["p_ready"], 4 * i + 4)
                    dve.reciprocal(small[:, 168:172], small[:, 164:168]).then_inc(s["rinv_ready"], 1)
                    for e in range(2):
                        dve.wait_ge(s["pt_done"], 2 * i + (e + 1))
                        dve.tensor_copy(pts[:, e], bank[4 + e].rearrange("p (a b q) -> p a b q", a=2, b=2)).then_inc(
                            s["pt_ready"], 1)
                dve.wait_ge(s["decay_in"], 16)
                dve.wait_ge(s["st_done"], i + 1)
                dve.wait_ge(s["ro_done"], i)
                dec_i = decay[:, ds(i, 1), :].rearrange("p a x -> p (a x)")
                for m in range(TT):
                    last = dve.tensor_tensor(sts[:, m], bank[1][:, m * T:(m + 1) * T],
                                             dec_i[:, P - m * P:P - m * P + T], ALU.mult)
                last.then_inc(s["st_ready"], 1)
                if more:
                    maxima(i + 1)
                if attend:
                    dve.wait_ge(s["y_na_hi"], i + 1)
                    dve.tensor_tensor(tile_of(act_lo, i), bank[6][:, T:2 * T], tile_of(act_hi, i).bitcast(F32),
                                      ALU.subtract).then_inc(s["y_na_lo"], 1)

            maxima(0)
            mixers(dve, turn)
            step[0] = base + NA_T // 3
            ss = small[:, 176:176 + RET_CT * TT]
            dve.wait_ge(s["ro_ready"], 3 * RET_CT)
            dve.tensor_scalar(ss, ss, 1.0 / P, EPS, ALU.mult, ALU.add).then_inc(s["ret_ms"], 1)
            dve.wait_ge(s["ret_root"], 1)
            dve.reciprocal(ss, ss).then_inc(s["ret_rs"], 1)
            dve.wait_ge(s["ret_rs"], 1)
            o_flat = o_all.rearrange("p h t v -> p (h t) v")
            dve.tensor_tensor(o_flat, o_flat, ss.unsqueeze(2).broadcast_to([P, RET_CT * TT, P]), ALU.mult).then_inc(
                s["on_ready"], 1)
            dve.wait_ge(s["silu_ready"], 1)
            for h in range(RET_CT):
                dve.wait_ge(s["ont_done"], h + 1)
                dve.tensor_tensor(y_f[:, h], bank[2 + h][:, 0:T], znr[:, NA_T + 3 * RET_CT + h],
                                  ALU.mult).then_inc(s["yf_ready"], 1)
            for h in range(RET_CT):
                k = (NA_W + RW_W) // P + h
                dve.wait_ge(s["y_ret_hi"], h + 1)
                dve.tensor_tensor(act_lo[:, k], y_f[:, h], act_hi[:, k].bitcast(F32),
                                  ALU.subtract).then_inc(s["y_lo"], 1)

            stream(dve, OUT_FIRST, KT, lo, begun=2)

            lo(UP_FIRST, 0)
            rs, h2 = small[:, 192:194], small[:, 208:210]

            def mean_of(part, name, count):
                dve.wait_ge(s[name], count)
                dve.tensor_scalar(part, part, 1.0 / D, EPS, ALU.mult, ALU.add).then_inc(s["yms_done"], 1)

            def inverse_of(part, count):
                dve.wait_ge(s["yroot_done"], count)
                dve.reciprocal(part, part).then_inc(s["yrs_done"], 1)
                dve.wait_ge(s["yrs_done"], count)

            def add_normed(dst, to, stage, name):
                mean_of(rs[:, 0:1], "yss_done", TT * (stage // 2) + 1)
                for t in range(TT):
                    inverse_of(rs[:, t:t + 1], TT * stage + t + 1)
                    y_t = psum[:, 4 * t:4 * t + 4].rearrange("p b n -> p (b n)")
                    nxt(dve.scalar_tensor_tensor(to[:, t], y_t, rs[:, t:t + 1], gains, ALU.mult, ALU.mult))
                    if t == 0:
                        mean_of(rs[:, 1:2], "yss_done", TT * (stage // 2) + 2)
                    dve.tensor_tensor(dst[:, t], x1[:, t], to[:, t], ALU.add).then_inc(s[name], 1)

            dve.wait_ge(s["x_again"], 16)
            dve.wait_ge(s["gain_in"], 16)
            add_normed(x1, y_sb, 0, "x1_ready")
            for t in range(TT):
                mean_of(h2[:, t:t + 1], "hss_done", t + 1)
                inverse_of(h2[:, t:t + 1], TT + t + 1)
                dve.tensor_scalar(y_sb[:, t], x1[:, t], h2[:, t:t + 1], None, ALU.mult).then_inc(s["xn_ready"], 1)
            split_h(("g2", KT))

            stream(dve, UP_FIRST, FF_T, lo, begun=1)

            def lo_down(c, i):
                m = c - DOWN_FIRST
                dve.wait_ge(s["uhi_done"], 4 * i + m + 1)
                dve.tensor_tensor(u_lo[:, c % U_RING], tile_of(u, 4 * i + m), u_hi[:, c % U_RING].bitcast(F32),
                                  ALU.subtract).then_inc(s["ulo_done"], 1)
                lo(c, i)

            stream(dve, DOWN_FIRST, FF_T, lo_down)

            dve.wait_ge(s["gain_in"], 32)
            add_normed(o_sb, o_sb, 2, "o_ready")

        @block.scalar
        def _(act):
            for t in range(TT):
                act.wait_ge(s[("x_in", "x_in_next")[t]], 16)
                act.activation(x_n[:, t], x_in[:, t], ACT.Square, accum_out=small[:, t:t + 1]).then_inc(s["ss_done"], 1)
                act.wait_ge(s["ms_done"], t + 1)
                act.activation(small[:, 4 + t:5 + t], small[:, 2 + t:3 + t], ACT.Sqrt).then_inc(s["sq_done"], 1)
            act.wait_ge(s["vec_ready"], 1)

            def split_h(gain):
                for k in range(KT):
                    act.wait_ge(s["xt_done"], gain[1] + k + 1)
                    act.activation(act_hi[:, k], bank[2 + k % 6][:, 0:T], ACT.Copy,
                                   scale=vect(gain[0])[:, k:k + 1]).then_inc(s["h_hi"], 1)

            def hi(c, i):
                raw_landed(act, c, i)
                if not (isinstance(i, int) and 4 * i + c < 2):
                    act.wait_ge(s["gemm_done"], 4 * i + c - 1)
                act.activation(w_hi[:, c % 2], raw[:, c % RAW], ACT.Copy).then_inc(s["hi_done"], 1)

            split_h(("g1", 0))
            act.wait_ge(s["coef_ready"], 2)


            def to_zs(k, i):
                n = 2 if not (isinstance(i, int) and 2 * i + k == RW_PAIRS - 1) else 1
                act.wait_ge(s["gemm_done"], 4 * i + 2 * k + n)
                act.wait_ge(s["pad_free"], 2 * i + k + 1)
                ps = bank[k % 2][:, 0:n * T]
                act.activation(zpad[:, k % 2, 0:n, 1:T + 1], ps.rearrange("p (a t) -> p a t", a=n), ACT.Copy)
                for j in range(n):
                    ct = 4 * i + 2 * k + j
                    last = act.activation(zs[:, ds(ct, 1), :].rearrange("p a t -> p (a t)"), ps[:, j * T:(j + 1) * T],
                                          ACT.Copy, scale=small[:, ds(ct + 64, 1)])
                last.then_inc(s["bank_free"], 1)

            stream(act, 0, RW_T, hi, to_zs)

            act.wait_ge(s["pad_free"], 2 + RW_PAIRS)
            act.activation(z_wd, z_wd, ACT.Tanh).then_inc(s["wd_ready"], 1)
            act.activation(z_gd, z_gd, ACT.Sigmoid)
            for n, (dst, bias_name) in enumerate(((sig_w, "w0"), (rate, "a0"))):
                for d in range(2):
                    for t in range(RW_CT):
                        f = (n * 2 + d) * (RW_CT // 2) + t // 2
                        if f == 3 and t % 2 == 0:
                            for k in range(3):
                                act.wait_ge(s["kk_summed"], k + 1)
                                act.activation(kk_ss[:, 2 * k:2 * k + 2].rearrange("p a t -> p (a t)"), bank[5 + k],
                                               ACT.Sqrt).then_inc(s["kk_root"], 1)
                        if t % 2 == 0:
                            act.wait_ge(s["lora_done"], f + 1)
                        last = act.activation(dst[:, d, t], bank[2 + f % 6][:, (t % 2) * T:(t % 2 + 1) * T], ACT.Sigmoid,
                                              bias=vect(bias_name)[:, d * RW_CT + t:d * RW_CT + t + 1])
                        if t % 2:
                            last.then_inc(s["lora_free"], 1)
            act.wait_ge(s["lora_free"], 2 * RW_CT)

            act.wait_ge(s["kk_ready"], 1)

            def tilde(t, p):
                def decays(d):
                    if d == 0:
                        stand(act, "kd_summed", t, "act_passed")
                        stand(act, "tilde_ready", 2 * t, "act_passed")
                        for e in range(2):
                            act.activation(kd[:, e], tile_of(rate[:, e], t), ACT.Identity, bias=small[:, ds(t + 32, 1)],
                                           scale=vect("ka")[:, ds(t, 1)]).then_inc(s["kd_scaled"], 1)
                    act.wait_ge(s["cum_ready"], 5 * t + (3 * d + 2))
                    if d == 1:
                        act.wait_ge(s["tilde_ready"], 2 * t + 1)
                    act.activation(e_inc, cs, ACT.Exp, scale=-DECAY).then_inc(s["exp_ready"], 1)
                    act.activation(e_exc, ce, ACT.Exp, scale=-DECAY).then_inc(s["exp_ready"], 1)
                    act.activation(e_inv, cs, ACT.Exp, scale=DECAY).then_inc(s["exp_ready"], 1)

                def again(d):
                    act.wait_ge(s["tilde_ready"], 2 * t + (d + 1))
                    for v in (ar[p][:, d], bk[:, d]):
                        last = act.activation(v[C:P, :, 2 * C:3 * C], v[C:P, :, 0:C], ACT.Copy)
                    last.then_inc(s["again_ready"], 1)

                return [lambda: decays(0), lambda: None, lambda: again(0), lambda: decays(1), lambda: None,
                        lambda: again(1)]

            def products(t, p, first, second):
                run(first[:2])
                act.wait_ge(s["bkt_done"], t + 1)
                for e in range(2):
                    act.activation(bkt[p][:, e], bank[4 + e].rearrange("p (n k) -> p n k", k=C), ACT.Copy).then_inc(
                        s["bkt_ready"], 1)
                run(first[2:])
                run(second)

            def level(t, p, n, pieces, ahead):
                run(pieces)
                run(ahead)

            def chunk(b, q, n):
                gy = [bank[e][:, 0:2 * C].rearrange("p (d v) -> p d v", d=2) for e in range(2)]
                both = slice(n, 2 * NC - n, 2 * NC - 1 - 2 * n)

                def g():
                    act.wait_ge(s["gy_done"], 4 * b + (n + 1))
                    act.activation(gs[0:C], gy[0][0:C], ACT.Copy).then_inc(s["g_low"], 1)

                def u():
                    act.wait_ge(s["u_done"], 4 * b + (n + 1))
                    act.activation(uv[q][0:C, both, 0], bank[3][0:C, 0:2 * C].rearrange("p (d v) -> p d v", d=2),
                                   ACT.Copy).then_inc(s["u_low"], 1)

                def y():
                    if n >= 2:
                        return
                    act.wait_ge(s["y_done"], 4 * b + (n + 1))
                    y_i = chunks(tile_of(zk, b))
                    order = slice(n, NC - n, NC - 1 - 2 * n)
                    act.activation(y_i[0:C, order], gy[1][0:C], ACT.Copy)
                    act.activation(y_i[C:P, order], gy[0][C:P], ACT.Copy).then_inc(s["y_copied"], 1)

                return g, u, y

            rstd = small[:, 128:128 + RW_CT * NC]

            def root(tiles, count):
                act.wait_ge(s["ln_ms"], count)
                part = rstd[:, tiles.start * NC:tiles.stop * NC]
                act.activation(part, part, ACT.Sqrt).then_inc(s["ln_root"], 1)

            def take_gate(n):
                act.wait_ge(s["gate_done"], n + 1)
                act.activation(gate[:, 2 * n:2 * n + 2].rearrange("p a t -> p (a t)"), gate_bank[n], ACT.Copy).then_inc(
                    s["gate_ready"], 1)

            rw_tiles(act, tilde, products, level, chunk,
                     closing=[lambda: None] * 5 + [lambda: root(slice(0, RW_CT - 1), 1)],
                     tail=[lambda n=n: take_gate(n) for n in range(3)])
            root(slice(RW_CT - 1, RW_CT), 2)
            hi(RW_T, 0)
            hi(RW_T + 1, 0)

            def to_znr(k, i):
                act.wait_ge(s["y_rw_ready"], 1)
                act.wait_ge(s["gemm_done"], 4 * i + (RW_T + 2 * k + 2))
                act.activation(znr[:, ds(4 * i + 2 * k, 2), :].rearrange("p a t -> p (a t)"), bank[(k + RW_PAIRS) % 2],
                               ACT.Copy).then_inc(s["bank_free"], 1)

            stream(act, RW_T, NA_T + RET_T, hi, to_znr, begun=2)

            act.wait_ge(s["bank_free"], RW_PAIRS + NR_PAIRS)
            for t in range(TT):
                act.wait_ge(s["vna_done"], t + 1)
                act.activation(v_na[:, t], bank[4 + t], ACT.Copy).then_inc(s["vna_ready"], 1)
            act.activation(silu_s, znr[:, NA_T + 3 * RET_CT:NA_T + 4 * RET_CT], ACT.Sigmoid).then_inc(s["silu_sig"], 1)
            for t in range(RW_CT):
                act.activation(act_hi[:, NA_T // 3 + t], y_rw[:, t], ACT.Copy).then_inc(s["y_rw_hi"], 1)
            act.wait_ge(s["silu_ready"], 1)

            def turn(i, attend, more=False):
                if attend:
                    act.wait_ge(s["mx_ready"], i + 1)
                    for e in range(2):
                        for t in range(TT):
                            n = 2 * e + t
                            act.activation(sx[:, e, t], scores[:, e, t], ACT.Exp, bias=small[:, 160 + n:161 + n],
                                           accum_out=small[:, 164 + n:165 + n]).then_inc(s["p_ready"], 1)
                act.wait_ge(s["vt_done"], i + 1)
                act.wait_ge(s["ro_done"], i)
                act.activation(v_tok, bank[7][:, 0:T].rearrange("p (t v) -> p t v", t=TT), ACT.Copy).then_inc(
                    s["v_tok_ready"], 1)
                if not attend:
                    hi(OUT_FIRST + i - NA_T // 3, 0)
                if attend:
                    act.wait_ge(s["rinv_ready"], i + 1)
                    act.wait_ge(s["o_done"], i + 1)
                    for e in range(2):
                        for t in range(TT):
                            n = 2 * e + t
                            act.activation(yq[:, t, e * C:(e + 1) * C], bank[6][:, (2 * t + e) * C:(2 * t + e + 1) * C],
                                           ACT.Copy, scale=small[:, 168 + n:169 + n]).then_inc(s["yq_ready"], 1)
                act.wait_ge(s["ro_done"], i + 1)
                act.wait_ge(s["ro_ready"], 3 * i)
                act.activation(o_all[:, ds(i, 1)].rearrange("p a t v -> p (a t v)"), bank[7][:, T:2 * T],
                               ACT.Copy).then_inc(s["ro_ready"], 1)
                for t in range(TT):
                    act.activation(junk[:, t], bank[7][:, T + t * P:T + (t + 1) * P], ACT.Square,
                                   accum_out=small[:, ds(2 * i + (176 + t), 1)]).then_inc(s["ro_ready"], 1)
                if attend:
                    act.wait_ge(s["yqt_done"], i + 1)
                    act.activation(tile_of(act_hi, i), bank[6][:, T:2 * T], ACT.Copy).then_inc(s["y_na_hi"], 1)

            mixers(act, turn)
            ss = small[:, 176:176 + RET_CT * TT]
            act.wait_ge(s["ret_ms"], 1)
            act.activation(ss, ss, ACT.Sqrt).then_inc(s["ret_root"], 1)
            for h in range(RET_CT):
                act.wait_ge(s["yf_ready"], h + 1)
                act.activation(act_hi[:, (NA_W + RW_W) // P + h], y_f[:, h], ACT.Copy).then_inc(s["y_ret_hi"], 1)

            stream(act, OUT_FIRST, KT, hi, begun=2)

            def out_sums(k, stage):
                for t in range(TT):
                    if t == 0:
                        act.wait_ge(s["half_done"], stage // 2 + 1)
                    else:
                        act.wait_ge(s["gemm_done"], k)
                    act.activation(y_sb[:, t], psum[:, 4 * t:4 * t + 4].rearrange("p b n -> p (b n)"), ACT.Square,
                                   accum_out=small[:, 192 + t:193 + t]).then_inc(s["yss_done"], 1)
                    root_of(small[:, 192 + t:193 + t], TT * stage + t + 1)

            def root_of(part, count):
                act.wait_ge(s["yms_done"], count)
                act.activation(part, part, ACT.Sqrt).then_inc(s["yroot_done"], 1)

            hi(UP_FIRST, 0)
            out_sums(UP_FIRST, 0)
            hi(UP_FIRST + 1, 0)
            for t in range(TT):
                act.wait_ge(s["x1_ready"], t + 1)
                act.activation(y_sb[:, t], x1[:, t], ACT.Square, accum_out=small[:, 208 + t:209 + t]).then_inc(
                    s["hss_done"], 1)
                root_of(small[:, 208 + t:209 + t], TT + t + 1)
            split_h(("g2", KT))

            def to_relu(k, i):
                act.wait_ge(s["gemm_done"], 4 * i + (UP_FIRST + 2 * k + 2))
                act.wait_ge(s["relu_free"], 2 * i + k + 1)
                act.activation(relu_t[:, k % 2], bank[(k + RW_PAIRS + NR_PAIRS) % 2], ACT.Relu).then_inc(
                    s["bank_free"], 1)

            

            def hi_down(c, i):
                m = c - DOWN_FIRST
                act.wait_ge(s["gemm_done"], 4 * i + c - (U_RING - 1))
                act.activation(u_hi[:, c % U_RING], tile_of(u, 4 * i + m), ACT.Copy).then_inc(s["uhi_done"], 1)
                hi(c, i)

            stream(act, UP_FIRST, FF_T, hi, to_relu, begun=2, then=lambda: hi_down(DOWN_FIRST, 0))
            act.wait_ge(s["relu_free"], 2 + UP_PAIRS)
            stream(act, DOWN_FIRST, FF_T, hi_down, begun=1)
            out_sums(DOWN_FIRST + FF_T, 2)

        @block.tensor
        def _(pe):
            def turned(src, first):
                for k in range(KT):
                    if k >= 6:
                        pe.wait_ge(s["h_lo"], first + k - 5)
                    for t in range(TT):
                        if k == 0:
                            pe.wait_ge(s["xn_ready"], TT * (first // KT) + t + 1)
                        last = pe.transpose(bank[2 + k % 6][:, t * P:(t + 1) * P], src[:, t, k * P:(k + 1) * P], ident)
                    last.then_inc(s["xt_done"], 1)

            pe.wait_ge(s["consts_in"], 16)
            pe.wait_ge(s["vec_in"], 16 * len(VEC))
            pe.transpose(bank[1][:, 0:VEC_N], vstage[0:VEC_N, :], ident[0:VEC_N, 0:VEC_N]).then_inc(s["vec_t"], 1)
            turned(x_n, 0)
            pe.wait_ge(s["h_lo"], KT)
            pe.wait_ge(s["vec_ready"], 1)

            def split_ready(c, i):
                pe.wait_ge(s["hi_done"], 4 * i + c + 1)
                pe.wait_ge(s["lo_done"], 4 * i + c + 1)

            def columns(c, i, k, pairs, wait=True):
                split_ready(c, i)
                q = pairs + k // 2
                if k % 2 == 0 and wait:
                    pe.wait_ge(s["bank_free"], 2 * i + q - 1)
                dst = bank[q % 2][:, (k % 2) * T:(k % 2 + 1) * T]
                for kt in range(KT):
                    wh = w_hi[:, c % 2, kt * P:(kt + 1) * P]
                    pe.matmul(dst, wh, act_hi[:, kt], start=kt == 0, stop=False)
                    pe.matmul(dst, wh, act_lo[:, kt], start=False, stop=False)
                    last = pe.matmul(dst, w_lo[:, c % 2, kt * P:(kt + 1) * P], act_hi[:, kt], start=False,
                                     stop=kt == KT - 1)
                last.then_inc(s["gemm_done"], 1)

            for k in range(4):
                columns(k, 0, k, 0, wait=False)
            with pe.Fori(0, (RW_T - 5) // 4) as i:
                for k in range(4):
                    columns(4 + k, i, 4 + k, 0)
            columns(RW_T - 1, 0, RW_T - 1, 0)

            pe.wait_ge(s["wd_ready"], 1)
            pe.wait_ge(s["lora_in"], 32)
            for n, (w_s, z_s) in enumerate(((w2s, z_wd), (a2s, z_ad))):
                for d in range(2):
                    for t in range(RW_CT):
                        f = (n * 2 + d) * (RW_CT // 2) + t // 2
                        if t % 2 == 0 and f == 3:
                            pe.wait_ge(s["kk_sqd"], 1)
                            for k in range(3):
                                pe.matmul(bank[5 + k], ones, kk_sq[:, 2 * k:2 * k + 2].rearrange("p a t -> p (a t)"),
                                          start=True, stop=True).then_inc(s["kk_summed"], 1)
                        if t % 2 == 0 and 3 <= f < 6:
                            pe.wait_ge(s["kk_root"], f - 2)
                        if t % 2 == 0 and f >= 6:
                            pe.wait_ge(s["lora_free"], f - 5)
                        h = slice(d * C, (d + 1) * C)
                        last = pe.matmul(bank[2 + f % 6][:, (t % 2) * T:(t % 2 + 1) * T], w_s[h, t * P:(t + 1) * P],
                                         z_s[h, :], start=True, stop=True)
                        if t % 2:
                            last.then_inc(s["lora_done"], 1)
            pe.wait_ge(s["lora_free"], 2 * RW_CT)
            pe.wait_ge(s["bank_free"], RW_PAIRS)

            def tilde(t, p):
                return ()

            def products(t, p, first, second):
                stand(pe, "z_ready", 2 * t, "pe_passed")
                for d in range(2):
                    stand(pe, "tilde_ready", 2 * t + (d + 1), "pe_passed")
                    for e in range(2):
                        h = slice(e * C, e * C + C)
                        if e == 1:
                            stand(pe, "again_ready", 2 * t + (d + 1), "pe_passed")
                        for c in range(NC):
                            last = pe.matmul(bank[4 + 2 * d + e][:, c * P:(c + 1) * P], bk[h, d, c, e * C:e * C + P],
                                             ar[p][h, d, c, e * C:e * C + P], start=True, stop=True)
                    last.then_inc(s["bm_done"], 1)
                    run(first[d:d + 1])
                stand(pe, "bm_ready", 4 * t + 2, "pe_passed")
                for d in range(2):
                    for e in range(2):
                        h = slice(e * C, e * C + C)
                        for c in range(NC):
                            last = pe.transpose(bank[4 + e][:, (d * NC + c) * C:(d * NC + c + 1) * C],
                                                bk[h, d, c, e * C:e * C + P], ident[h, h])
                last.then_inc(s["bkt_done"], 1)
                run(first[2:])
                stand(pe, "v_copied", t + 1, "pe_passed")
                stand(pe, "bonus_in", t + 1, "pe_passed")
                stand(pe, "vb_ready", 3 * t, "pe_passed")
                pe.matmul(bank[2][:, T:2 * T], ones, tmp, start=True, stop=True)
                run(second[:1])
                for c in range(NC):
                    for e in range(2):
                        h, o = slice(e * C, e * C + C), slice((1 - e) * C, (2 - e) * C)
                        last = pe.matmul(bank[2][o, c * C:(c + 1) * C], vst[h, c * C:(c + 1) * C], ident[h, h],
                                         start=True, stop=True)
                last.then_inc(s["vb_done"], 1)
                run(second[1:])
                stand(pe, "bkt_ready", 2 * t + 2, "pe_passed")
                stand(pe, "bm_ready", 4 * t + 4, "pe_passed")

            def level(t, p, n, pieces, ahead):
                for d in range(2):
                    run(pieces[d:d + 1])
                    stand(pe, "zd_ready", 10 * t + (2 * n + d + 1), "pe_passed")
                    for m in range(NC):
                        for e in range(2):
                            h = slice(e * C, e * C + C)
                            last = pe.matmul(bank[4 + d][h, m * C:(m + 1) * C], bms[p][h, (2 * d + e) * NC + m, h],
                                             zd[h, d * NC + m], start=True, stop=True)
                    last.then_inc(s["p1_done"], 1)
                for d in range(2):
                    stand(pe, "zt_ready", 10 * t + (2 * n + d + 1), "pe_passed")
                    stand(pe, "p1_ready", 10 * t + (2 * n + d + 1), "pe_passed")
                    by, of = (zt, p1s) if n < len(LEVELS) - 1 else (p1s, zt)
                    for m in range(NC):
                        for e in range(2):
                            h = slice(e * C, e * C + C)
                            last = pe.matmul(bank[4 + d][h, T + m * C:T + (m + 1) * C], by[h, d * NC + m],
                                             of[h, d * NC + m], start=True, stop=True)
                    last.then_inc(s["q_done"], 1)
                    if d == 0:
                        run(pieces[2:])

            def chunk(b, q, n):
                gy = [bank[e][:, 0:2 * C].rearrange("p (d v) -> p d v", d=2) for e in range(2)]
                cd = (n, NC - 1 - n)
                at = (0, 1) if n < 2 else (1, 0)

                def g():
                    if n in (0, 3):
                        stand(pe, "y_added", 2 * b + n // 3, "pe_passed")
                    else:
                        stand(pe, "y_copied", 2 * b + n, "pe_passed")
                    if n == 0:
                        stand(pe, "z_ready", 2 * b + 2, "pe_passed")
                    for d in range(2):
                        for e in range(2):
                            h, o = slice(e * C, e * C + C), slice((1 - e) * C, (2 - e) * C)
                            last = pe.matmul(gy[e][h, at[d]], bms[q][o, (2 * d + e) * NC + cd[d], h],
                                             uv[q][o, d * NC + cd[d], e], start=d == 0, stop=n == 0,
                                             skip_group_check=True)
                    if n:
                        last.then_inc(s["v_part"], 1)
                        stand(pe, "s_ready", 3 * b + n, "pe_passed")
                        stand(pe, "v_part", 3 * b + n, "pe_passed")
                        for d in range(2):
                            for e in range(2):
                                h = slice(e * C, e * C + C)
                                last = pe.matmul(gy[e][h, at[d]], ar[q][h, d, cd[d], 2 * e * C:2 * e * C + C], state[h, d],
                                                 start=False, stop=True, skip_group_check=True)
                    last.then_inc(s["gy_done"], 1)

                def u():
                    stand(pe, "g_low", 4 * b + (n + 1), "pe_passed")
                    stand(pe, "g_high", 4 * b + (n + 1), "pe_passed")
                    for d in range(2):
                        for e in range(2):
                            h = slice(e * C, e * C + C)
                            last = pe.matmul(bank[3][h, d * C:(d + 1) * C], az[q][h, d * NC + cd[d]], gs[h, at[d]],
                                             start=True, stop=True)
                    last.then_inc(s["u_done"], 1)
                    if n:
                        for d in range(2):
                            for e in range(2):
                                h, o = slice(e * C, e * C + C), slice((1 - e) * C, (2 - e) * C)
                                pe.matmul(gy[e][o, at[d]], ar[q][h, d, cd[d], C:2 * C], state[h, d], start=d == 0,
                                          stop=False, skip_group_check=True)

                def state_and_y():
                    stand(pe, "u_low", 4 * b + (n + 1), "pe_passed")
                    stand(pe, "u_high", 4 * b + (n + 1), "pe_passed")
                    if n < NC - 1:
                        for d in range(2):
                            for e in range(2):
                                last = pe.matmul(bank[3][e * C:(e + 1) * C, d * C:(d + 1) * C],
                                                 bkt[q][:, e, d * NC + cd[d]], uv[q][:, d * NC + cd[d], e],
                                                 start=True, stop=True)
                        last.then_inc(s["s_done"], 1)
                    for d in range(2):
                        for e in range(2):
                            o = slice((1 - e) * C, (2 - e) * C)
                            last = pe.matmul(gy[e][o, at[d]], bms[q][:, (2 * d + e) * NC + cd[d], o],
                                             uv[q][:, d * NC + cd[d], e], start=n == 0 and d == 0, stop=True,
                                             skip_group_check=True)
                    last.then_inc(s["y_done"], 1)

                return g, u, state_and_y

            def gate_products(n):
                pe.wait_ge(s["g2_in"], 16)
                for t in range(2 * n, 2 * n + 2):
                    last = pe.matmul(gate_bank[n][:, (t % 2) * T:(t % 2 + 1) * T], g2s[:, t * P:(t + 1) * P], z_gd,
                                     start=True, stop=True)
                last.then_inc(s["gate_done"], 1)

            def turn_y(tiles):
                for t in tiles:
                    for c in range(NC):
                        for e in range(2):
                            h, o = slice(e * C, e * C + C), slice((1 - e) * C, (2 - e) * C)
                            at = (t % 2) * T + c * C
                            last = pe.matmul(yt_bank[t // 2][h, at:at + C], zk[o, t, c * C:(c + 1) * C], ident[o, o],
                                             start=True, stop=True)
                    if t % 2:
                        last.then_inc(s["yt_done"], 1)

            def turn_first():
                pe.wait_ge(s["ln_ready"], 1)
                turn_y(range(0, RW_CT - 2))

            rw_tiles(pe, tilde, products, level, chunk,
                     tail=[lambda n=n: gate_products(n) for n in range(3)] + [turn_first])
            pe.wait_ge(s["gate_ready"], 3)
            pe.wait_ge(s["ln_ready"], 2)
            turn_y(range(RW_CT - 2, RW_CT))

            for k in range(2):
                columns(RW_T + k, 0, k, RW_PAIRS)
            for k in range(2, 4):
                columns(RW_T + k, 0, k, RW_PAIRS)
            with pe.Fori(0, (NA_T + RET_T) // 4 - 1) as i:
                for k in range(4):
                    columns(RW_T + 4 + k, i, k + 4, RW_PAIRS)

            pe.wait_ge(s["bank_free"], RW_PAIRS + NR_PAIRS)
            for t in range(TT):
                for n in range(NA_W // P):
                    last = pe.transpose(bank[4 + t][:, n * P:(n + 1) * P], znr[:, 2 * NA_W // P + n, t * P:(t + 1) * P],
                                        ident)
                last.then_inc(s["vna_done"], 1)
            pe.wait_ge(s["bias_ready"], NA_HEADS)
            pe.wait_ge(s["flip_in"], 16)

            def attention_scores(i):
                pe.wait_ge(s["k_copied"], i + 1)
                pe.wait_ge(s["q_ready"], i + 1)
                for e in range(2):
                    h = slice(e * C, e * C + C)
                    pe.matmul(bank[2 + e], flip, bias[:, ds(i * 2 + e, 1), :, :].rearrange("p h t k -> p (h t k)"),
                              start=True, stop=False)
                    for t in range(TT):
                        last = pe.matmul(bank[2 + e][:, t * T:(t + 1) * T], q_s[h, t * P:(t + 1) * P], k_s[h, :],
                                         start=False, stop=t == TT - 1)
                last.then_inc(s["sc_done"], 1)

            def turn(i, attend, more=False):
                pe.wait_ge(s["qk_ready"], 2 * i)
                for n in range(2):
                    last = pe.matmul(bank[0][:, n * T:(n + 1) * T], turn_pairs, tile_of(znr, i + (NA_T + n * RET_CT)),
                                     start=True, stop=True)
                last.then_inc(s["rot_done"], 1)
                pe.wait_ge(s["rot_in"], 3 * i + 3)
                pe.wait_ge(s["v_tok_ready"], i)
                pe.wait_ge(s["ro_ready"], 3 * i)
                for t in range(TT):
                    last = pe.transpose(bank[7][:, t * P:(t + 1) * P], v_cp[:, t * P:(t + 1) * P], ident)
                last.then_inc(s["vt_done"], 1)
                if attend:
                    pe.wait_ge(s["pt_ready"], 2 * i)
                    for e in range(2):
                        pe.wait_ge(s["p_ready"], 4 * i + (2 * e + 2))
                        for kt in range(TT):
                            for t in range(TT):
                                last = pe.transpose(bank[4 + e][:, (2 * kt + t) * P:(2 * kt + t + 1) * P],
                                                    sx[:, e, t, kt * P:(kt + 1) * P], ident)
                        last.then_inc(s["pt_done"], 1)
                    if more:
                        attention_scores(i + 1)
                pe.wait_ge(s["qk_ready"], 2 * i + 2)
                pe.wait_ge(s["st_ready"], i)
                for m in range(TT):
                    last = pe.matmul(bank[1][:, m * T:(m + 1) * T], qk[:, 1, m * P:(m + 1) * P], qk[:, 0], start=True,
                                     stop=True)
                last.then_inc(s["st_done"], 1)
                if attend:
                    pe.wait_ge(s["pt_ready"], 2 * i + 2)
                    pe.wait_ge(s["y_na_lo"], i)
                    for t in range(TT):
                        for e in range(2):
                            for kt in range(TT):
                                last = pe.matmul(bank[6][:, (2 * t + e) * C:(2 * t + e + 1) * C], pts[:, e, kt, t],
                                                 v_na[:, kt, ds(i * P + e * C, C)], start=kt == 0, stop=kt == TT - 1)
                    last.then_inc(s["o_done"], 1)
                pe.wait_ge(s["st_ready"], i + 1)
                pe.wait_ge(s["v_tok_ready"], i + 1)
                for t in range(TT):
                    for m in range(TT):
                        last = pe.matmul(bank[7][:, T + t * P:T + (t + 1) * P], sts[:, m, t * P:(t + 1) * P], v_tok[:, m],
                                         start=m == 0, stop=m == TT - 1)
                last.then_inc(s["ro_done"], 1)
                if attend:
                    pe.wait_ge(s["yq_ready"], 4 * i + 4)
                    for t in range(TT):
                        last = pe.transpose(bank[6][:, T + t * P:T + (t + 1) * P], yq[:, t], ident)
                    last.then_inc(s["yqt_done"], 1)

            attention_scores(0)
            pe.wait_ge(s["vna_ready"], TT)
            mixers(pe, turn)
            pe.wait_ge(s["on_ready"], 1)
            for h in range(RET_CT):
                for t in range(TT):
                    last = pe.transpose(bank[2 + h][:, t * P:(t + 1) * P], o_all[:, h, t], ident)
                last.then_inc(s["ont_done"], 1)

            def rows(c, i, lhs_hi, lhs_lo, first=False, final=False):
                split_ready(c, i)
                for t in range(TT):
                    h = slice(t * P, (t + 1) * P)
                    for lhs, w, a, z in ((lhs_hi, w_hi, first, False), (lhs_hi, w_lo, False, False),
                                         (lhs_lo, w_hi, False, final)):
                        for b in range(4):
                            last = pe.matmul(bank[4 * t + b], lhs[:, h], w[:, c % 2, b * 512:(b + 1) * 512],
                                             start=a, stop=z)
                    if t == 0 and final:
                        last.then_inc(s["half_done"], 1)
                last.then_inc(s["gemm_done"], 1)

            pe.wait_ge(s["y_lo"], RW_CT + RET_CT)
            for n in range(KT):
                rows(OUT_FIRST + n, 0, act_hi[:, n], act_lo[:, n], n == 0, n == KT - 1)

            turned(y_sb, KT)
            pe.wait_ge(s["h_lo"], 2 * KT)
            with pe.Fori(0, FF_T // 4) as i:
                for k in range(4):
                    columns(UP_FIRST + k, i, k, RW_PAIRS + NR_PAIRS)

            pe.wait_ge(s["bank_free"], RW_PAIRS + NR_PAIRS + UP_PAIRS)

            def down(c, i, **ends):
                m = c - DOWN_FIRST
                pe.wait_ge(s["uhi_done"], 4 * i + m + 1)
                pe.wait_ge(s["ulo_done"], 4 * i + m + 1)
                rows(c, i, u_hi[:, c % U_RING], u_lo[:, c % U_RING], **ends)

            down(DOWN_FIRST, 0, first=True)
            with pe.Fori(0, (FF_T - 1) // 4) as i:
                for k in range(4):
                    down(DOWN_FIRST + 1 + k, i)
            for n in range(FF_T - 3, FF_T):
                down(DOWN_FIRST + n, 0, final=n == FF_T - 1)


_INS = ("x", "pre_mix_g", "w_in", "na_rpb", "rw_mu_prev", "rw_mu_next", "rw_w0", "rw_w2", "rw_a0", "rw_a2", "rw_k_k",
        "rw_k_a", "rw_r_k", "rw_g2", "rw_lnx_g", "rw_lnx_b", "w_out", "post_mix_g", "pre_mlp_g", "w_up", "w_down",
        "post_mlp_g")


def kernel(**inputs):
    import concourse.bacc as bacc
    from concourse.bass_utils import run_bass_kernel_spmd

    nc = bacc.Bacc("TRN2", target_bir_lowering=False, num_devices=1)
    tables, decays = constants()
    arrays = {f"in_{n}": np.ascontiguousarray(inputs[n]) for n in _INS}
    arrays["in_tables"], arrays["in_decays"] = tables, decays
    args = [nc.dram_tensor(n, a.shape, mybir.dt.from_np(a.dtype), kind="ExternalInput").ap() for n, a in arrays.items()]
    args.append(nc.dram_tensor("out_x", (1, T, D), F32, kind="ExternalOutput").ap())
    layer(nc, *args)
    r = run_bass_kernel_spmd(nc, [arrays], core_ids=[0])
    return r.results[0]["out_x"]
```
